# Optimizing a Trainium2 kernel written in Bass

```python
import math
import jax, jax.numpy as jnp
from jax import lax
import numpy as np

D_MODEL = 1024
BATCH = 1
SEQ = 1024
DEPTH = 1

HEAD_DIM = 64
MIX_WIDTH = D_MODEL
A_WIDTH = MIX_WIDTH // 2
A_Q_HEADS = A_WIDTH // HEAD_DIM
A_KV_HEADS = A_Q_HEADS // 4
A_GROUP = A_Q_HEADS // A_KV_HEADS
A_KV_WIDTH = A_KV_HEADS * HEAD_DIM
WINDOW = 128
BLOCK = 128
SPAN = BLOCK + 2 * WINDOW
B_WIDTH = MIX_WIDTH - A_WIDTH
B_HEADS = B_WIDTH // (2 * HEAD_DIM)
B_VDIM = 2 * HEAD_DIM

ROPE_THETA = 10000.0
EPS = 1e-6
SCALE = 1.0 / math.sqrt(HEAD_DIM)
NEG = -1e30

IN_SIZES = (A_WIDTH, A_KV_WIDTH, A_KV_WIDTH, A_WIDTH, B_WIDTH, B_WIDTH, B_WIDTH, B_WIDTH)
IN_WIDTH = sum(IN_SIZES)
IN_SPLITS = tuple(int(v) for v in np.cumsum(IN_SIZES)[:-1])

kernel_name = "hymba_swa_sink_diffattn_adaln_encoder"

def _lambda_init(layer_idx):
    return 0.8 - 0.6 * math.exp(-0.3 * layer_idx)

def _rmsnorm(x, gain):
    xf = x.astype(jnp.float32)
    y = xf * lax.rsqrt(jnp.mean(xf * xf, axis=-1, keepdims=True) + EPS)
    return (y * gain.astype(jnp.float32)).astype(x.dtype)

def _rope_tables(positions):
    inv_freq = 1.0 / (ROPE_THETA ** (jnp.arange(0, HEAD_DIM, 2, dtype=jnp.float32) / HEAD_DIM))
    ang = positions.astype(jnp.float32)[..., None] * inv_freq
    ang = jnp.concatenate([ang, ang], axis=-1)
    return jnp.cos(ang), jnp.sin(ang)

def _rope(x, cos, sin):
    shape = cos.shape[:2] + (1,) * (x.ndim - 3) + (HEAD_DIM,)
    cos = cos.reshape(shape)
    sin = sin.reshape(shape)
    xf = x.astype(jnp.float32)
    x1, x2 = jnp.split(xf, 2, axis=-1)
    rot = jnp.concatenate([-x2, x1], axis=-1)
    return (xf * cos + rot * sin).astype(x.dtype)

def _windowed_gqa_sink(q, k, v, sink):
    B, S = q.shape[0], q.shape[1]
    nblk = S // BLOCK
    kp = jnp.pad(k, ((0, 0), (WINDOW, WINDOW), (0, 0), (0, 0)))
    vp = jnp.pad(v, ((0, 0), (WINDOW, WINDOW), (0, 0), (0, 0)))
    qblocks = jnp.moveaxis(q.reshape(B, nblk, BLOCK, A_KV_HEADS, A_GROUP, HEAD_DIM), 1, 0)
    sink_f = sink.astype(jnp.float32)[None, :, :, None, None]

    def one_block(args):
        i, qb = args
        start = i * BLOCK
        kb = lax.dynamic_slice_in_dim(kp, start, SPAN, axis=1)
        vb = lax.dynamic_slice_in_dim(vp, start, SPAN, axis=1)
        s = jnp.einsum('bqkgd,bjkd->bkgqj', qb, kb).astype(jnp.float32) * SCALE
        qpos = start + jnp.arange(BLOCK)
        kpos = start - WINDOW + jnp.arange(SPAN)
        valid = (kpos[None, :] >= 0) & (kpos[None, :] < S) & (jnp.abs(qpos[:, None] - kpos[None, :]) <= WINDOW)
        s = jnp.where(valid, s, NEG)
        m = jnp.maximum(jnp.max(s, axis=-1, keepdims=True), sink_f)
        p = jnp.exp(s - m)
        p = p / (jnp.sum(p, axis=-1, keepdims=True) + jnp.exp(sink_f - m))
        return jnp.einsum('bkgqj,bjkd->bqkgd', p.astype(vb.dtype), vb)

    o = lax.map(one_block, (jnp.arange(nblk), qblocks))
    return jnp.moveaxis(o, 0, 1).reshape(B, S, A_WIDTH)

def _diff_attention(q, k, v, lam, subln_gain, lambda_init):
    B, S = q.shape[0], q.shape[1]
    nblk = S // BLOCK
    qblocks = jnp.moveaxis(q.reshape(B, nblk, BLOCK, B_HEADS, 2, HEAD_DIM), 1, 0)

    def one_block(qb):
        s = jnp.einsum('bqhcd,bjhcd->bhcqj', qb, k).astype(jnp.float32) * SCALE
        p = jax.nn.softmax(s, axis=-1)
        attn = p[:, :, 0] - lam * p[:, :, 1]
        return jnp.einsum('bhqj,bjhe->bqhe', attn.astype(v.dtype), v)

    o = lax.map(one_block, qblocks)
    o = jnp.moveaxis(o, 0, 1).reshape(B, S, B_HEADS, B_VDIM)
    o = _rmsnorm(o, subln_gain) * (1.0 - lambda_init)
    return o.reshape(B, S, B_WIDTH)

def _layer(x, c, cos, sin, w_ada, b_ada, norm_gain, w_in, q_norm_a, k_norm_a, sink_a,
           q_norm_b, k_norm_b, lambda_q1, lambda_k1, lambda_q2, lambda_k2, subln_gain, w_out,
           lambda_init):
    B, S, _ = x.shape
    mod = jax.nn.silu(c) @ w_ada + b_ada
    shift, scale, gate = jnp.split(mod, 3, axis=-1)
    h = _rmsnorm(x, norm_gain) * (1.0 + scale[:, None, :]) + shift[:, None, :]
    proj = h @ w_in
    qa, ka, va, ga, qb, kb, vb, gb = jnp.split(proj, IN_SPLITS, axis=-1)

    qa = _rope(_rmsnorm(qa.reshape(B, S, A_KV_HEADS, A_GROUP, HEAD_DIM), q_norm_a), cos, sin)
    ka = _rope(_rmsnorm(ka.reshape(B, S, A_KV_HEADS, HEAD_DIM), k_norm_a), cos, sin)
    va = va.reshape(B, S, A_KV_HEADS, HEAD_DIM)
    ya = _windowed_gqa_sink(qa, ka, va, sink_a.reshape(A_KV_HEADS, A_GROUP))

    qb = _rope(_rmsnorm(qb.reshape(B, S, B_HEADS, 2, HEAD_DIM), q_norm_b), cos, sin)
    kb = _rope(_rmsnorm(kb.reshape(B, S, B_HEADS, 2, HEAD_DIM), k_norm_b), cos, sin)
    vb = vb.reshape(B, S, B_HEADS, B_VDIM)
    f32 = jnp.float32
    lam = (jnp.exp(jnp.sum(lambda_q1.astype(f32) * lambda_k1.astype(f32)))
           - jnp.exp(jnp.sum(lambda_q2.astype(f32) * lambda_k2.astype(f32))) + lambda_init)
    yb = _diff_attention(qb, kb, vb, lam, subln_gain, lambda_init)

    y = jnp.concatenate([ya * jax.nn.silu(ga), yb * jax.nn.silu(gb)], axis=-1) @ w_out
    return x + gate[:, None, :] * y

def setup_inputs(seed: int = 0) -> dict:
    key = jax.random.key(seed)
    ks = jax.random.split(key, 20)
    f32 = jnp.float32
    nrm = lambda k, shape, s: jax.random.normal(k, shape, f32) * s
    L = DEPTH
    return {
        "x": nrm(ks[0], (BATCH, SEQ, D_MODEL), 1.0),
        "c": nrm(ks[1], (BATCH, D_MODEL), 1.0),
        "positions": (jnp.arange(SEQ, dtype=jnp.int32)[None, :]
                      + jax.random.randint(ks[2], (BATCH, 1), 0, 4096, dtype=jnp.int32)),
        "w_ada": nrm(ks[3], (L, D_MODEL, 3 * D_MODEL), D_MODEL ** -0.5),
        "b_ada": nrm(ks[4], (L, 3 * D_MODEL), 0.02),
        "norm_gain": 1.0 + nrm(ks[5], (L, D_MODEL), 0.05),
        "w_in": nrm(ks[6], (L, D_MODEL, IN_WIDTH), D_MODEL ** -0.5),
        "q_norm_a": 1.0 + nrm(ks[7], (L, HEAD_DIM), 0.05),
        "k_norm_a": 1.0 + nrm(ks[8], (L, HEAD_DIM), 0.05),
        "sink_a": nrm(ks[9], (L, A_Q_HEADS), 0.5),
        "q_norm_b": 1.0 + nrm(ks[10], (L, HEAD_DIM), 0.05),
        "k_norm_b": 1.0 + nrm(ks[11], (L, HEAD_DIM), 0.05),
        "lambda_q1": nrm(ks[12], (L, HEAD_DIM), 0.1),
        "lambda_k1": nrm(ks[13], (L, HEAD_DIM), 0.1),
        "lambda_q2": nrm(ks[14], (L, HEAD_DIM), 0.1),
        "lambda_k2": nrm(ks[15], (L, HEAD_DIM), 0.1),
        "subln_gain": 1.0 + nrm(ks[16], (L, B_VDIM), 0.05),
        "w_out": nrm(ks[17], (L, MIX_WIDTH, D_MODEL), MIX_WIDTH ** -0.5),
    }

def reference(x, c, positions, w_ada, b_ada, norm_gain, w_in, q_norm_a, k_norm_a, sink_a,
              q_norm_b, k_norm_b, lambda_q1, lambda_k1, lambda_q2, lambda_k2, subln_gain, w_out):
    cos, sin = _rope_tables(positions)
    h = x
    for l in range(DEPTH):
        h = _layer(h, c, cos, sin, w_ada[l], b_ada[l], norm_gain[l], w_in[l], q_norm_a[l],
                   k_norm_a[l], sink_a[l], q_norm_b[l], k_norm_b[l], lambda_q1[l], lambda_k1[l],
                   lambda_q2[l], lambda_k2[l], subln_gain[l], w_out[l], _lambda_init(l))
    return h


_drawn_inputs = setup_inputs


def setup_inputs(seed=0):
    import zlib

    import numpy as np

    out = dict(_drawn_inputs(seed))
    spreads = {}
    factors = {'b_ada': 3.169,
     'norm_gain': 3.053,
     'q_norm_a': 8.0,
     'k_norm_a': 8.0,
     'sink_a': 8.0,
     'q_norm_b': 8.0,
     'k_norm_b': 8.0,
     'lambda_q1': 8.0,
     'lambda_k1': 6.333,
     'lambda_q2': 64.0,
     'lambda_k2': 8.0,
     'subln_gain': 3.91}
    for name, (base, spread) in spreads.items():
        noise = np.random.default_rng([zlib.crc32(name.encode()), seed]).standard_normal(out[name].shape)
        drawn = base * np.exp(spread * noise) if base else spread * noise
        out[name] = __import__('jax').numpy.asarray(drawn.astype(out[name].dtype))
    for name, factor in factors.items():
        out[name] = (out[name] * factor).astype(out[name].dtype)
    return out
```

```python
import numpy as np
from contextlib import ExitStack

import concourse.bass as bass
from concourse import mybir

F32 = mybir.dt.float32
F32R = mybir.dt.float32r
I32 = mybir.dt.int32
ACT = mybir.ActivationFunctionType
ALU = mybir.AluOpType
AXX = mybir.AxisListType.X

P = 128
S = 1024
D = 1024
HD = 64
NT = S // P
NK = D // P
CW = 512
HB = 4
HA = 8
GA = 2
NFULL = 6
NPROJ = (NFULL + 1) * NT
EPS = 1e-6
LAMBDA_INIT = 0.2
ROPE_THETA = 10000.0
MAGIC = 1.5 * 2.0 ** 23
PI_IN = 3.1415925
MASKED = -1e30


def columns(parts):
    at, out = 0, {}
    for name, n in parts:
        out[name] = (at, at + n)
        at += n
    return out, at


PARAMS, N_PARAMS = columns((("gain", 4 * HD), ("gain_swapped", 4 * HD), ("sink", HA), ("subln", 2 * HD),
                            ("lambdas", 4 * HD), ("c", NK), ("b_shift", NK), ("b_scale", NK),
                            ("norm_gain", NK)))
CONSTS, N_CONSTS = columns((("identity", P), ("halves", HD), ("ones", P), ("band", 3 * P), ("inv_freq", HD // 2),
                            ("gain_scale", 4 * HD), ("swap_scale", 4 * HD)))


def two_pi_parts():
    rest, parts = 2 * np.pi, []
    for _ in range(3):
        step = 2.0 ** (np.floor(np.log2(rest)) - 8)
        parts.append(float(np.floor(rest / step) * step))
        rest -= parts[-1]
    return parts + [float(np.float32(rest))]


def hymba_kernel(nc, x, w_ada, w_in, w_kv, w_out, params, positions, b_gate, consts, out, debug=None):
    gates_dram = nc.dram_tensor("gates_dram", [S, D], F32, kind="Internal").ap()
    mem = ExitStack()

    def sb(name, shape, dt=F32):
        return mem.enter_context(nc.sbuf_tensor(name, shape, dt))

    def sem(name):
        return mem.enter_context(nc.semaphore(name))

    def phase_tensors(makers):
        with ExitStack() as scope:
            return [scope.enter_context(nc.sbuf_tensor(n, s, d)) for n, s, d in makers]

    with mem:
        cst = sb("cst", [P, N_CONSTS])
        par = sb("par", [P, N_PARAMS])
        ident_r = sb("ident_r", [P, P], F32R)
        gate_row = sb("gate_row", [P, D])
        small = sb("small", [P, 128])
        kv_a = sb("kv_a", [P, NT, 4 * HD])
        q_a = sb("q_a", [P, NT, HA * HD])

        def const(name):
            return cst[:, CONSTS[name][0]:CONSTS[name][1]]

        def param(name):
            return par[:, PARAMS[name][0]:PARAMS[name][1]]

        first = [("qk_b", [P, 2, NT, CW], F32), ("v_b", [P, NT, CW], F32)]
        (qk_b, v_b, h_hi, h_lo, w_hi, w_lo, w_raw, sq, rot, cos_sin, tab, stat) = phase_tensors(first + [
            ("h_hi", [P, NK, S], F32R), ("h_lo", [P, NK, S], F32R),
            ("w_hi", [P, NK, CW], F32R), ("w_lo", [P, NK, CW], F32R),
            ("w_raw", [P, 4, CW], F32), ("sq", [P, 2, CW], F32), ("rot", [P, 2, CW], F32),
            ("cos_sin", [P, 2, NT, HD // 2], F32), ("tab", [P, 2, NT, HD], F32),
            ("stat", [P, 4, NT, HA], F32)])
        hold, mod_acc = phase_tensors([("hold_qkv", [P, 3, NT, CW], F32), ("mod_acc", [P, 2 * D], F32)])
        (_, y_b, o_tb, prob, q1t, q2t, kt, q_st, k_st, v_hi, v_lo, at_hi, at_lo, bst) = phase_tensors([
            ("hold_qkv2", [P, 3, NT, CW], F32),
            ("y_b", [P, NT, CW], F32), ("o_tb", [P, 2, 2 * P], F32), ("prob", [P, 2, S], F32),
            ("q1t", [P, 2, S], F32R), ("q2t", [P, 2, S], F32R), ("kt", [P, 2, S], F32R),
            ("q_st", [P, NT, 2, 3, HD], F32R), ("k_st", [P, NT, 2, 2, HD], F32R),
            ("v_hi", [P, NT, P], F32R), ("v_lo", [P, NT, P], F32R),
            ("at_hi", [P, NT, 2, 2 * P], F32R), ("at_lo", [P, NT, 2, 2 * P], F32R),
            ("bst", [P, 8, NT], F32)])
        lower = [("wo_hi", [P, NK, D], F32R), ("ka_st", [P, NT, GA, 2, HD], F32R), ("wo_raw", [P, 2, D], F32),
                 ("hold_yb", [P, NT, CW], F32), ("wo_lo", [P, NK, D], F32R)]
        (wo_hi, ka_st, wo_raw, _, wo_lo, kta, qa_st, qa1, qa2, va_st, masked, prob_a, pt_hi, pt_lo, o_ta,
         ast) = phase_tensors(lower + [
            ("kta", [P, GA, S], F32R), ("qa_st", [P, HA, 3, HD], F32R),
            ("qa1", [P, HA, P], F32R), ("qa2", [P, HA, P], F32R), ("va_st", [P, 3, GA, 2, HD], F32R),
            ("masked", [P, 2, 3 * P], F32), ("prob_a", [P, 4, 3 * P], F32),
            ("pt_hi", [P, GA, 3, 4 * P], F32R), ("pt_lo", [P, GA, 3, 4 * P], F32R),
            ("o_ta", [P, GA, 4 * P], F32), ("ast", [P, 8, HA], F32)])
        (_, _, _, _, _, x_res, gates, y_cat, y_sq, yt_hi, yt_lo, o_out, cst3) = phase_tensors(
            [(n + "_", s, d) for n, s, d in lower] + [
            ("x_res", [P, 3, D], F32), ("gates", [P, 3, D], F32), ("y_cat", [P, 2, D], F32),
            ("y_sq", [P, CW], F32), ("yt_hi", [P, 2, NK, P], F32R), ("yt_lo", [P, 2, NK, P], F32R),
            ("o_out", [P, 2, D], F32), ("cst3", [P, 4, NT, HB], F32)])

        ps = [mem.enter_context(nc.psum_tensor(f"ps{i}", [P, 2, 512], F32)) for i in range(4)]
        acc = [ps[i // 2][:, i % 2, :] for i in range(4)]

        silu_c, scale_a, shift_b = small[:, 0:8], small[:, 8:16], small[:, 16:24]
        x_ssq, x_ms, x_std, x_rstd = (small[:, 24 + 8 * i:32 + 8 * i] for i in range(4))
        ones, neg_lam = small[:, 56:57], small[:, 57:58]
        lam_sum, lam_exp = small[:, 58:60], small[:, 60:62]
        pos_f = small[:, 72:80]
        pos_i = small[:, 64:72].bitcast(I32)

        ada = qk_b[:, :, :, :].rearrange("p a t c -> p (a t c)").rearrange("p (s n) -> p s n", s=4)
        x_t = [v_b[:, :, :].rearrange("p t c -> p (t c)").rearrange("p (k s) -> p k s", k=NK // 2),
               q_a[:, :, :].rearrange("p t c -> p (t c)").rearrange("p (k s) -> p k s", k=NK // 2)]
        x_in = kv_a[:, :, :].rearrange("p t c -> p (t c)").rearrange("p (s n) -> p s n", s=2)
        gate_in = v_b[:, :, :].rearrange("p t c -> p (t c)").rearrange("p (s n) -> p s n", s=4)
        ang = sq[:, :, :].rearrange("p a c -> p (a c)")[:, 0:NT * HD // 2]
        ang_n, ang_r = (rot[:, i, 0:NT * HD // 2] for i in range(2))
        ang_c = sq[:, 1, 0:NT * HD // 2]

        load = sem("load")
        ada_in = [sem(f"ada_in{i}") for i in range(4)]
        ada_sum = sem("ada_sum")
        x_loaded = [sem(f"x_loaded{i}") for i in range(2)]
        x_squared, x_mean, x_root = sem("x_squared"), sem("x_mean"), sem("x_root")
        x_recip, x_normed, x_turned, x_kept = sem("x_recip"), sem("x_normed"), sem("x_turned"), sem("x_kept")
        setup_dve, setup_act, trig_step = sem("setup_dve"), sem("setup_act"), sem("trig_step")
        mod_cols, mod_done = sem("mod_cols"), sem("mod_done")
        h_affine, h_split, h_ready = sem("h_affine"), sem("h_split"), sem("h_ready")
        w_loaded = [sem(f"w_loaded{i}") for i in range(4)]
        w_hi_done, w_ready, w_slot_free = sem("w_hi_done"), sem("w_ready"), sem("w_slot_free")
        proj_done = sem("proj_done")
        bank_free = [sem(f"bank_free{i}") for i in range(4)]
        squared, ssq_done, std_done, rstd_done = sem("squared"), sem("ssq_done"), sem("std_done"), sem("rstd_done")
        table_done, rot_step, rope_done = sem("table_done"), sem("rot_step"), sem("rope_done")
        silu_out = sem("silu_out")
        gate_stored = [sem(f"gate_stored{i}") for i in range(2)]
        gate_loaded = [sem(f"gate_loaded{i}") for i in range(4)]
        gate_sum, gate_mm, gate_done, bg_in = sem("gate_sum"), sem("gate_mm"), sem("gate_done"), sem("bg_in")
        b_stage, b_v, b_v_free = sem("b_stage"), sem("b_v"), sem("b_v_free")
        b_set, b_set_act, b_set_dve = sem("b_set"), sem("b_set_act"), sem("b_set_dve")
        b_qk, b_max, b_exp = sem("b_qk"), sem("b_max"), sem("b_exp")
        b_small, b_attn, b_turn, b_hi, b_lo = sem("b_small"), sem("b_attn"), sem("b_turn"), sem("b_hi"), sem("b_lo")
        b_pv, b_ot, b_back, b_y = sem("b_pv"), sem("b_ot"), sem("b_back"), sem("b_y")
        a_kst, a_kset, a_kt_act, a_kt_dve = sem("a_kst"), sem("a_kset"), sem("a_kt_act"), sem("a_kt_dve")
        a_qst, a_vst, a_qset, a_qt_act, a_qt_dve = (sem("a_qst"), sem("a_vst"), sem("a_qset"),
                                                    sem("a_qt_act"), sem("a_qt_dve"))
        a_qk, a_max, a_neg, a_exp, a_turn, a_hi, a_lo = (sem("a_qk"), sem("a_max"), sem("a_neg"), sem("a_exp"),
                                                         sem("a_turn"), sem("a_hi"), sem("a_lo"))
        a_pv, a_ot, a_back, a_y = sem("a_pv"), sem("a_ot"), sem("a_back"), sem("a_y")
        a_sink, a_sink_exp, a_den = sem("a_sink"), sem("a_sink_exp"), sem("a_den")
        wo_in = [sem(f"wo_in{i}") for i in range(2)]
        wo_split = sem("wo_split")
        c_in = [sem(f"c_in{i}") for i in range(3)]
        c_sq, c_ssq, c_std, c_rstd, c_norm, c_gain, c_cat = (sem("c_sq"), sem("c_ssq"), sem("c_std"), sem("c_rstd"),
                                                             sem("c_norm"), sem("c_gain"), sem("c_cat"))
        c_turn, c_hi, c_lo, c_mm, c_scaled, c_out = (sem("c_turn"), sem("c_hi"), sem("c_lo"), sem("c_mm"),
                                                     sem("c_scaled"), sem("c_out"))
        carrier = {e: sem(f"wait_carrier_{e}") for e in ("pool", "dve")}
        stored = [sem(f"stored{i}") for i in range(2)]

        groups = ((0, 1), (1, 4), (4, 8))
        ROPE0 = 2
        BANK0 = 1

        def heads(ap, n):
            return ap.rearrange("p (h d) -> p h d", h=n)

        def wait_apart(name, engine, semaphore, value):
            engine.wait_ge(semaphore, value)
            if not isinstance(value, int):
                engine.sem_inc(carrier[name], 1)

        block = mem.enter_context(nc.Block())

        @block.sync
        def _(sp):
            sp.dma_start(par[:, :], params).then_inc(load, 16)
            sp.dma_start(cst[:, :], consts).then_inc(load, 16)
            sp.dma_start(pos_i, positions).then_inc(load, 16)
            for k in range(NK):
                if k >= 4:
                    sp.wait_ge(ada_sum, k - 3)
                sp.dma_start(ada[:, k % 4, :], w_ada[k * P:(k + 1) * P, 0:2 * D]).then_inc(ada_in[k % 4], 16)
                if k >= 2:
                    sp.wait_ge(x_turned, k - 1)
                sp.dma_start(x_in[:, k % 2, :], x[k * P:(k + 1) * P, :]).then_inc(x_loaded[k % 2], 16)
                if k < 4:
                    sp.dma_start(w_raw[:, k, :], w_in[k, :, :]).then_inc(w_loaded[k], 16)
            with sp.Fori(0, NFULL - 1) as ci:
                for k in range(4, 4 + NK):
                    sp.wait_ge(w_ready, ci * NK + k - 3)
                    sp.dma_start(w_raw[:, k % 4:k % 4 + 1, :],
                                 w_in[bass.ds(ci * NK + k, 1), :, :].rearrange("o p n -> p o n")
                                 ).then_inc(w_loaded[k % 4], 16)
            for k in range(4, NK):
                sp.wait_ge(w_ready, (NFULL - 1) * NK + k - 3)
                sp.dma_start(w_raw[:, k % 4, :], w_in[(NFULL - 1) * NK + k, :, :]).then_inc(w_loaded[k % 4], 16)
            for k in range(NK):
                sp.wait_ge(w_ready, NFULL * NK + k - 3)
                sp.dma_start(w_raw[:, k % 4, 0:4 * HD], w_kv[k, :, :]).then_inc(w_loaded[k % 4], 16)
            sp.wait_ge(b_lo, HB * NT)
            sp.wait_ge(b_back, HB * 4)
            for k in range(NK):
                if k >= 2:
                    sp.wait_ge(wo_split, 2 * (k - 1))
                sp.dma_start(wo_raw[:, k % 2, :], w_out[k * P:(k + 1) * P, :]).then_inc(wo_in[k % 2], 16)
            sp.wait_ge(a_y, NT)
            sp.dma_start(o_out[:, 0, :], b_gate.broadcast_to([P, D])).then_inc(bg_in, 16)
            for t in range(NT + 3):
                if t >= 3:
                    sp.wait_ge(c_out, t - 2)
                    sp.dma_start(out[(t - 3) * P:(t - 2) * P, :], o_out[:, (t - 3) % 2, :]
                                 ).then_inc(stored[(t - 3) % 2], 16)
                if t < NT:
                    sp.dma_start(gates[:, t % 3, :], gates_dram[t * P:(t + 1) * P, :]).then_inc(c_in[t % 3], 16)
                    sp.dma_start(x_res[:, t % 3, :], x[t * P:(t + 1) * P, :]).then_inc(c_in[t % 3], 16)
            for b in range(2):
                sp.wait_ge(stored[b], 16 * NT // 2)

        @block.gpsimd
        def _(pool):
            def rope(place, n_heads, t, m):
                n = n_heads * HD
                v = place.rearrange("p (h e d) -> p h e d", h=n_heads, e=2)
                c = tab[:, 0, t, :].unsqueeze(1).broadcast_to([P, n_heads, HD])
                s = tab[:, 1, t, :].rearrange("p (e d) -> p e d", e=2)
                r = rot[:, t % 2, 0:n].rearrange("p (h e d) -> p h e d", h=n_heads, e=2)
                pool.tensor_tensor(heads(sq[:, t % 2, 0:n], n_heads), heads(place, n_heads), c, ALU.mult
                                   ).then_inc(rot_step, 1)
                for e in range(2):
                    pool.tensor_tensor(r[:, :, e, :], v[:, :, 1 - e, :],
                                       s[:, e, :].unsqueeze(1).broadcast_to([P, n_heads, HD // 2]), ALU.mult
                                       ).then_inc(rot_step, 1)
                wait_apart("pool", pool, rot_step, 3 * m + 3)
                pool.tensor_tensor(place, sq[:, t % 2, 0:n], rot[:, t % 2, 0:n], ALU.add).then_inc(rope_done, 1)

            def tables(g, m0):
                wait_apart("pool", pool, rope_done, ROPE0 + m0)
                gain = heads(param("gain"), 4)[:, bass.ds(g, 1), :].rearrange("p o (e d) -> p o e d", e=2)
                swap = heads(param("gain_swapped"), 4)[:, bass.ds(g, 1), :].rearrange("p o (e d) -> p o e d", e=2)
                for i, w in enumerate((gain, swap)):
                    for e in range(2):
                        dst = tab[:, i, :, :].rearrange("p t (e d) -> p t e d", e=2)[:, :, e, :]
                        pool.tensor_tensor(dst, cos_sin[:, i, :, :],
                                           w[:, :, e, :].broadcast_to([P, NT, HD // 2]),
                                           ALU.mult).then_inc(table_done, 1)

            def norm_chunk(ci, g, place, n_heads):
                tables(g, g * NT)
                wait_apart("pool", pool, table_done, 4 * g + 4)
                for t in range(NT):
                    wait_apart("pool", pool, bank_free[t % 4], 2 * ci + t // 4 + 1 + BANK0)
                    rope(place(t), n_heads, t, g * NT + t)

            for b in range(4):
                pool.sem_inc(bank_free[b], BANK0)
            for b in range(2):
                pool.sem_inc(gate_stored[b], 16)
            pool.sem_inc(rope_done, ROPE0)
            pool.wait_ge(setup_act, 3)
            pool.wait_ge(setup_dve, 3)
            with pool.Fori(0, 2) as ci:
                norm_chunk(ci, ci, lambda t: qk_b[:, bass.ds(ci, 1), t, :].rearrange("p o c -> p (o c)"), 8)
            pool.wait_ge(h_ready, 3)
            for k in range(NK):
                if k >= 4:
                    pool.wait_ge(gate_sum, k - 3)
                pool.dma_start(gate_in[:, k % 4, :], w_ada[k * P:(k + 1) * P, 2 * D:3 * D]
                               ).then_inc(gate_loaded[k % 4], 16)
            norm_chunk(5, 2, lambda t: q_a[:, t, :], HA)
            norm_chunk(6, 3, lambda t: kv_a[:, t, 0:2 * HD], GA)

            wait_apart("pool", pool, rope_done, ROPE0 + 4 * NT)
            for b in range(4):
                pool.wait_ge(bank_free[b], 2 * (NFULL + 1) + BANK0)
            for b in range(2):
                pool.wait_ge(gate_stored[b], 16 * (1 + NT))

            def hi(dst, src, done):
                one = ones
                while len(one.shape) < len(src.shape):
                    one = one.unsqueeze(1)
                pool.tensor_tensor(dst, src, one.broadcast_to(list(src.shape)), ALU.mult).then_inc(done, 1)

            def lo(dst, src, high, done):
                pool.tensor_tensor(dst, src, high.bitcast(F32), ALU.subtract).then_inc(done, 1)

            def stage(h):
                q = qk_b[:, 0, :, bass.ds(h * P, P)].rearrange("p t (c d) -> p t c d", c=2)
                k = qk_b[:, 1, :, bass.ds(h * P, P)].rearrange("p t (c d) -> p t c d", c=2)
                for c in range(2):
                    hi(q_st[:, :, c, 0, :], q[:, :, c, :], b_stage)
                    hi(q_st[:, :, c, 2, :], q[:, :, c, :], b_stage)
                    hi(k_st[:, :, c, 0, :], k[:, :, c, :], b_stage)
                wait_apart("pool", pool, b_stage, 10 * h + 6)
                for c in range(2):
                    lo(q_st[:, :, c, 1, :], q[:, :, c, :], q_st[:, :, c, 0, :], b_stage)
                    lo(k_st[:, :, c, 1, :], k[:, :, c, :], k_st[:, :, c, 0, :], b_stage)

            def stage_v(h, half):
                r = slice(4 * half, 4 * half + 4)
                v = v_b[:, r, bass.ds(h * P, P)]
                hi(v_hi[:, r, :], v, b_v)
                wait_apart("pool", pool, b_v, 4 * h + 2 * half + 1)
                lo(v_lo[:, r, :], v, v_hi[:, r, :], b_v)

            stage(0)
            stage_v(0, 0)
            stage_v(0, 1)
            with pool.Fori(1, HB) as h:
                wait_apart("pool", pool, b_set, 6 * h)
                stage(h)
                wait_apart("pool", pool, b_v_free, h)
                stage_v(h, 0)
                wait_apart("pool", pool, b_pv, 4 * h)
                stage_v(h, 1)

            pool.wait_ge(b_lo, HB * NT)
            pool.wait_ge(b_back, HB * 4)
            pool.wait_ge(b_y, HB * 4)
            ka = kv_a[:, :, 0:2 * HD].rearrange("p t (g d) -> p t g d", g=GA)
            for g in range(GA):
                hi(ka_st[:, :, g, 0, :], ka[:, :, g, :], a_kst)
            pool.wait_ge(a_kst, 2)
            for g in range(GA):
                lo(ka_st[:, :, g, 1, :], ka[:, :, g, :], ka_st[:, :, g, 0, :], a_kst)

            def stage_a(i, k0, nk, wait):
                if wait:
                    wait_apart("pool", pool, a_qset, 2 * i)
                q = heads(q_a[:, bass.ds(i, 1), :].rearrange("p o c -> p (o c)"), HA)
                hi(qa_st[:, :, 0, :], q, a_qst)
                hi(qa_st[:, :, 2, :], q, a_qst)
                wait_apart("pool", pool, a_qst, 3 * i + 1)
                lo(qa_st[:, :, 1, :], q, qa_st[:, :, 0, :], a_qst)
                if wait:
                    wait_apart("pool", pool, a_pv, 2 * i)
                for g in range(GA):
                    v = kv_a[:, bass.ds(k0, nk), 2 * HD + g * HD:2 * HD + (g + 1) * HD]
                    hi(va_st[:, 0:nk, g, 0, :], v, a_vst)
                    wait_apart("pool", pool, a_vst, 4 * i + 2 * g + 1)
                    lo(va_st[:, 0:nk, g, 1, :], v, va_st[:, 0:nk, g, 0, :], a_vst)

            def split_wo(k):
                pool.wait_ge(wo_in[k % 2], 16 * (k // 2 + 1))
                hi(wo_hi[:, k, :], wo_raw[:, k % 2, :], wo_split)
                pool.wait_ge(wo_split, 2 * k + 1)
                lo(wo_lo[:, k, :], wo_raw[:, k % 2, :], wo_hi[:, k, :], wo_split)

            stage_a(0, 0, 2, False)
            stage_a(1, 0, 3, True)
            for k in range(2):
                split_wo(k)
            for i in range(2, NT - 1):
                stage_a(i, i - 1, 3, True)
                split_wo(i)
            stage_a(NT - 1, NT - 2, 2, True)
            split_wo(NT - 1)

            pool.wait_ge(a_y, NT)

            def squares(t):
                if t >= 1:
                    pool.wait_ge(c_ssq, 2 * t - 1)
                yb = y_b[:, t, :]
                pool.tensor_tensor(y_sq[:, :], yb, yb, ALU.mult).then_inc(c_sq, 1)

            def gated(t):
                s = t % 2
                pool.wait_ge(c_in[t % 3], 32 * (t // 3 + 1))
                if t >= 2:
                    pool.wait_ge(c_turn, t - 1)
                pool.tensor_tensor(y_cat[:, s, 0:CW], q_a[:, t, :], gates[:, t % 3, 0:CW], ALU.mult
                                   ).then_inc(c_cat, 1)
                pool.wait_ge(c_norm, t + 1)
                pool.tensor_tensor(heads(y_cat[:, s, CW:D], HB), heads(y_b[:, t, :], HB),
                                   param("subln").unsqueeze(1).broadcast_to([P, HB, 2 * HD]), ALU.mult
                                   ).then_inc(c_gain, 1)
                pool.wait_ge(c_gain, t + 1)
                pool.tensor_tensor(y_cat[:, s, CW:D], y_cat[:, s, CW:D], gates[:, t % 3, CW:D], ALU.mult
                                   ).then_inc(c_cat, 1)

            def residual(t):
                s = t % 2
                pool.wait_ge(c_scaled, t + 1)
                pool.tensor_tensor(o_out[:, s, :], o_out[:, s, :], x_res[:, t % 3, :], ALU.add).then_inc(c_out, 1)

            squares(0)
            gated(0)
            squares(1)
            for t in range(NT):
                if t + 1 < NT:
                    gated(t + 1)
                if t + 2 < NT:
                    squares(t + 2)
                if t >= 1:
                    residual(t - 1)
            residual(NT - 1)

        @block.scalar
        def _(act):
            act.wait_ge(load, 48)
            act.activation(silu_c, param("c"), ACT.Silu).then_inc(setup_act, 1)
            act.wait_ge(setup_dve, 4)
            act.activation(cos_sin[:, 0, :, :].rearrange("p t d -> p (t d)"), ang_c, ACT.Sin).then_inc(setup_act, 1)
            act.activation(cos_sin[:, 1, :, :].rearrange("p t d -> p (t d)"), ang_r, ACT.Sin).then_inc(setup_act, 1)

            def split_w(k):
                act.wait_ge(w_loaded[k % 4], 16 * (k // 4 + 1))
                act.activation(w_hi[:, k, :], w_raw[:, k % 4, :], ACT.Copy).then_inc(w_hi_done, 1)

            act.wait_ge(setup_act, 3)
            for k in range(NK):
                act.wait_ge(x_loaded[k % 2], 16 * (k // 2 + 1))
                if k >= 1:
                    act.wait_ge(x_mean, k)
                act.activation(sq[:, :, :].rearrange("p a c -> p (a c)"), x_in[:, k % 2, :], ACT.Square,
                               accum_out=x_ssq[:, k:k + 1]).then_inc(x_squared, 1)
                if k < 4:
                    split_w(k)
                act.wait_ge(x_mean, k + 1)
                act.activation(x_std[:, k:k + 1], x_ms[:, k:k + 1], ACT.Sqrt).then_inc(x_root, 1)
                act.wait_ge(x_turned, k + 1)
                for half in range(2):
                    act.activation(x_t[half][:, :, k * P:(k + 1) * P], ps[2 + k % 2][:, half, :].rearrange(
                        "p (k s) -> p k s", k=4), ACT.Copy).then_inc(x_kept, 1)
            for k in range(4, NK):
                split_w(k)
            act.wait_ge(mod_done, 2)
            act.wait_ge(x_kept, 2 * NK)
            for a, b in groups:
                for k in range(NK):
                    place = x_t[k // 4][:, k % 4, a * P:b * P]
                    act.activation(place, place, ACT.Identity, bias=shift_b[:, k:k + 1],
                                   scale=scale_a[:, k:k + 1]).then_inc(h_affine, 1)

            def refill(ci, n):
                for k in range(NK):
                    if k < NK - 1:
                        act.wait_ge(w_slot_free, (NK - 1) * ci + k + 1)
                    else:
                        act.wait_ge(proj_done, NT * ci + NT)
                    act.wait_ge(w_loaded[k % 4], 32 * ci + 16 * (k // 4) + 48)
                    act.activation(w_hi[:, k, 0:n], w_raw[:, k % 4, 0:n], ACT.Copy).then_inc(w_hi_done, 1)

            def norm_tile(ci, t, m, n):
                act.wait_ge(proj_done, NT * ci + t + 1)
                act.wait_ge(rope_done, m + t + 1)
                act.activation(sq[:, t % 2, 0:n], acc[t % 4][:, 0:n], ACT.Square).then_inc(squared, 1)
                act.wait_ge(ssq_done, 2 * (m + t) + 2)
                act.activation(stat[:, 2, t, 0:n // HD], stat[:, 1, t, 0:n // HD], ACT.Sqrt).then_inc(std_done, 1)

            def copy_tile(ci, t):
                act.wait_ge(proj_done, NT * ci + t + 1)
                act.activation(v_b[:, t, :], acc[t % 4], ACT.Copy).then_inc(bank_free[t % 4], 1)

            def gate_tile(ci, t):
                act.wait_ge(proj_done, NT * ci + t + 1)
                act.wait_ge(gate_stored[t % 2], (ci - 3) * (16 * NT // 2) + 16 * (t // 2) + 16)
                act.activation(sq[:, t % 2, :], acc[t % 4], ACT.Silu).then_inc(bank_free[t % 4], 1)
                act.wait_ge(bank_free[t % 4], 2 * ci + t // 4 + 1 + BANK0)
                act.dma_start(gates_dram[t * P:(t + 1) * P, bass.ds((ci - 3) * CW, CW)], sq[:, t % 2, :]
                              ).then_inc(gate_stored[t % 2], 16)

            with act.Fori(0, 2) as ci:
                for t in range(NT - 1):
                    norm_tile(ci, t, ci * NT, CW)
                refill(ci, CW)
                norm_tile(ci, NT - 1, ci * NT, CW)
            act.wait_ge(gate_sum, NK)
            for t in range(NT - 1):
                copy_tile(2, t)
            refill(2, CW)
            copy_tile(2, NT - 1)
            act.wait_ge(rope_done, ROPE0 + 2 * NT)
            with act.Fori(3, 5) as ci:
                for t in range(NT - 1):
                    gate_tile(ci, t)
                refill(ci, CW)
                gate_tile(ci, NT - 1)
            for b in range(2):
                act.wait_ge(gate_stored[b], 16 * (1 + NT))
            for t in range(NT - 1):
                norm_tile(5, t, 2 * NT, CW)
            refill(5, 4 * HD)
            norm_tile(5, NT - 1, 2 * NT, CW)
            for t in range(NT):
                norm_tile(6, t, 3 * NT, 2 * HD)

            act.wait_ge(setup_dve, 6)
            act.activation(lam_exp, lam_sum, ACT.Exp).then_inc(setup_act, 1)

            def set_copy(h, s):
                act.wait_ge(b_set, 6 * h + s + 1)
                act.activation((q1t, q2t, kt)[s % 3][:, s // 3, :],
                               ps[s % 3][:, :, :].rearrange("p a c -> p (a c)"), ACT.Copy).then_inc(b_set_act, 1)

            def exponentials(h, j):
                for c in range(2):
                    act.wait_ge(b_max, 16 * h + 2 * j + c + 1)
                    act.activation(prob[:, c, :], ps[c][:, :, :].rearrange("p a c -> p (a c)"), ACT.Exp,
                                   bias=bst[:, c, j:j + 1], accum_out=bst[:, 2 + c, j:j + 1]).then_inc(b_exp, 1)

            def attn_hi(h, j):
                act.wait_ge(b_turn, NT * h + j + 1)
                act.activation(at_hi[:, :, j // 2 % 2, (j % 2) * P:(j % 2 + 1) * P],
                               ps[2][:, :, :].rearrange("p a (k s) -> p (a k) s", k=4), ACT.Copy).then_inc(b_hi, 1)

            def o_copy(h, m):
                act.wait_ge(b_pv, 4 * h + m + 1)
                act.activation(o_tb[:, m % 2, :], ps[3][:, 0, (m % 2) * 2 * P:(m % 2 + 1) * 2 * P], ACT.Copy
                               ).then_inc(b_ot, 1)

            for s in (0, 2, 4):
                set_copy(0, s)
            exponentials(0, 0)

            def head(h, last):
                for j in range(NT):
                    if j >= 1:
                        attn_hi(h, j - 1)
                        exponentials(h, j)
                    if j in (3, 5, 7):
                        o_copy(h, (j - 3) // 2)
                attn_hi(h, NT - 1)
                if not last:
                    for s in (0, 2, 4):
                        set_copy(h + 1, s)
                    exponentials(h + 1, 0)
                o_copy(h, 3)

            with act.Fori(0, HB - 1) as h:
                head(h, False)
            head(HB - 1, True)

            act.wait_ge(a_kset, 1)
            act.activation(kta[:, 0, :], ps[0][:, :, :].rearrange("p a c -> p (a c)"), ACT.Copy).then_inc(a_kt_act, 1)

            def q_copy(i):
                act.wait_ge(a_qset, 2 * i + 1)
                act.activation(qa1[:, :, :].rearrange("p h s -> p (h s)"),
                               ps[3][:, :, :].rearrange("p a c -> p (a c)"), ACT.Copy).then_inc(a_qt_act, 1)

            def pa_hi(i, hh, nk):
                act.wait_ge(a_turn, HA * i + hh + 1)
                act.activation(pt_hi[:, hh // 4, 0:nk, (hh % 4) * P:(hh % 4 + 1) * P],
                               ps[1][:, hh % 2, 0:nk * P].rearrange("p (k s) -> p k s", k=nk), ACT.Copy
                               ).then_inc(a_hi, 1)

            def oa_copy(i, g):
                act.wait_ge(a_pv, 2 * i + g + 1)
                act.activation(o_ta[:, g, :], ps[2][:, 0, :], ACT.Copy).then_inc(a_ot, 1)

            def tile_a(i, nk, first, last):
                for hh in range(HA):
                    act.wait_ge(a_neg, HA * i + hh + 1)
                    if hh >= 4:
                        act.wait_ge(a_turn, HA * i + hh - 3)
                    act.activation(prob_a[:, hh % 4, 0:nk * P], masked[:, hh % 2, 0:nk * P], ACT.Exp,
                                   bias=ast[:, 1, hh:hh + 1], accum_out=ast[:, 2, hh:hh + 1]).then_inc(a_exp, 1)
                    if hh >= 1:
                        pa_hi(i, hh - 1, nk)
                    if hh == 1 and not first:
                        oa_copy(i - 1, 1)
                    if hh == 7:
                        oa_copy(i, 0)
                pa_hi(i, HA - 1, nk)
                act.wait_ge(a_sink, i + 1)
                act.activation(ast[:, 4, :], ast[:, 3, :], ACT.Exp).then_inc(a_sink_exp, 1)
                if not last:
                    q_copy(i + 1)
                else:
                    oa_copy(i, 1)

            q_copy(0)
            tile_a(0, 2, True, False)
            with act.Fori(1, NT - 1) as i:
                tile_a(i, 3, False, False)
            tile_a(NT - 1, 2, False, True)

            def root(t):
                act.wait_ge(c_ssq, 2 * t + 2)
                act.activation(cst3[:, 2, t, :], cst3[:, 1, t, :], ACT.Sqrt).then_inc(c_std, 1)

            def y_hi(t):
                act.wait_ge(c_turn, t + 1)
                act.activation(yt_hi[:, t % 2, :, :].rearrange("p k s -> p (k s)"),
                               ps[2][:, :, :].rearrange("p a c -> p (a c)"), ACT.Copy).then_inc(c_hi, 1)

            for t in range(NT):
                root(t)
                y_hi(t)

        @block.vector
        def _(dve):
            dve.memset(ones, 1.0).then_inc(setup_dve, 1)
            dve.wait_ge(load, 48)
            dve.tensor_tensor(param("gain"), param("gain"), const("gain_scale"), ALU.mult).then_inc(setup_dve, 1)
            dve.tensor_tensor(param("gain_swapped"), param("gain_swapped"), const("swap_scale"), ALU.mult
                              ).then_inc(setup_dve, 1)
            n_trig = [0]

            def link(instruction):
                n_trig[0] += 1
                instruction.then_inc(trig_step, 1)
                dve.wait_ge(trig_step, n_trig[0])

            link(dve.tensor_copy(ident_r[:, :], const("identity")))
            link(dve.tensor_copy(pos_f, pos_i))
            link(dve.tensor_tensor(ang.rearrange("p (t d) -> p t d", t=NT),
                                   pos_f.unsqueeze(2).broadcast_to([P, NT, HD // 2]),
                                   const("inv_freq").unsqueeze(1).broadcast_to([P, NT, HD // 2]), ALU.mult))
            for place, turn in ((ang_r, 0.0), (ang_c, 0.25)):
                link(dve.tensor_scalar(ang_n, ang, 1.0 / (2 * np.pi), turn, ALU.mult, ALU.add))
                link(dve.tensor_scalar(ang_n, ang_n, MAGIC, MAGIC, ALU.add, ALU.subtract))
                src = ang
                for part in two_pi_parts():
                    link(dve.scalar_tensor_tensor(place, ang_n, -part, src, ALU.mult, ALU.add))
                    src = place
                link(dve.tensor_scalar(place, place, turn * 2 * np.pi, PI_IN, ALU.add, ALU.min))
                link(dve.tensor_scalar(place, place, -PI_IN, None, ALU.max))
            dve.tensor_copy(small[:, 80:81], ones).then_inc(setup_dve, 1)

            def low_w(k):
                dve.wait_ge(w_hi_done, k + 1)
                dve.tensor_tensor(w_lo[:, k, :], w_raw[:, k % 4, :], w_hi[:, k, :].bitcast(F32), ALU.subtract
                                  ).then_inc(w_ready, 1)

            acc2 = mod_acc[:, :]
            for k in range(NK):
                dve.wait_ge(ada_in[k % 4], 16 * (k // 4 + 1))
                if k == 0:
                    dve.wait_ge(setup_act, 1)
                    dve.tensor_scalar(acc2, ada[:, 0, :], silu_c[:, 0:1], None, ALU.mult).then_inc(ada_sum, 1)
                else:
                    dve.wait_ge(ada_sum, k)
                    dve.scalar_tensor_tensor(acc2, ada[:, k % 4, :], silu_c[:, k:k + 1], acc2, ALU.mult, ALU.add
                                             ).then_inc(ada_sum, 1)
                dve.wait_ge(x_squared, k + 1)
                dve.tensor_scalar(x_ms[:, k:k + 1], x_ssq[:, k:k + 1], 1.0 / D, EPS, ALU.mult, ALU.add
                                  ).then_inc(x_mean, 1)
                if k < 4:
                    low_w(k)
                dve.wait_ge(x_root, k + 1)
                dve.reciprocal(x_rstd[:, k:k + 1], x_std[:, k:k + 1]).then_inc(x_recip, 1)
                dve.wait_ge(x_recip, k + 1)
                dve.tensor_scalar(x_in[:, k % 2, :], x_in[:, k % 2, :], x_rstd[:, k:k + 1], None, ALU.mult
                                  ).then_inc(x_normed, 1)
            for k in range(4, NK):
                low_w(k)
            dve.wait_ge(mod_cols, 1)
            dve.tensor_tensor(shift_b, ps[0][:, 0, 0:8], param("b_shift"), ALU.add).then_inc(mod_done, 1)
            link(dve.tensor_tensor(scale_a, ps[0][:, 0, 8:16], param("b_scale"), ALU.add))
            dve.scalar_tensor_tensor(scale_a, scale_a, 1.0, param("norm_gain"), ALU.add, ALU.mult
                                     ).then_inc(mod_done, 1)
            for n, (a, b) in enumerate(groups):
                for half in range(2):
                    dve.wait_ge(h_affine, NK * n + 4 * half + 4)
                    dve.tensor_copy(h_hi[:, 4 * half:4 * half + 4, a * P:b * P], x_t[half][:, :, a * P:b * P]
                                    ).then_inc(h_split, 1)
                for half in range(2):
                    dve.wait_ge(h_split, 2 * n + half + 1)
                    low = dve.tensor_tensor(h_lo[:, 4 * half:4 * half + 4, a * P:b * P],
                                            x_t[half][:, :, a * P:b * P],
                                            h_hi[:, 4 * half:4 * half + 4, a * P:b * P].bitcast(F32), ALU.subtract)
                low.then_inc(h_ready, 1)

            def refill(ci, n):
                for k in range(NK):
                    dve.wait_ge(w_hi_done, NK * ci + k + NK + 1)
                    dve.tensor_tensor(w_lo[:, k, 0:n], w_raw[:, k % 4, 0:n], w_hi[:, k, 0:n].bitcast(F32),
                                      ALU.subtract).then_inc(w_ready, 1)

            def norm_tile(ci, t, m, place, n):
                nh = n // HD
                dve.wait_ge(squared, m + t + 1)
                dve.tensor_reduce(stat[:, 0, t, 0:nh], heads(sq[:, t % 2, 0:n], nh), AXX, ALU.add
                                  ).then_inc(ssq_done, 1)
                dve.wait_ge(ssq_done, 2 * (m + t) + 1)
                dve.tensor_scalar(stat[:, 1, t, 0:nh], stat[:, 0, t, 0:nh], 1.0 / HD, EPS, ALU.mult, ALU.add
                                  ).then_inc(ssq_done, 1)
                dve.wait_ge(std_done, m + t + 1)
                dve.reciprocal(stat[:, 3, t, 0:nh], stat[:, 2, t, 0:nh]).then_inc(rstd_done, 1)
                dve.wait_ge(rstd_done, m + t + 1)
                if n < CW:
                    dve.tensor_copy(kv_a[:, t, 2 * HD:4 * HD], acc[t % 4][:, 2 * HD:4 * HD])
                dve.tensor_tensor(heads(place, nh), heads(acc[t % 4][:, 0:n], nh),
                                  stat[:, 3, t, 0:nh].unsqueeze(2).broadcast_to([P, nh, HD]), ALU.mult
                                  ).then_inc(bank_free[t % 4], 1)

            def norm_chunk(ci, m, place, n, next_n):
                for t in range(NT - 1):
                    norm_tile(ci, t, m, place(t), n)
                if next_n:
                    refill(ci, next_n)
                norm_tile(ci, NT - 1, m, place(NT - 1), n)

            with dve.Fori(0, 2) as ci:
                norm_chunk(ci, ci * NT, lambda t: qk_b[:, bass.ds(ci, 1), t, :].rearrange("p o c -> p (o c)"),
                           CW, CW)
            for k in range(NK):
                dve.wait_ge(gate_loaded[k % 4], 16 * (k // 4 + 1))
                if k == 0:
                    dve.tensor_scalar(gate_row[:, :], gate_in[:, 0, :], silu_c[:, 0:1], None, ALU.mult
                                      ).then_inc(gate_sum, 1)
                else:
                    dve.wait_ge(gate_sum, k)
                    dve.scalar_tensor_tensor(gate_row[:, :], gate_in[:, k % 4, :], silu_c[:, k:k + 1],
                                             gate_row[:, :], ALU.mult, ALU.add).then_inc(gate_sum, 1)
            lam = param("lambdas").rearrange("p (a b d) -> p a b d", a=2, b=2)
            link(dve.tensor_tensor(lam[:, :, 0, :], lam[:, :, 0, :], lam[:, :, 1, :], ALU.mult))
            dve.tensor_reduce(lam_sum, lam[:, :, 0, :], AXX, ALU.add).then_inc(setup_dve, 1)
            dve.tensor_scalar(param("subln"), param("subln"), 1.0 - LAMBDA_INIT, None, ALU.mult
                              ).then_inc(setup_dve, 1)
            refill(2, CW)
            with dve.Fori(3, 5) as ci:
                refill(ci, CW)
            norm_chunk(5, 2 * NT, lambda t: q_a[:, t, :], CW, 4 * HD)
            norm_chunk(6, 3 * NT, lambda t: kv_a[:, t, 0:2 * HD], 2 * HD, 0)

            dve.wait_ge(setup_act, 4)
            link(dve.tensor_scalar(neg_lam, lam_exp[:, 1:2], lam_exp[:, 0:1], -LAMBDA_INIT, ALU.subtract, ALU.add))

            def set_copy(h, s):
                dve.wait_ge(b_set, 6 * h + s + 1)
                dve.tensor_copy((q1t, q2t, kt)[s % 3][:, s // 3, :],
                                ps[s % 3][:, :, :].rearrange("p a c -> p (a c)")).then_inc(b_set_dve, 1)

            def maxima(h, j):
                for c in range(2):
                    dve.wait_ge(b_qk, 16 * h + 2 * j + c + 1)
                    dve.tensor_reduce(bst[:, c, j:j + 1], ps[c][:, :, :].rearrange("p a c -> p (a c)"), AXX,
                                      ALU.max, negate=True).then_inc(b_max, 1)

            def attn_lo(h, j):
                dve.wait_ge(b_hi, NT * h + j + 1)
                place = slice((j % 2) * P, (j % 2 + 1) * P)
                dve.tensor_tensor(at_lo[:, :, j // 2 % 2, place],
                                  ps[2][:, :, :].rearrange("p a (k s) -> p (a k) s", k=4),
                                  at_hi[:, :, j // 2 % 2, place].bitcast(F32), ALU.subtract).then_inc(b_lo, 1)

            def combine(h, j):
                dve.wait_ge(b_exp, 16 * h + 2 * j + 2)
                dve.reciprocal(bst[:, 4:6, j:j + 1], bst[:, 2:4, j:j + 1]).then_inc(b_small, 1)
                dve.wait_ge(b_small, 2 * NT * h + 2 * j + 1)
                dve.scalar_tensor_tensor(bst[:, 6, j:j + 1], bst[:, 2, j:j + 1], bst[:, 5, j:j + 1], neg_lam,
                                         ALU.mult, ALU.mult).then_inc(b_small, 1)
                dve.wait_ge(b_small, 2 * NT * h + 2 * j + 2)
                dve.scalar_tensor_tensor(prob[:, 0, :], prob[:, 1, :], bst[:, 6, j:j + 1], prob[:, 0, :],
                                         ALU.mult, ALU.add).then_inc(b_attn, 1)

            def write_y(h, m):
                dve.wait_ge(b_back, 4 * h + m + 1)
                dve.tensor_tensor(y_b[:, 2 * m:2 * m + 2, bass.ds(h * P, P)],
                                  ps[3][:, 1, (m % 2) * 2 * P:(m % 2 + 1) * 2 * P].rearrange("p (t d) -> p t d", t=2),
                                  bst[:, 4, 2 * m:2 * m + 2].unsqueeze(2).broadcast_to([P, 2, P]), ALU.mult
                                  ).then_inc(b_y, 1)

            for s in (1, 3, 5):
                set_copy(0, s)
            maxima(0, 0)

            def head(h, last):
                for j in range(NT):
                    if j >= 1:
                        maxima(h, j)
                        attn_lo(h, j - 1)
                    if j in (4, 6):
                        write_y(h, (j - 4) // 2)
                    combine(h, j)
                attn_lo(h, NT - 1)
                if not last:
                    for s in (1, 3, 5):
                        set_copy(h + 1, s)
                write_y(h, 2)
                if not last:
                    maxima(h + 1, 0)
                write_y(h, 3)

            with dve.Fori(0, HB - 1) as h:
                head(h, False)
            head(HB - 1, True)

            dve.wait_ge(a_kset, 2)
            dve.tensor_copy(kta[:, 1, :], ps[1][:, :, :].rearrange("p a c -> p (a c)")).then_inc(a_kt_dve, 1)

            def q_copy(i):
                dve.wait_ge(a_qset, 2 * i + 2)
                dve.tensor_copy(qa2[:, :, :].rearrange("p h s -> p (h s)"),
                                ps[3][:, :, :].rearrange("p a c -> p (a c)")).then_inc(a_qt_dve, 1)

            def pa_lo(i, hh, nk):
                dve.wait_ge(a_hi, HA * i + hh + 1)
                place = slice((hh % 4) * P, (hh % 4 + 1) * P)
                dve.tensor_tensor(pt_lo[:, hh // 4, 0:nk, place],
                                  ps[1][:, hh % 2, 0:nk * P].rearrange("p (k s) -> p k s", k=nk),
                                  pt_hi[:, hh // 4, 0:nk, place].bitcast(F32), ALU.subtract).then_inc(a_lo, 1)

            def write_ya(i):
                dve.wait_ge(a_back, 2 * i + 2)
                dve.tensor_tensor(q_a[:, bass.ds(i, 1), :].rearrange("p o (h d) -> p (o h) d", h=HA),
                                  heads(ps[2][:, 1, :], HA),
                                  ast[:, 6, :].unsqueeze(2).broadcast_to([P, HA, HD]), ALU.mult).then_inc(a_y, 1)

            def tile_a(i, nk, first, last):
                off = P if first else 0
                for hh in range(HA):
                    wait_apart("dve", dve, a_qk, HA * i + hh + 1)
                    if hh >= 2:
                        wait_apart("dve", dve, a_exp, HA * i + hh - 1)
                    dve.tensor_tensor_reduce(out=masked[:, hh % 2, 0:nk * P], in0=ps[0][:, hh % 2, 0:nk * P],
                                             in1=const("band")[:, off:off + nk * P], scale=1.0,
                                             scalar=param("sink")[:, hh:hh + 1], op0=ALU.add, op1=ALU.max,
                                             accum_out=ast[:, 0, hh:hh + 1]).then_inc(a_max, 1)
                    dve.wait_ge(a_max, HA * i + hh + 1)
                    dve.tensor_scalar(ast[:, 1, hh:hh + 1], ast[:, 0, hh:hh + 1], -1.0, None, ALU.mult
                                      ).then_inc(a_neg, 1)
                    if hh >= 2:
                        pa_lo(i, hh - 2, nk)
                    if hh == 4 and not first:
                        write_ya(i - 1)
                dve.wait_ge(a_neg, HA * i + HA)
                dve.tensor_tensor(ast[:, 3, :], ast[:, 1, :], param("sink"), ALU.add).then_inc(a_sink, 1)
                pa_lo(i, 6, nk)
                pa_lo(i, 7, nk)
                dve.wait_ge(a_sink_exp, i + 1)
                dve.tensor_tensor(ast[:, 5, :], ast[:, 4, :], ast[:, 2, :], ALU.add).then_inc(a_den, 1)
                dve.wait_ge(a_den, 2 * i + 1)
                dve.reciprocal(ast[:, 6, :], ast[:, 5, :]).then_inc(a_den, 1)
                if not last:
                    q_copy(i + 1)
                else:
                    dve.wait_ge(a_den, 2 * i + 2)
                    write_ya(i)

            q_copy(0)
            tile_a(0, 2, True, False)
            with dve.Fori(1, NT - 1) as i:
                tile_a(i, 3, False, False)
            tile_a(NT - 1, 2, False, True)

            dve.wait_ge(gate_mm, 1)
            dve.wait_ge(bg_in, 16)
            dve.wait_ge(a_den, 2 * NT)
            dve.tensor_tensor(gate_row[:, :], ps[3][:, :, :].rearrange("p a c -> p (a c)"),
                              o_out[:, 0, :], ALU.add).then_inc(gate_done, 1)

            def statistics(t):
                dve.wait_ge(c_sq, t + 1)
                dve.tensor_reduce(cst3[:, 0, t, :], heads(y_sq[:, :], HB), AXX, ALU.add).then_inc(c_ssq, 1)
                dve.wait_ge(c_ssq, 2 * t + 1)
                dve.tensor_scalar(cst3[:, 1, t, :], cst3[:, 0, t, :], 1.0 / (2 * HD), EPS, ALU.mult, ALU.add
                                  ).then_inc(c_ssq, 1)
                dve.wait_ge(c_std, t + 1)
                dve.reciprocal(cst3[:, 3, t, :], cst3[:, 2, t, :]).then_inc(c_rstd, 1)
                dve.wait_ge(c_rstd, t + 1)
                dve.tensor_tensor(heads(y_b[:, t, :], HB), heads(y_b[:, t, :], HB),
                                  cst3[:, 3, t, :].unsqueeze(2).broadcast_to([P, HB, 2 * HD]), ALU.mult
                                  ).then_inc(c_norm, 1)

            def y_low(t):
                dve.wait_ge(c_hi, t + 1)
                dve.tensor_tensor(yt_lo[:, t % 2, :, :].rearrange("p k s -> p (k s)"),
                                  ps[2][:, :, :].rearrange("p a c -> p (a c)"),
                                  yt_hi[:, t % 2, :, :].rearrange("p k s -> p (k s)").bitcast(F32), ALU.subtract
                                  ).then_inc(c_lo, 1)

            def scaled(t):
                dve.wait_ge(c_mm, t + 1)
                if t >= 2:
                    dve.wait_ge(stored[t % 2], 16 * (t // 2))
                dve.tensor_tensor(o_out[:, t % 2, :], ps[t % 2][:, :, :].rearrange("p a c -> p (a c)"),
                                  gate_row[:, :], ALU.mult).then_inc(c_scaled, 1)

            statistics(0)
            for t in range(NT):
                if t + 1 < NT:
                    statistics(t + 1)
                y_low(t)
                if t >= 1:
                    scaled(t - 1)
            scaled(NT - 1)

        @block.tensor
        def _(pe):
            ident = const("identity")
            pe.wait_ge(load, 48)
            pe.wait_ge(setup_dve, 4)
            for t in range(NT):
                pe.wait_ge(x_normed, t + 1)
                if t >= 2:
                    pe.wait_ge(x_kept, 2 * (t - 1))
                for k in range(NK):
                    last = pe.transpose(ps[2 + t % 2][:, k // 4, (k % 4) * P:(k % 4 + 1) * P],
                                        x_in[:, t % 2, k * P:(k + 1) * P], ident)
                last.then_inc(x_turned, 1)
            pe.wait_ge(ada_sum, NK)
            for j in range(16):
                last = pe.matmul(ps[0][:, 0, j:j + 1], mod_acc[:, j * P:(j + 1) * P], ones, start=True, stop=True)
            last.then_inc(mod_cols, 1)
            pe.wait_ge(mod_done, 2)

            def proj_chunk(ci, n):
                for t in range(NT):
                    pe.wait_ge(bank_free[t % 4], 2 * ci + t // 4 + BANK0)
                    if t in (0, 1, 4):
                        pe.wait_ge(h_ready, (0, 1, 4).index(t) + 1)
                    tok = slice(t * P, (t + 1) * P)
                    for k in range(NK):
                        if t == 0:
                            pe.wait_ge(w_ready, NK * ci + k + 1)
                        pe.matmul(acc[t % 4][:, 0:n], h_hi[:, k, tok], w_hi[:, k, 0:n], start=(k == 0), stop=False)
                        pe.matmul(acc[t % 4][:, 0:n], h_hi[:, k, tok], w_lo[:, k, 0:n], start=False, stop=False)
                        last = pe.matmul(acc[t % 4][:, 0:n], h_lo[:, k, tok], w_hi[:, k, 0:n], start=False,
                                         stop=(k == NK - 1))
                        if t == NT - 1 and k < NK - 1:
                            last.then_inc(w_slot_free, 1)
                    last.then_inc(proj_done, 1)

            with pe.Fori(0, NFULL) as ci:
                proj_chunk(ci, CW)
            proj_chunk(NFULL, 4 * HD)

            def sets(h):
                pe.wait_ge(b_stage, 10 * h + 10)
                for s in range(6):
                    if s >= 3:
                        if s % 2 == 1:
                            pe.wait_ge(b_set_act, 3 * h + (s - 3) // 2 + 1)
                        else:
                            pe.wait_ge(b_set_dve, 3 * h + (s - 3) // 2 + 1)
                    c, kind = s // 3, s % 3
                    for t in range(NT):
                        src = (q_st[:, t, c, 0:2, :], q_st[:, t, c, 1:3, :], k_st[:, t, c, :, :])[kind]
                        last = pe.transpose(ps[s % 3][:, t // 4, (t % 4) * P:(t % 4 + 1) * P].bitcast(F32R),
                                            src.rearrange("p a d -> p (a d)"), ident_r[:, :])
                    last.then_inc(b_set, 1)

            def scores(h, j, lead):
                for c in range(2):
                    if lead:
                        if c == 0:
                            pe.wait_ge(b_set_act, 3 * h + 3)
                            pe.wait_ge(b_set_dve, 3 * h + 3)
                    else:
                        pe.wait_ge(b_exp, 16 * h + 2 * j + c - 1)
                    q = slice(j * P, (j + 1) * P)
                    for half in range(2):
                        kk = kt[:, c, half * 512:(half + 1) * 512]
                        pe.matmul(ps[c][:, half, :], q1t[:, c, q], kk, start=True, stop=False)
                        last = pe.matmul(ps[c][:, half, :], q2t[:, c, q], kk, start=False, stop=True)
                    last.then_inc(b_qk, 1)

            def turn(h, j):
                pe.wait_ge(b_attn, NT * h + j + 1)
                if j >= 1:
                    pe.wait_ge(b_lo, NT * h + j)
                for k in range(NT):
                    last = pe.transpose(ps[2][:, k // 4, (k % 4) * P:(k % 4 + 1) * P],
                                        prob[:, 0, k * P:(k + 1) * P], ident)
                last.then_inc(b_turn, 1)

            def pv(h, m, half):
                if half == 0:
                    pe.wait_ge(b_lo, NT * h + 2 * m + 2)
                pe.wait_ge(b_v, 4 * h + 2 * half + 2)
                if half == 0:
                    pe.wait_ge(b_ot, 4 * h + m)
                o = ps[3][:, 0, (m % 2) * 2 * P:(m % 2 + 1) * 2 * P]
                for k in range(4 * half, 4 * half + 4):
                    pe.matmul(o, v_hi[:, k, :], at_hi[:, k, m % 2, :], start=(k == 0), stop=False)
                    pe.matmul(o, v_hi[:, k, :], at_lo[:, k, m % 2, :], start=False, stop=False)
                    last = pe.matmul(o, v_lo[:, k, :], at_hi[:, k, m % 2, :], start=False, stop=(k == NT - 1))
                if half == 1:
                    last.then_inc(b_pv, 1)
                elif m == 3:
                    last.then_inc(b_v_free, 1)

            def back(h, m):
                pe.wait_ge(b_ot, 4 * h + m + 1)
                pe.wait_ge(b_y, 4 * h + m)
                for t in range(2):
                    last = pe.transpose(ps[3][:, 1, (2 * (m % 2) + t) * P:(2 * (m % 2) + t + 1) * P],
                                        o_tb[:, m % 2, t * P:(t + 1) * P], ident)
                last.then_inc(b_back, 1)

            sets(0)
            scores(0, 0, True)

            def head(h, last):
                for j in range(NT):
                    if j < NT - 1:
                        scores(h, j + 1, False)
                    if j >= 2:
                        pv(h, j // 2 - 1, j % 2)
                    turn(h, j)
                    if j in (3, 5, 7):
                        back(h, (j - 3) // 2)
                if not last:
                    pe.wait_ge(b_exp, 16 * h + 16)
                    pe.wait_ge(b_lo, NT * h + NT)
                    sets(h + 1)
                    scores(h + 1, 0, True)
                pv(h, 3, 0)
                pv(h, 3, 1)
                back(h, 3)

            with pe.Fori(0, HB - 1) as h:
                head(h, False)
            head(HB - 1, True)

            pe.wait_ge(a_kst, 4)
            for g in range(GA):
                for t in range(NT):
                    last = pe.transpose(ps[g][:, t // 4, (t % 4) * P:(t % 4 + 1) * P].bitcast(F32R),
                                        ka_st[:, t, g, :, :].rearrange("p a d -> p (a d)"), ident_r[:, :])
                last.then_inc(a_kset, 1)

            def q_sets(i):
                pe.wait_ge(a_qst, 3 * i + 3)
                for n in range(2):
                    if n == 1:
                        pe.wait_ge(a_qt_act, i + 1)
                    for hh in range(HA):
                        last = pe.transpose(ps[3][:, hh // 4, (hh % 4) * P:(hh % 4 + 1) * P].bitcast(F32R),
                                            qa_st[:, hh, n:n + 2, :].rearrange("p a d -> p (a d)"), ident_r[:, :])
                    last.then_inc(a_qset, 1)

            def scores_a(i, hh, k0, nk, wait):
                if wait:
                    pe.wait_ge(a_max, HA * i + hh - 1)
                elif hh == 0:
                    pe.wait_ge(a_qt_dve, i + 1)
                keys = kta[:, hh // 4, bass.ds(k0 * P, nk * P)]
                pe.matmul(ps[0][:, hh % 2, 0:nk * P], qa1[:, hh, :], keys, start=True, stop=False)
                pe.matmul(ps[0][:, hh % 2, 0:nk * P], qa2[:, hh, :], keys, start=False, stop=True
                          ).then_inc(a_qk, 1)

            def turn_a(i, hh, nk):
                pe.wait_ge(a_exp, HA * i + hh + 1)
                if hh >= 2:
                    pe.wait_ge(a_lo, HA * i + hh - 1)
                for k in range(nk):
                    last = pe.transpose(ps[1][:, hh % 2, k * P:(k + 1) * P], prob_a[:, hh % 4, k * P:(k + 1) * P],
                                        ident)
                last.then_inc(a_turn, 1)

            def pv_a(i, g, nk, first):
                pe.wait_ge(a_lo, HA * i + 4 * g + 4)
                pe.wait_ge(a_vst, 4 * i + 4)
                if not (first and g == 0):
                    pe.wait_ge(a_ot, 2 * i + g)
                for k in range(nk):
                    v = va_st[:, k, g, :, :].rearrange("p a d -> p (a d)")
                    pe.matmul(ps[2][:, 0, :], v, pt_hi[:, g, k, :], start=(k == 0), stop=False)
                    last = pe.matmul(ps[2][:, 0, :], v, pt_lo[:, g, k, :], start=False, stop=(k == nk - 1))
                last.then_inc(a_pv, 1)

            def back_a(i, first):
                for g in range(GA):
                    pe.wait_ge(a_ot, 2 * i + g + 1)
                    for n in range(4):
                        last = pe.matmul(ps[2][:, 1, (4 * g + n) * HD:(4 * g + n + 1) * HD],
                                         o_ta[:, g, n * P:(n + 1) * P], const("halves"), start=True, stop=True)
                    last.then_inc(a_back, 1)

            def tile_a(i, k0, nk, nk1, first, last):
                for hh in range(HA):
                    if hh + 2 < HA:
                        scores_a(i, hh + 2, k0, nk, True)
                    turn_a(i, hh, nk)
                    if hh == 2 and not first:
                        back_a(i - 1, first)
                    if hh == 5:
                        pv_a(i, 0, nk, first)
                if not last:
                    q_sets(i + 1)
                    k1 = 0 if first else k0 + 1
                    pe.wait_ge(a_max, HA * i + HA)
                    scores_a(i + 1, 0, k1, nk1, False)
                    scores_a(i + 1, 1, k1, nk1, False)
                pv_a(i, 1, nk, first)
                if last:
                    back_a(i, first)

            q_sets(0)
            pe.wait_ge(a_kt_act, 1)
            pe.wait_ge(a_kt_dve, 1)
            scores_a(0, 0, 0, 2, False)
            scores_a(0, 1, 0, 2, False)
            tile_a(0, 0, 2, 3, True, False)
            with pe.Fori(1, NT - 2) as i:
                tile_a(i, i - 1, 3, 3, False, False)
            tile_a(NT - 2, NT - 3, 3, 2, False, False)
            tile_a(NT - 1, NT - 2, 2, 0, False, True)

            for half in range(2):
                last = pe.matmul(ps[3][:, half, :], const("ones"), gate_row[:, half * 512:(half + 1) * 512],
                                 start=True, stop=True)
            last.then_inc(gate_mm, 1)

            def turn_y(t):
                pe.wait_ge(c_cat, 2 * t + 2)
                if t >= 1:
                    pe.wait_ge(c_lo, t)
                for k in range(NK):
                    last = pe.transpose(ps[2][:, k // 4, (k % 4) * P:(k % 4 + 1) * P],
                                        y_cat[:, t % 2, k * P:(k + 1) * P], ident)
                last.then_inc(c_turn, 1)

            pe.wait_ge(wo_split, 2 * NK)
            pe.wait_ge(a_y, NT)
            turn_y(0)
            for t in range(NT):
                pe.wait_ge(c_lo, t + 1)
                if t >= 2:
                    pe.wait_ge(c_scaled, t - 1)
                for half in range(2):
                    o = ps[t % 2][:, half, :]
                    w = slice(half * 512, (half + 1) * 512)
                    for k in range(NK):
                        pe.matmul(o, yt_hi[:, t % 2, k, :], wo_hi[:, k, w], start=(k == 0), stop=False)
                        pe.matmul(o, yt_hi[:, t % 2, k, :], wo_lo[:, k, w], start=False, stop=False)
                        last = pe.matmul(o, yt_lo[:, t % 2, k, :], wo_hi[:, k, w], start=False, stop=(k == NK - 1))
                    if half == 0 and t + 1 < NT:
                        turn_y(t + 1)
                last.then_inc(c_mm, 1)
    return nc


def constants():
    c = np.zeros((P, N_CONSTS), np.float32)

    def put(name, value):
        c[:, CONSTS[name][0]:CONSTS[name][1]] = value

    put("identity", np.eye(P))
    put("halves", np.concatenate([np.eye(HD)] * 2))
    put("ones", 1.0)
    q, k = np.arange(P)[:, None], np.arange(P)[None, :]
    band = np.zeros((P, 3 * P), np.float32)
    band[:, 0:P][k < q] = MASKED
    band[:, 2 * P:][k > q] = MASKED
    put("band", band)
    put("inv_freq", np.float32(1.0) / np.float32(ROPE_THETA) ** (np.arange(0, HD, 2, dtype=np.float32) / np.float32(HD)))
    scale = np.repeat(np.float32([HD ** -0.5, 1.0, HD ** -0.5, 1.0]), HD)
    put("gain_scale", scale)
    sign = np.tile(np.repeat(np.float32([-1.0, 1.0]), HD // 2), 4)
    put("swap_scale", scale * sign)
    return c


def kernel(x, c, positions, w_ada, b_ada, norm_gain, w_in, q_norm_a, k_norm_a, sink_a, q_norm_b, k_norm_b,
           lambda_q1, lambda_k1, lambda_q2, lambda_k2, subln_gain, w_out):
    import concourse.bacc as bacc
    from concourse.bass_utils import run_bass_kernel_spmd

    def a(v):
        return np.ascontiguousarray(np.asarray(v))

    gains = [a(v)[0] for v in (q_norm_b, k_norm_b, q_norm_a, k_norm_a)]
    swapped = [np.concatenate([g[HD // 2:], g[:HD // 2]]) for g in gains]
    b = a(b_ada)[0]

    def rows(v):
        return np.broadcast_to(v.reshape(1, -1), (P, v.size))

    def cols(v):
        return v.reshape(NK, P).T

    params = np.concatenate([
        rows(np.concatenate(gains)), rows(np.concatenate(swapped)), rows(a(sink_a)[0]), rows(a(subln_gain)[0]),
        rows(np.concatenate([a(v)[0] for v in (lambda_q1, lambda_k1, lambda_q2, lambda_k2)])),
        cols(a(c)[0]), cols(b[0:D]), cols(b[D:2 * D]), cols(a(norm_gain)[0])], axis=1)
    w = a(w_in)[0]
    starts = (1280, 1792, 2304, 768, 2816, 0)
    chunks = np.stack([w[:, s:s + CW] for s in starts]).reshape(NFULL * NK, P, CW)
    arrays = {
        "x": a(x)[0], "w_ada": a(w_ada)[0], "w_in": a(chunks), "w_kv": a(w[:, 512:768].reshape(NK, P, 4 * HD)),
        "w_out": a(w_out)[0], "params": a(params), "positions": a(a(positions)[0].reshape(NT, P).T),
        "b_gate": a(b[2 * D:].reshape(1, D)), "consts": constants(),
    }
    nc = bacc.Bacc("TRN2", target_bir_lowering=False, num_devices=1)
    args = [nc.dram_tensor(f"in_{n}", v.shape, mybir.dt.from_np(v.dtype), kind="ExternalInput").ap()
            for n, v in arrays.items()]
    out = nc.dram_tensor("out", (S, D), F32, kind="ExternalOutput").ap()
    hymba_kernel(nc, *args, out)
    r = run_bass_kernel_spmd(nc, [{f"in_{n}": v for n, v in arrays.items()}], core_ids=[0])
    return r.results[0]["out"].reshape(1, S, D)
```

```python
import numpy as np
from contextlib import ExitStack

import concourse.bass as bass
from concourse import mybir

F32 = mybir.dt.float32
F32R = mybir.dt.float32r
I32 = mybir.dt.int32
ACT = mybir.ActivationFunctionType
ALU = mybir.AluOpType
AXX = mybir.AxisListType.X

P = 128
S = 1024
D = 1024
HD = 64
NT = S // P
NK = D // P
CW = 512
HB = 4
HA = 8
GA = 2
NFULL = 6
NPROJ = (NFULL + 1) * NT
EPS = 1e-6
LAMBDA_INIT = 0.2
ROPE_THETA = 10000.0
MAGIC = 1.5 * 2.0 ** 23
PI_IN = 3.1415925
MASKED = -1e30


def columns(parts):
    at, out = 0, {}
    for name, n in parts:
        out[name] = (at, at + n)
        at += n
    return out, at


PARAMS, N_PARAMS = columns((("gain", 4 * HD), ("gain_swapped", 4 * HD), ("sink", HA), ("subln", 2 * HD),
                            ("lambdas", 4 * HD), ("c", NK), ("b_shift", NK), ("b_scale", NK),
                            ("norm_gain", NK)))
CONSTS, N_CONSTS = columns((("identity", P), ("halves", HD), ("ones", P), ("band", 3 * P), ("inv_freq", HD // 2),
                            ("gain_scale", 4 * HD), ("swap_scale", 4 * HD)))


def two_pi_parts():
    rest, parts = 2 * np.pi, []
    for _ in range(3):
        step = 2.0 ** (np.floor(np.log2(rest)) - 8)
        parts.append(float(np.floor(rest / step) * step))
        rest -= parts[-1]
    return parts + [float(np.float32(rest))]


def hymba_kernel(nc, x, w_ada, w_in, w_kv, w_out, params, positions, b_gate, consts, out, debug=None):
    gates_dram = nc.dram_tensor("gates_dram", [S, D], F32, kind="Internal").ap()
    mem = ExitStack()

    def sb(name, shape, dt=F32):
        return mem.enter_context(nc.sbuf_tensor(name, shape, dt))

    def sem(name):
        return mem.enter_context(nc.semaphore(name))

    def phase_tensors(makers):
        with ExitStack() as scope:
            return [scope.enter_context(nc.sbuf_tensor(n, s, d)) for n, s, d in makers]

    with mem:
        cst = sb("cst", [P, N_CONSTS])
        par = sb("par", [P, N_PARAMS])
        ident_r = sb("ident_r", [P, P], F32R)
        gate_row = sb("gate_row", [P, D])
        small = sb("small", [P, 128])
        kv_a = sb("kv_a", [P, NT, 4 * HD])
        q_a = sb("q_a", [P, NT, HA * HD])

        def const(name):
            return cst[:, CONSTS[name][0]:CONSTS[name][1]]

        def param(name):
            return par[:, PARAMS[name][0]:PARAMS[name][1]]

        first = [("qk_b", [P, 2, NT, CW], F32), ("v_b", [P, NT, CW], F32)]
        (qk_b, v_b, h_hi, h_lo, w_hi, w_lo, w_raw, sq, rot, cos_sin, tab, stat) = phase_tensors(first + [
            ("h_hi", [P, NK, S], F32R), ("h_lo", [P, NK, S], F32R),
            ("w_hi", [P, NK, CW], F32R), ("w_lo", [P, NK, CW], F32R),
            ("w_raw", [P, 4, CW], F32), ("sq", [P, 2, CW], F32), ("rot", [P, 2, CW], F32),
            ("cos_sin", [P, 2, NT, HD // 2], F32), ("tab", [P, 2, NT, HD], F32),
            ("stat", [P, 4, NT, HA], F32)])
        hold, mod_acc = phase_tensors([("hold_qkv", [P, 3, NT, CW], F32), ("mod_acc", [P, 2 * D], F32)])
        (_, y_b, o_tb, prob, q1t, q2t, kt, q_st, k_st, v_hi, v_lo, at_hi, at_lo, bst) = phase_tensors([
            ("hold_qkv2", [P, 3, NT, CW], F32),
            ("y_b", [P, NT, CW], F32), ("o_tb", [P, 2, 2 * P], F32), ("prob", [P, 2, 2, S], F32),
            ("q1t", [P, 2, S], F32R), ("q2t", [P, 2, S], F32R), ("kt", [P, 2, S], F32R),
            ("q_st", [P, NT, 2, 3, HD], F32R), ("k_st", [P, NT, 2, 2, HD], F32R),
            ("v_hi", [P, NT, P], F32R), ("v_lo", [P, NT, P], F32R),
            ("at_hi", [P, NT, 2, 2 * P], F32R), ("at_lo", [P, NT, 2, 2 * P], F32R),
            ("bst", [P, 8, NT], F32)])
        lower = [("wo_hi", [P, NK, D], F32R), ("ka_st", [P, NT, GA, 2, HD], F32R), ("wo_raw", [P, 2, D], F32),
                 ("hold_yb", [P, NT, CW], F32), ("wo_lo", [P, NK, D], F32R)]
        (wo_hi, ka_st, wo_raw, _, wo_lo, kta, qa_st, qa1, qa2, va_st, masked, prob_a, pt_hi, pt_lo, o_ta,
         ast) = phase_tensors(lower + [
            ("kta", [P, GA, S], F32R), ("qa_st", [P, HA, 3, HD], F32R),
            ("qa1", [P, HA, P], F32R), ("qa2", [P, HA, P], F32R), ("va_st", [P, 3, GA, 2, HD], F32R),
            ("masked", [P, 2, 3 * P], F32), ("prob_a", [P, 4, 3 * P], F32),
            ("pt_hi", [P, GA, 3, 4 * P], F32R), ("pt_lo", [P, GA, 3, 4 * P], F32R),
            ("o_ta", [P, GA, 4 * P], F32), ("ast", [P, 8, HA], F32)])
        (_, _, _, _, _, x_res, gates, y_cat, y_sq, yt_hi, yt_lo, o_out, cst3) = phase_tensors(
            [(n + "_", s, d) for n, s, d in lower] + [
            ("x_res", [P, 3, D], F32), ("gates", [P, 3, D], F32), ("y_cat", [P, 2, D], F32),
            ("y_sq", [P, CW], F32), ("yt_hi", [P, 2, NK, P], F32R), ("yt_lo", [P, 2, NK, P], F32R),
            ("o_out", [P, 2, D], F32), ("cst3", [P, 4, NT, HB], F32)])

        ps = [mem.enter_context(nc.psum_tensor(f"ps{i}", [P, 2, 512], F32)) for i in range(4)]
        acc = [ps[i // 2][:, i % 2, :] for i in range(4)]

        silu_c, scale_a, shift_b = small[:, 0:8], small[:, 8:16], small[:, 16:24]
        x_ssq, x_ms, x_std, x_rstd = (small[:, 24 + 8 * i:32 + 8 * i] for i in range(4))
        ones, neg_lam = small[:, 56:57], small[:, 57:58]
        lam_sum, lam_exp = small[:, 58:60], small[:, 60:62]
        pos_f = small[:, 72:80]
        pos_i = small[:, 64:72].bitcast(I32)

        ada = qk_b[:, :, :, :].rearrange("p a t c -> p (a t c)").rearrange("p (s n) -> p s n", s=4)
        x_t = [v_b[:, :, :].rearrange("p t c -> p (t c)").rearrange("p (k s) -> p k s", k=NK // 2),
               q_a[:, :, :].rearrange("p t c -> p (t c)").rearrange("p (k s) -> p k s", k=NK // 2)]
        x_in = kv_a[:, :, :].rearrange("p t c -> p (t c)").rearrange("p (s n) -> p s n", s=2)
        gate_in = v_b[:, :, :].rearrange("p t c -> p (t c)").rearrange("p (s n) -> p s n", s=4)
        ang = sq[:, :, :].rearrange("p a c -> p (a c)")[:, 0:NT * HD // 2]
        ang_n, ang_r = (rot[:, i, 0:NT * HD // 2] for i in range(2))
        ang_c = sq[:, 1, 0:NT * HD // 2]

        load = sem("load")
        ada_in = [sem(f"ada_in{i}") for i in range(4)]
        ada_sum = sem("ada_sum")
        x_loaded = [sem(f"x_loaded{i}") for i in range(2)]
        x_squared, x_mean, x_root = sem("x_squared"), sem("x_mean"), sem("x_root")
        x_recip, x_normed, x_turned, x_kept = sem("x_recip"), sem("x_normed"), sem("x_turned"), sem("x_kept")
        setup_dve, setup_act, trig_step = sem("setup_dve"), sem("setup_act"), sem("trig_step")
        mod_cols, mod_done = sem("mod_cols"), sem("mod_done")
        h_affine, h_split, h_ready = sem("h_affine"), sem("h_split"), sem("h_ready")
        w_loaded = [sem(f"w_loaded{i}") for i in range(4)]
        w_hi_done, w_ready, w_slot_free = sem("w_hi_done"), sem("w_ready"), sem("w_slot_free")
        proj_done = sem("proj_done")
        bank_free = [sem(f"bank_free{i}") for i in range(4)]
        squared, ssq_done, std_done, rstd_done = sem("squared"), sem("ssq_done"), sem("std_done"), sem("rstd_done")
        table_done, rot_step, rope_done = sem("table_done"), sem("rot_step"), sem("rope_done")
        silu_out = sem("silu_out")
        gate_stored = [sem(f"gate_stored{i}") for i in range(2)]
        gate_loaded = [sem(f"gate_loaded{i}") for i in range(4)]
        gate_sum, gate_mm, gate_done, bg_in = sem("gate_sum"), sem("gate_mm"), sem("gate_done"), sem("bg_in")
        b_stage, b_v, b_v_free = sem("b_stage"), sem("b_v"), sem("b_v_free")
        b_first_hi, b_first_lo, b_scaled = sem("b_first_hi"), sem("b_first_lo"), sem("b_scaled")
        b_set, b_set_act, b_set_dve = sem("b_set"), sem("b_set_act"), sem("b_set_dve")
        b_qk, b_max, b_exp = sem("b_qk"), sem("b_max"), sem("b_exp")
        b_small, b_turn, b_hi, b_lo = sem("b_small"), sem("b_turn"), sem("b_hi"), sem("b_lo")
        b_attn = [sem(f"b_attn{i}") for i in range(2)]
        b_pv, b_ot, b_back, b_y = sem("b_pv"), sem("b_ot"), sem("b_back"), sem("b_y")
        a_kst, a_kset, a_kt_act, a_kt_dve = sem("a_kst"), sem("a_kset"), sem("a_kt_act"), sem("a_kt_dve")
        a_qst, a_vst, a_qset, a_qt_act, a_qt_dve = (sem("a_qst"), sem("a_vst"), sem("a_qset"),
                                                    sem("a_qt_act"), sem("a_qt_dve"))
        a_qk, a_max, a_neg, a_exp, a_turn, a_hi, a_lo = (sem("a_qk"), sem("a_max"), sem("a_neg"), sem("a_exp"),
                                                         sem("a_turn"), sem("a_hi"), sem("a_lo"))
        a_pv, a_ot, a_back, a_y = sem("a_pv"), sem("a_ot"), sem("a_back"), sem("a_y")
        a_sink, a_sink_exp, a_den = sem("a_sink"), sem("a_sink_exp"), sem("a_den")
        wo_in = [sem(f"wo_in{i}") for i in range(2)]
        wo_split = sem("wo_split")
        c_in = [sem(f"c_in{i}") for i in range(3)]
        c_sq, c_ssq, c_std, c_rstd, c_norm, c_gain, c_cat = (sem("c_sq"), sem("c_ssq"), sem("c_std"), sem("c_rstd"),
                                                             sem("c_norm"), sem("c_gain"), sem("c_cat"))
        c_turn, c_hi, c_lo, c_mm, c_scaled, c_out = (sem("c_turn"), sem("c_hi"), sem("c_lo"), sem("c_mm"),
                                                     sem("c_scaled"), sem("c_out"))
        carrier = {e: sem(f"wait_carrier_{e}") for e in ("pool", "dve")}
        stored = [sem(f"stored{i}") for i in range(2)]

        groups = ((0, 1), (1, 4), (4, 8))
        ROPE0 = 2
        BANK0 = 1

        def heads(ap, n):
            return ap.rearrange("p (h d) -> p h d", h=n)

        def wait_apart(name, engine, semaphore, value):
            engine.wait_ge(semaphore, value)
            if not isinstance(value, int):
                engine.sem_inc(carrier[name], 1)

        STEP0 = 6

        def steps(engine, step):
            for s in range(STEP0):
                step(0, s, True)
            with engine.Fori(0, HB - 1) as h:
                for s in range(STEP0, STEP0 + NT):
                    step(h, s, True)
            for s in range(STEP0, STEP0 + NT):
                step(HB - 1, s, s < NT)

        def head_q(h):
            return qk_b[:, 0, :, bass.ds(h * P, P)].rearrange("p t (c d) -> p t c d", c=2)

        def head_k(h):
            return qk_b[:, 1, :, bass.ds(h * P, P)].rearrange("p t (c d) -> p t c d", c=2)

        block = mem.enter_context(nc.Block())

        @block.sync
        def _(sp):
            sp.dma_start(par[:, :], params).then_inc(load, 16)
            sp.dma_start(cst[:, :], consts).then_inc(load, 16)
            sp.dma_start(pos_i, positions).then_inc(load, 16)
            for k in range(NK):
                if k >= 4:
                    sp.wait_ge(ada_sum, k - 3)
                sp.dma_start(ada[:, k % 4, :], w_ada[k * P:(k + 1) * P, 0:2 * D]).then_inc(ada_in[k % 4], 16)
                if k >= 2:
                    sp.wait_ge(x_turned, k - 1)
                sp.dma_start(x_in[:, k % 2, :], x[k * P:(k + 1) * P, :]).then_inc(x_loaded[k % 2], 16)
                if k < 4:
                    sp.dma_start(w_raw[:, k, :], w_in[k, :, :]).then_inc(w_loaded[k], 16)
            with sp.Fori(0, NFULL - 1) as ci:
                for k in range(4, 4 + NK):
                    sp.wait_ge(w_ready, ci * NK + k - 3)
                    sp.dma_start(w_raw[:, k % 4:k % 4 + 1, :],
                                 w_in[bass.ds(ci * NK + k, 1), :, :].rearrange("o p n -> p o n")
                                 ).then_inc(w_loaded[k % 4], 16)
            for k in range(4, NK):
                sp.wait_ge(w_ready, (NFULL - 1) * NK + k - 3)
                sp.dma_start(w_raw[:, k % 4, :], w_in[(NFULL - 1) * NK + k, :, :]).then_inc(w_loaded[k % 4], 16)
            for k in range(NK):
                sp.wait_ge(w_ready, NFULL * NK + k - 3)
                sp.dma_start(w_raw[:, k % 4, 0:4 * HD], w_kv[k, :, :]).then_inc(w_loaded[k % 4], 16)
            sp.wait_ge(b_lo, HB * NT)
            sp.wait_ge(b_back, HB * 4)
            for k in range(NK):
                if k >= 2:
                    sp.wait_ge(wo_split, 2 * (k - 1))
                sp.dma_start(wo_raw[:, k % 2, :], w_out[k * P:(k + 1) * P, :]).then_inc(wo_in[k % 2], 16)
            sp.wait_ge(a_y, NT)
            sp.dma_start(o_out[:, 0, :], b_gate.broadcast_to([P, D])).then_inc(bg_in, 16)
            for t in range(NT + 3):
                if t >= 3:
                    sp.wait_ge(c_out, t - 2)
                    sp.dma_start(out[(t - 3) * P:(t - 2) * P, :], o_out[:, (t - 3) % 2, :]
                                 ).then_inc(stored[(t - 3) % 2], 16)
                if t < NT:
                    sp.dma_start(gates[:, t % 3, :], gates_dram[t * P:(t + 1) * P, :]).then_inc(c_in[t % 3], 16)
                    sp.dma_start(x_res[:, t % 3, :], x[t * P:(t + 1) * P, :]).then_inc(c_in[t % 3], 16)
            for b in range(2):
                sp.wait_ge(stored[b], 16 * NT // 2)

        @block.gpsimd
        def _(pool):
            def rope(place, n_heads, t, m):
                n = n_heads * HD
                v = place.rearrange("p (h e d) -> p h e d", h=n_heads, e=2)
                c = tab[:, 0, t, :].unsqueeze(1).broadcast_to([P, n_heads, HD])
                s = tab[:, 1, t, :].rearrange("p (e d) -> p e d", e=2)
                r = rot[:, t % 2, 0:n].rearrange("p (h e d) -> p h e d", h=n_heads, e=2)
                pool.tensor_tensor(heads(sq[:, t % 2, 0:n], n_heads), heads(place, n_heads), c, ALU.mult
                                   ).then_inc(rot_step, 1)
                for e in range(2):
                    pool.tensor_tensor(r[:, :, e, :], v[:, :, 1 - e, :],
                                       s[:, e, :].unsqueeze(1).broadcast_to([P, n_heads, HD // 2]), ALU.mult
                                       ).then_inc(rot_step, 1)
                wait_apart("pool", pool, rot_step, 3 * m + 3)
                pool.tensor_tensor(place, sq[:, t % 2, 0:n], rot[:, t % 2, 0:n], ALU.add).then_inc(rope_done, 1)

            def tables(g, m0):
                wait_apart("pool", pool, rope_done, ROPE0 + m0)
                gain = heads(param("gain"), 4)[:, bass.ds(g, 1), :].rearrange("p o (e d) -> p o e d", e=2)
                swap = heads(param("gain_swapped"), 4)[:, bass.ds(g, 1), :].rearrange("p o (e d) -> p o e d", e=2)
                for i, w in enumerate((gain, swap)):
                    for e in range(2):
                        dst = tab[:, i, :, :].rearrange("p t (e d) -> p t e d", e=2)[:, :, e, :]
                        pool.tensor_tensor(dst, cos_sin[:, i, :, :],
                                           w[:, :, e, :].broadcast_to([P, NT, HD // 2]),
                                           ALU.mult).then_inc(table_done, 1)

            def norm_chunk(ci, g, place, n_heads):
                tables(g, g * NT)
                wait_apart("pool", pool, table_done, 4 * g + 4)
                for t in range(NT):
                    wait_apart("pool", pool, bank_free[t % 4], 2 * ci + t // 4 + 1 + BANK0)
                    rope(place(t), n_heads, t, g * NT + t)

            for b in range(4):
                pool.sem_inc(bank_free[b], BANK0)
            for b in range(2):
                pool.sem_inc(gate_stored[b], 16)
            pool.sem_inc(rope_done, ROPE0)
            pool.wait_ge(setup_act, 3)
            pool.wait_ge(setup_dve, 3)
            with pool.Fori(0, 2) as ci:
                norm_chunk(ci, ci, lambda t: qk_b[:, bass.ds(ci, 1), t, :].rearrange("p o c -> p (o c)"), 8)
            pool.wait_ge(h_ready, 3)
            for k in range(NK):
                if k >= 4:
                    pool.wait_ge(gate_sum, k - 3)
                pool.dma_start(gate_in[:, k % 4, :], w_ada[k * P:(k + 1) * P, 2 * D:3 * D]
                               ).then_inc(gate_loaded[k % 4], 16)
            norm_chunk(5, 2, lambda t: q_a[:, t, :], HA)
            norm_chunk(6, 3, lambda t: kv_a[:, t, 0:2 * HD], GA)

            wait_apart("pool", pool, rope_done, ROPE0 + 4 * NT)
            for b in range(4):
                pool.wait_ge(bank_free[b], 2 * (NFULL + 1) + BANK0)
            for b in range(2):
                pool.wait_ge(gate_stored[b], 16 * (1 + NT))

            def hi(dst, src, done):
                one = ones
                while len(one.shape) < len(src.shape):
                    one = one.unsqueeze(1)
                pool.tensor_tensor(dst, src, one.broadcast_to(list(src.shape)), ALU.mult).then_inc(done, 1)

            def lo(dst, src, high, done):
                pool.tensor_tensor(dst, src, high.bitcast(F32), ALU.subtract).then_inc(done, 1)

            def stage_high(h, c):
                if c == 0:
                    wait_apart("pool", pool, b_set, 6 * h)
                hi(q_st[:, :, c, 0, :], head_q(h)[:, :, c, :], b_stage)
                hi(q_st[:, :, c, 2, :], head_q(h)[:, :, c, :], b_stage)
                hi(k_st[:, :, c, 0, :], head_k(h)[:, :, c, :], b_stage)

            def stage_low(h):
                wait_apart("pool", pool, b_stage, 10 * h - 4)
                for c in range(2):
                    lo(q_st[:, :, c, 1, :], head_q(h)[:, :, c, :], q_st[:, :, c, 0, :], b_stage)
                    lo(k_st[:, :, c, 1, :], head_k(h)[:, :, c, :], k_st[:, :, c, 0, :], b_stage)

            def stage_v(h, half):
                r = slice(4 * half, 4 * half + 4)
                v = v_b[:, r, bass.ds(h * P, P)]
                hi(v_hi[:, r, :], v, b_v)
                wait_apart("pool", pool, b_v, 4 * h + 2 * half + 1)
                lo(v_lo[:, r, :], v, v_hi[:, r, :], b_v)

            def combine(h, s):
                wait_apart("pool", pool, b_small, 2 * (NT * h + s) + 2)
                pool.tensor_tensor(prob[:, 0, 1, :], prob[:, 0, 1, :],
                                   bst[:, 6, s % NT:s % NT + 1].broadcast_to([P, S]), ALU.mult
                                   ).then_inc(b_scaled, 1)
                wait_apart("pool", pool, b_scaled, 4 * h + s // 2 + 1)
                pool.tensor_tensor(prob[:, 0, 0, :], prob[:, 0, 0, :], prob[:, 0, 1, :], ALU.add
                                   ).then_inc(b_attn[0], 1)

            def between(h, more):
                combine(h, 6)
                combine(h, 8)
                wait_apart("pool", pool, b_v_free, h + 1)
                stage_v(h + 1, 0)
                combine(h, 10)
                wait_apart("pool", pool, b_pv, 4 * h + 4)
                stage_v(h + 1, 1)
                if more:
                    stage_high(h + 2, 0)
                combine(h, 12)
                if more:
                    stage_high(h + 2, 1)
                    stage_low(h + 2)

            stage_v(0, 0)
            stage_v(0, 1)
            combine(0, 0)
            stage_high(1, 0)
            combine(0, 2)
            stage_high(1, 1)
            stage_low(1)
            combine(0, 4)
            with pool.Fori(0, HB - 2) as h:
                between(h, True)
            between(HB - 2, False)
            combine(HB - 1, 6)

            pool.wait_ge(b_lo, HB * NT)
            pool.wait_ge(b_back, HB * 4)
            pool.wait_ge(b_y, HB * 4)
            ka = kv_a[:, :, 0:2 * HD].rearrange("p t (g d) -> p t g d", g=GA)
            for g in range(GA):
                hi(ka_st[:, :, g, 0, :], ka[:, :, g, :], a_kst)
            pool.wait_ge(a_kst, 2)
            for g in range(GA):
                lo(ka_st[:, :, g, 1, :], ka[:, :, g, :], ka_st[:, :, g, 0, :], a_kst)

            def stage_a(i, k0, nk, wait):
                if wait:
                    wait_apart("pool", pool, a_qset, 2 * i)
                q = heads(q_a[:, bass.ds(i, 1), :].rearrange("p o c -> p (o c)"), HA)
                hi(qa_st[:, :, 0, :], q, a_qst)
                hi(qa_st[:, :, 2, :], q, a_qst)
                wait_apart("pool", pool, a_qst, 3 * i + 1)
                lo(qa_st[:, :, 1, :], q, qa_st[:, :, 0, :], a_qst)
                if wait:
                    wait_apart("pool", pool, a_pv, 2 * i)
                for g in range(GA):
                    v = kv_a[:, bass.ds(k0, nk), 2 * HD + g * HD:2 * HD + (g + 1) * HD]
                    hi(va_st[:, 0:nk, g, 0, :], v, a_vst)
                    wait_apart("pool", pool, a_vst, 4 * i + 2 * g + 1)
                    lo(va_st[:, 0:nk, g, 1, :], v, va_st[:, 0:nk, g, 0, :], a_vst)

            def split_wo(k):
                pool.wait_ge(wo_in[k % 2], 16 * (k // 2 + 1))
                hi(wo_hi[:, k, :], wo_raw[:, k % 2, :], wo_split)
                pool.wait_ge(wo_split, 2 * k + 1)
                lo(wo_lo[:, k, :], wo_raw[:, k % 2, :], wo_hi[:, k, :], wo_split)

            stage_a(0, 0, 2, False)
            stage_a(1, 0, 3, True)
            for k in range(2):
                split_wo(k)
            for i in range(2, NT - 1):
                stage_a(i, i - 1, 3, True)
                split_wo(i)
            stage_a(NT - 1, NT - 2, 2, True)
            split_wo(NT - 1)

            pool.wait_ge(a_y, NT)

            def squares(t):
                if t >= 1:
                    pool.wait_ge(c_ssq, 2 * t - 1)
                yb = y_b[:, t, :]
                pool.tensor_tensor(y_sq[:, :], yb, yb, ALU.mult).then_inc(c_sq, 1)

            def gated(t):
                s = t % 2
                pool.wait_ge(c_in[t % 3], 32 * (t // 3 + 1))
                if t >= 2:
                    pool.wait_ge(c_turn, t - 1)
                pool.tensor_tensor(y_cat[:, s, 0:CW], q_a[:, t, :], gates[:, t % 3, 0:CW], ALU.mult
                                   ).then_inc(c_cat, 1)
                pool.wait_ge(c_norm, t + 1)
                pool.tensor_tensor(heads(y_cat[:, s, CW:D], HB), heads(y_b[:, t, :], HB),
                                   param("subln").unsqueeze(1).broadcast_to([P, HB, 2 * HD]), ALU.mult
                                   ).then_inc(c_gain, 1)
                pool.wait_ge(c_gain, t + 1)
                pool.tensor_tensor(y_cat[:, s, CW:D], y_cat[:, s, CW:D], gates[:, t % 3, CW:D], ALU.mult
                                   ).then_inc(c_cat, 1)

            def residual(t):
                s = t % 2
                pool.wait_ge(c_scaled, t + 1)
                pool.tensor_tensor(o_out[:, s, :], o_out[:, s, :], x_res[:, t % 3, :], ALU.add).then_inc(c_out, 1)

            squares(0)
            gated(0)
            squares(1)
            for t in range(NT):
                if t + 1 < NT:
                    gated(t + 1)
                if t + 2 < NT:
                    squares(t + 2)
                if t >= 1:
                    residual(t - 1)
            residual(NT - 1)

        @block.scalar
        def _(act):
            act.wait_ge(load, 48)
            act.activation(silu_c, param("c"), ACT.Silu).then_inc(setup_act, 1)
            act.wait_ge(setup_dve, 4)
            act.activation(cos_sin[:, 0, :, :].rearrange("p t d -> p (t d)"), ang_c, ACT.Sin).then_inc(setup_act, 1)
            act.activation(cos_sin[:, 1, :, :].rearrange("p t d -> p (t d)"), ang_r, ACT.Sin).then_inc(setup_act, 1)

            def split_w(k):
                act.wait_ge(w_loaded[k % 4], 16 * (k // 4 + 1))
                act.activation(w_hi[:, k, :], w_raw[:, k % 4, :], ACT.Copy).then_inc(w_hi_done, 1)

            act.wait_ge(setup_act, 3)
            for k in range(NK):
                act.wait_ge(x_loaded[k % 2], 16 * (k // 2 + 1))
                if k >= 1:
                    act.wait_ge(x_mean, k)
                act.activation(sq[:, :, :].rearrange("p a c -> p (a c)"), x_in[:, k % 2, :], ACT.Square,
                               accum_out=x_ssq[:, k:k + 1]).then_inc(x_squared, 1)
                if k < 4:
                    split_w(k)
                act.wait_ge(x_mean, k + 1)
                act.activation(x_std[:, k:k + 1], x_ms[:, k:k + 1], ACT.Sqrt).then_inc(x_root, 1)
                act.wait_ge(x_turned, k + 1)
                for half in range(2):
                    act.activation(x_t[half][:, :, k * P:(k + 1) * P], ps[2 + k % 2][:, half, :].rearrange(
                        "p (k s) -> p k s", k=4), ACT.Copy).then_inc(x_kept, 1)
            for k in range(4, NK):
                split_w(k)
            act.wait_ge(mod_done, 2)
            act.wait_ge(x_kept, 2 * NK)
            for a, b in groups:
                for k in range(NK):
                    place = x_t[k // 4][:, k % 4, a * P:b * P]
                    act.activation(place, place, ACT.Identity, bias=shift_b[:, k:k + 1],
                                   scale=scale_a[:, k:k + 1]).then_inc(h_affine, 1)

            def refill(ci, n):
                for k in range(NK):
                    if k < NK - 1:
                        act.wait_ge(w_slot_free, (NK - 1) * ci + k + 1)
                    else:
                        act.wait_ge(proj_done, NT * ci + NT)
                    act.wait_ge(w_loaded[k % 4], 32 * ci + 16 * (k // 4) + 48)
                    act.activation(w_hi[:, k, 0:n], w_raw[:, k % 4, 0:n], ACT.Copy).then_inc(w_hi_done, 1)

            def norm_tile(ci, t, m, n):
                act.wait_ge(proj_done, NT * ci + t + 1)
                act.wait_ge(rope_done, m + t + 1)
                act.activation(sq[:, t % 2, 0:n], acc[t % 4][:, 0:n], ACT.Square).then_inc(squared, 1)
                act.wait_ge(ssq_done, 2 * (m + t) + 2)
                act.activation(stat[:, 2, t, 0:n // HD], stat[:, 1, t, 0:n // HD], ACT.Sqrt).then_inc(std_done, 1)

            def copy_tile(ci, t):
                act.wait_ge(proj_done, NT * ci + t + 1)
                act.activation(v_b[:, t, :], acc[t % 4], ACT.Copy).then_inc(bank_free[t % 4], 1)

            def gate_tile(ci, t):
                act.wait_ge(proj_done, NT * ci + t + 1)
                act.wait_ge(gate_stored[t % 2], (ci - 3) * (16 * NT // 2) + 16 * (t // 2) + 16)
                act.activation(sq[:, t % 2, :], acc[t % 4], ACT.Silu).then_inc(bank_free[t % 4], 1)
                act.wait_ge(bank_free[t % 4], 2 * ci + t // 4 + 1 + BANK0)
                act.dma_start(gates_dram[t * P:(t + 1) * P, bass.ds((ci - 3) * CW, CW)], sq[:, t % 2, :]
                              ).then_inc(gate_stored[t % 2], 16)

            with act.Fori(0, 2) as ci:
                for t in range(NT - 1):
                    norm_tile(ci, t, ci * NT, CW)
                refill(ci, CW)
                norm_tile(ci, NT - 1, ci * NT, CW)
            act.wait_ge(gate_sum, NK)
            for t in range(NT - 1):
                copy_tile(2, t)
            refill(2, CW)
            copy_tile(2, NT - 1)
            act.wait_ge(rope_done, ROPE0 + 2 * NT)
            with act.Fori(3, 5) as ci:
                for t in range(NT - 1):
                    gate_tile(ci, t)
                refill(ci, CW)
                gate_tile(ci, NT - 1)
            for b in range(2):
                act.wait_ge(gate_stored[b], 16 * (1 + NT))
            for t in range(NT - 1):
                norm_tile(5, t, 2 * NT, CW)
            refill(5, 4 * HD)
            norm_tile(5, NT - 1, 2 * NT, CW)
            for t in range(NT):
                norm_tile(6, t, 3 * NT, 2 * HD)

            act.wait_ge(setup_dve, 6)
            act.activation(lam_exp, lam_sum, ACT.Exp).then_inc(setup_act, 1)

            act.wait_ge(proj_done, NPROJ)
            for place, src in ((0, 0), (2, 0)):
                act.activation(q_st[:, :, :, place, :], head_q(0), ACT.Copy).then_inc(b_first_hi, 1)
                if place == 0:
                    act.activation(k_st[:, :, :, 0, :], head_k(0), ACT.Copy).then_inc(b_first_hi, 1)

            def set_copy(h, n):
                act.wait_ge(b_set, 6 * h + n + 1)
                act.activation((q1t, q2t, kt)[n % 3][:, n // 3, :],
                               ps[n % 2][:, :, :].rearrange("p a c -> p (a c)"), ACT.Copy).then_inc(b_set_act, 1)

            for n in (0, 2, 4):
                set_copy(0, n)

            def o_copy(h, s, new):
                if s % 2 == 1 and s >= 5 and (new or s < NT + 5):
                    m = (s - 5) // 2
                    act.wait_ge(b_pv, 4 * h + m + 1)
                    act.activation(o_tb[:, m % 2, :], ps[3][:, 0, (m % 2) * 2 * P:(m % 2 + 1) * 2 * P], ACT.Copy
                                   ).then_inc(b_ot, 1)

            def step(h, s, new):
                g = NT * h + s
                if s >= 2 and (new or s < NT + 2):
                    act.wait_ge(b_turn, g - 1)
                    act.activation(at_hi[:, :, (s - 2) // 2 % 2, (s % 2) * P:(s % 2 + 1) * P],
                                   ps[2][:, :, :].rearrange("p a (k s) -> p (a k) s", k=4), ACT.Copy
                                   ).then_inc(b_hi, 1)
                if not new:
                    o_copy(h, s, new)
                    return
                for c in range(2):
                    act.wait_ge(b_max, 2 * g + c + 1)
                    act.activation(prob[:, s % 2, c, :], ps[c][:, :, :].rearrange("p a c -> p (a c)"), ACT.Exp,
                                   bias=bst[:, c, s % NT:s % NT + 1],
                                   accum_out=bst[:, 2 + c, s % NT:s % NT + 1]).then_inc(b_exp, 1)
                if s == NT - 1 and not (isinstance(h, int) and h == HB - 1):
                    for n in (0, 2, 4):
                        set_copy(h + 1, n)
                o_copy(h, s, new)

            steps(act, step)

            act.wait_ge(a_kset, 1)
            act.activation(kta[:, 0, :], ps[0][:, :, :].rearrange("p a c -> p (a c)"), ACT.Copy).then_inc(a_kt_act, 1)

            def q_copy(i):
                act.wait_ge(a_qset, 2 * i + 1)
                act.activation(qa1[:, :, :].rearrange("p h s -> p (h s)"),
                               ps[3][:, :, :].rearrange("p a c -> p (a c)"), ACT.Copy).then_inc(a_qt_act, 1)

            def pa_hi(i, hh, nk):
                act.wait_ge(a_turn, HA * i + hh + 1)
                act.activation(pt_hi[:, hh // 4, 0:nk, (hh % 4) * P:(hh % 4 + 1) * P],
                               ps[1][:, hh % 2, 0:nk * P].rearrange("p (k s) -> p k s", k=nk), ACT.Copy
                               ).then_inc(a_hi, 1)

            def oa_copy(i, g):
                act.wait_ge(a_pv, 2 * i + g + 1)
                act.activation(o_ta[:, g, :], ps[2][:, 0, :], ACT.Copy).then_inc(a_ot, 1)

            def tile_a(i, nk, first, last):
                for hh in range(HA):
                    act.wait_ge(a_neg, HA * i + hh + 1)
                    if hh >= 4:
                        act.wait_ge(a_turn, HA * i + hh - 3)
                    act.activation(prob_a[:, hh % 4, 0:nk * P], masked[:, hh % 2, 0:nk * P], ACT.Exp,
                                   bias=ast[:, 1, hh:hh + 1], accum_out=ast[:, 2, hh:hh + 1]).then_inc(a_exp, 1)
                    if hh >= 1:
                        pa_hi(i, hh - 1, nk)
                    if hh == 1 and not first:
                        oa_copy(i - 1, 1)
                    if hh == 7:
                        oa_copy(i, 0)
                pa_hi(i, HA - 1, nk)
                act.wait_ge(a_sink, i + 1)
                act.activation(ast[:, 4, :], ast[:, 3, :], ACT.Exp).then_inc(a_sink_exp, 1)
                if not last:
                    q_copy(i + 1)
                else:
                    oa_copy(i, 1)

            q_copy(0)
            tile_a(0, 2, True, False)
            with act.Fori(1, NT - 1) as i:
                tile_a(i, 3, False, False)
            tile_a(NT - 1, 2, False, True)

            def root(t):
                act.wait_ge(c_ssq, 2 * t + 2)
                act.activation(cst3[:, 2, t, :], cst3[:, 1, t, :], ACT.Sqrt).then_inc(c_std, 1)

            def y_hi(t):
                act.wait_ge(c_turn, t + 1)
                act.activation(yt_hi[:, t % 2, :, :].rearrange("p k s -> p (k s)"),
                               ps[2][:, :, :].rearrange("p a c -> p (a c)"), ACT.Copy).then_inc(c_hi, 1)

            for t in range(NT):
                root(t)
                y_hi(t)

        @block.vector
        def _(dve):
            dve.memset(ones, 1.0).then_inc(setup_dve, 1)
            dve.wait_ge(load, 48)
            dve.tensor_tensor(param("gain"), param("gain"), const("gain_scale"), ALU.mult).then_inc(setup_dve, 1)
            dve.tensor_tensor(param("gain_swapped"), param("gain_swapped"), const("swap_scale"), ALU.mult
                              ).then_inc(setup_dve, 1)
            n_trig = [0]

            def link(instruction):
                n_trig[0] += 1
                instruction.then_inc(trig_step, 1)
                dve.wait_ge(trig_step, n_trig[0])

            link(dve.tensor_copy(ident_r[:, :], const("identity")))
            link(dve.tensor_copy(pos_f, pos_i))
            link(dve.tensor_tensor(ang.rearrange("p (t d) -> p t d", t=NT),
                                   pos_f.unsqueeze(2).broadcast_to([P, NT, HD // 2]),
                                   const("inv_freq").unsqueeze(1).broadcast_to([P, NT, HD // 2]), ALU.mult))
            for place, turn in ((ang_r, 0.0), (ang_c, 0.25)):
                link(dve.tensor_scalar(ang_n, ang, 1.0 / (2 * np.pi), turn, ALU.mult, ALU.add))
                link(dve.tensor_scalar(ang_n, ang_n, MAGIC, MAGIC, ALU.add, ALU.subtract))
                src = ang
                for part in two_pi_parts():
                    link(dve.scalar_tensor_tensor(place, ang_n, -part, src, ALU.mult, ALU.add))
                    src = place
                link(dve.tensor_scalar(place, place, turn * 2 * np.pi, PI_IN, ALU.add, ALU.min))
                link(dve.tensor_scalar(place, place, -PI_IN, None, ALU.max))
            dve.tensor_copy(small[:, 80:81], ones).then_inc(setup_dve, 1)

            def low_w(k):
                dve.wait_ge(w_hi_done, k + 1)
                dve.tensor_tensor(w_lo[:, k, :], w_raw[:, k % 4, :], w_hi[:, k, :].bitcast(F32), ALU.subtract
                                  ).then_inc(w_ready, 1)

            acc2 = mod_acc[:, :]
            for k in range(NK):
                dve.wait_ge(ada_in[k % 4], 16 * (k // 4 + 1))
                if k == 0:
                    dve.wait_ge(setup_act, 1)
                    dve.tensor_scalar(acc2, ada[:, 0, :], silu_c[:, 0:1], None, ALU.mult).then_inc(ada_sum, 1)
                else:
                    dve.wait_ge(ada_sum, k)
                    dve.scalar_tensor_tensor(acc2, ada[:, k % 4, :], silu_c[:, k:k + 1], acc2, ALU.mult, ALU.add
                                             ).then_inc(ada_sum, 1)
                dve.wait_ge(x_squared, k + 1)
                dve.tensor_scalar(x_ms[:, k:k + 1], x_ssq[:, k:k + 1], 1.0 / D, EPS, ALU.mult, ALU.add
                                  ).then_inc(x_mean, 1)
                if k < 4:
                    low_w(k)
                dve.wait_ge(x_root, k + 1)
                dve.reciprocal(x_rstd[:, k:k + 1], x_std[:, k:k + 1]).then_inc(x_recip, 1)
                dve.wait_ge(x_recip, k + 1)
                dve.tensor_scalar(x_in[:, k % 2, :], x_in[:, k % 2, :], x_rstd[:, k:k + 1], None, ALU.mult
                                  ).then_inc(x_normed, 1)
            for k in range(4, NK):
                low_w(k)
            dve.wait_ge(mod_cols, 1)
            dve.tensor_tensor(shift_b, ps[0][:, 0, 0:8], param("b_shift"), ALU.add).then_inc(mod_done, 1)
            link(dve.tensor_tensor(scale_a, ps[0][:, 0, 8:16], param("b_scale"), ALU.add))
            dve.scalar_tensor_tensor(scale_a, scale_a, 1.0, param("norm_gain"), ALU.add, ALU.mult
                                     ).then_inc(mod_done, 1)
            for n, (a, b) in enumerate(groups):
                for half in range(2):
                    dve.wait_ge(h_affine, NK * n + 4 * half + 4)
                    dve.tensor_copy(h_hi[:, 4 * half:4 * half + 4, a * P:b * P], x_t[half][:, :, a * P:b * P]
                                    ).then_inc(h_split, 1)
                for half in range(2):
                    dve.wait_ge(h_split, 2 * n + half + 1)
                    low = dve.tensor_tensor(h_lo[:, 4 * half:4 * half + 4, a * P:b * P],
                                            x_t[half][:, :, a * P:b * P],
                                            h_hi[:, 4 * half:4 * half + 4, a * P:b * P].bitcast(F32), ALU.subtract)
                low.then_inc(h_ready, 1)

            def refill(ci, n):
                for k in range(NK):
                    dve.wait_ge(w_hi_done, NK * ci + k + NK + 1)
                    dve.tensor_tensor(w_lo[:, k, 0:n], w_raw[:, k % 4, 0:n], w_hi[:, k, 0:n].bitcast(F32),
                                      ALU.subtract).then_inc(w_ready, 1)

            def norm_tile(ci, t, m, place, n):
                nh = n // HD
                dve.wait_ge(squared, m + t + 1)
                dve.tensor_reduce(stat[:, 0, t, 0:nh], heads(sq[:, t % 2, 0:n], nh), AXX, ALU.add
                                  ).then_inc(ssq_done, 1)
                dve.wait_ge(ssq_done, 2 * (m + t) + 1)
                dve.tensor_scalar(stat[:, 1, t, 0:nh], stat[:, 0, t, 0:nh], 1.0 / HD, EPS, ALU.mult, ALU.add
                                  ).then_inc(ssq_done, 1)
                dve.wait_ge(std_done, m + t + 1)
                dve.reciprocal(stat[:, 3, t, 0:nh], stat[:, 2, t, 0:nh]).then_inc(rstd_done, 1)
                dve.wait_ge(rstd_done, m + t + 1)
                if n < CW:
                    dve.tensor_copy(kv_a[:, t, 2 * HD:4 * HD], acc[t % 4][:, 2 * HD:4 * HD])
                dve.tensor_tensor(heads(place, nh), heads(acc[t % 4][:, 0:n], nh),
                                  stat[:, 3, t, 0:nh].unsqueeze(2).broadcast_to([P, nh, HD]), ALU.mult
                                  ).then_inc(bank_free[t % 4], 1)

            def norm_chunk(ci, m, place, n, next_n):
                for t in range(NT - 1):
                    norm_tile(ci, t, m, place(t), n)
                if next_n:
                    refill(ci, next_n)
                norm_tile(ci, NT - 1, m, place(NT - 1), n)

            with dve.Fori(0, 2) as ci:
                norm_chunk(ci, ci * NT, lambda t: qk_b[:, bass.ds(ci, 1), t, :].rearrange("p o c -> p (o c)"),
                           CW, CW)
            for k in range(NK):
                dve.wait_ge(gate_loaded[k % 4], 16 * (k // 4 + 1))
                if k == 0:
                    dve.tensor_scalar(gate_row[:, :], gate_in[:, 0, :], silu_c[:, 0:1], None, ALU.mult
                                      ).then_inc(gate_sum, 1)
                else:
                    dve.wait_ge(gate_sum, k)
                    dve.scalar_tensor_tensor(gate_row[:, :], gate_in[:, k % 4, :], silu_c[:, k:k + 1],
                                             gate_row[:, :], ALU.mult, ALU.add).then_inc(gate_sum, 1)
            lam = param("lambdas").rearrange("p (a b d) -> p a b d", a=2, b=2)
            link(dve.tensor_tensor(lam[:, :, 0, :], lam[:, :, 0, :], lam[:, :, 1, :], ALU.mult))
            dve.tensor_reduce(lam_sum, lam[:, :, 0, :], AXX, ALU.add).then_inc(setup_dve, 1)
            dve.tensor_scalar(param("subln"), param("subln"), 1.0 - LAMBDA_INIT, None, ALU.mult
                              ).then_inc(setup_dve, 1)
            refill(2, CW)
            with dve.Fori(3, 5) as ci:
                refill(ci, CW)
            norm_chunk(5, 2 * NT, lambda t: q_a[:, t, :], CW, 4 * HD)
            norm_chunk(6, 3 * NT, lambda t: kv_a[:, t, 0:2 * HD], 2 * HD, 0)

            dve.wait_ge(setup_act, 4)
            link(dve.tensor_scalar(neg_lam, lam_exp[:, 1:2], lam_exp[:, 0:1], -LAMBDA_INIT, ALU.subtract, ALU.add))

            for n, (st, src) in enumerate(((q_st, head_q(0)), (k_st, head_k(0)))):
                dve.wait_ge(b_first_hi, n + 1)
                dve.tensor_tensor(st[:, :, :, 1, :], src, st[:, :, :, 0, :].bitcast(F32), ALU.subtract
                                  ).then_inc(b_first_lo, 1)

            def set_copy(h, n):
                dve.wait_ge(b_set, 6 * h + n + 1)
                dve.tensor_copy((q1t, q2t, kt)[n % 3][:, n // 3, :],
                                ps[n % 2][:, :, :].rearrange("p a c -> p (a c)")).then_inc(b_set_dve, 1)

            for n in (1, 3, 5):
                set_copy(0, n)

            def write_y(h, s):
                if s % 2 == 1 and s >= 7:
                    m = (s - 7) // 2
                    dve.wait_ge(b_back, 4 * h + m + 1)
                    dve.tensor_tensor(y_b[:, 2 * (m % 4):2 * (m % 4) + 2, bass.ds((h + m // 4) * P, P)],
                                      ps[3][:, 1, (m % 2) * 2 * P:(m % 2 + 1) * 2 * P].rearrange(
                                          "p (t d) -> p t d", t=2),
                                      bst[:, 4, 2 * (m % 4):2 * (m % 4) + 2].unsqueeze(2).broadcast_to([P, 2, P]),
                                      ALU.mult).then_inc(b_y, 1)

            def step(h, s, new):
                g = NT * h + s
                j = s % NT
                if new:
                    for c in range(2):
                        dve.wait_ge(b_qk, 2 * g + c + 1)
                        dve.tensor_reduce(bst[:, c, j:j + 1], ps[c][:, :, :].rearrange("p a c -> p (a c)"), AXX,
                                          ALU.max, negate=True).then_inc(b_max, 1)
                if s >= 2 and (new or s < NT + 2):
                    dve.wait_ge(b_hi, g - 1)
                    place = slice((s % 2) * P, (s % 2 + 1) * P)
                    dve.tensor_tensor(at_lo[:, :, (s - 2) // 2 % 2, place],
                                      ps[2][:, :, :].rearrange("p a (k s) -> p (a k) s", k=4),
                                      at_hi[:, :, (s - 2) // 2 % 2, place].bitcast(F32), ALU.subtract
                                      ).then_inc(b_lo, 1)
                write_y(h, s)
                if not new:
                    return
                if s == NT - 1 and not (isinstance(h, int) and h == HB - 1):
                    for n in (1, 3, 5):
                        set_copy(h + 1, n)
                dve.wait_ge(b_exp, 2 * g + 2)
                dve.reciprocal(bst[:, 4:6, j:j + 1], bst[:, 2:4, j:j + 1]).then_inc(b_small, 1)
                dve.wait_ge(b_small, 2 * g + 1)
                dve.scalar_tensor_tensor(bst[:, 6, j:j + 1], bst[:, 2, j:j + 1], bst[:, 5, j:j + 1], neg_lam,
                                         ALU.mult, ALU.mult).then_inc(b_small, 1)
                if s % 2 == 1:
                    dve.wait_ge(b_small, 2 * g + 2)
                    dve.scalar_tensor_tensor(prob[:, 1, 0, :], prob[:, 1, 1, :], bst[:, 6, j:j + 1],
                                             prob[:, 1, 0, :], ALU.mult, ALU.add).then_inc(b_attn[1], 1)

            steps(dve, step)

            dve.wait_ge(a_kset, 2)
            dve.tensor_copy(kta[:, 1, :], ps[1][:, :, :].rearrange("p a c -> p (a c)")).then_inc(a_kt_dve, 1)

            def q_copy(i):
                dve.wait_ge(a_qset, 2 * i + 2)
                dve.tensor_copy(qa2[:, :, :].rearrange("p h s -> p (h s)"),
                                ps[3][:, :, :].rearrange("p a c -> p (a c)")).then_inc(a_qt_dve, 1)

            def pa_lo(i, hh, nk):
                dve.wait_ge(a_hi, HA * i + hh + 1)
                place = slice((hh % 4) * P, (hh % 4 + 1) * P)
                dve.tensor_tensor(pt_lo[:, hh // 4, 0:nk, place],
                                  ps[1][:, hh % 2, 0:nk * P].rearrange("p (k s) -> p k s", k=nk),
                                  pt_hi[:, hh // 4, 0:nk, place].bitcast(F32), ALU.subtract).then_inc(a_lo, 1)

            def write_ya(i):
                dve.wait_ge(a_back, 2 * i + 2)
                dve.tensor_tensor(q_a[:, bass.ds(i, 1), :].rearrange("p o (h d) -> p (o h) d", h=HA),
                                  heads(ps[2][:, 1, :], HA),
                                  ast[:, 6, :].unsqueeze(2).broadcast_to([P, HA, HD]), ALU.mult).then_inc(a_y, 1)

            def tile_a(i, nk, first, last):
                off = P if first else 0
                for hh in range(HA):
                    wait_apart("dve", dve, a_qk, HA * i + hh + 1)
                    if hh >= 2:
                        wait_apart("dve", dve, a_exp, HA * i + hh - 1)
                    dve.tensor_tensor_reduce(out=masked[:, hh % 2, 0:nk * P], in0=ps[0][:, hh % 2, 0:nk * P],
                                             in1=const("band")[:, off:off + nk * P], scale=1.0,
                                             scalar=param("sink")[:, hh:hh + 1], op0=ALU.add, op1=ALU.max,
                                             accum_out=ast[:, 0, hh:hh + 1]).then_inc(a_max, 1)
                    dve.wait_ge(a_max, HA * i + hh + 1)
                    dve.tensor_scalar(ast[:, 1, hh:hh + 1], ast[:, 0, hh:hh + 1], -1.0, None, ALU.mult
                                      ).then_inc(a_neg, 1)
                    if hh >= 2:
                        pa_lo(i, hh - 2, nk)
                    if hh == 4 and not first:
                        write_ya(i - 1)
                dve.wait_ge(a_neg, HA * i + HA)
                dve.tensor_tensor(ast[:, 3, :], ast[:, 1, :], param("sink"), ALU.add).then_inc(a_sink, 1)
                pa_lo(i, 6, nk)
                pa_lo(i, 7, nk)
                dve.wait_ge(a_sink_exp, i + 1)
                dve.tensor_tensor(ast[:, 5, :], ast[:, 4, :], ast[:, 2, :], ALU.add).then_inc(a_den, 1)
                dve.wait_ge(a_den, 2 * i + 1)
                dve.reciprocal(ast[:, 6, :], ast[:, 5, :]).then_inc(a_den, 1)
                if not last:
                    q_copy(i + 1)
                else:
                    dve.wait_ge(a_den, 2 * i + 2)
                    write_ya(i)

            q_copy(0)
            tile_a(0, 2, True, False)
            with dve.Fori(1, NT - 1) as i:
                tile_a(i, 3, False, False)
            tile_a(NT - 1, 2, False, True)

            dve.wait_ge(gate_mm, 1)
            dve.wait_ge(bg_in, 16)
            dve.wait_ge(a_den, 2 * NT)
            dve.tensor_tensor(gate_row[:, :], ps[3][:, :, :].rearrange("p a c -> p (a c)"),
                              o_out[:, 0, :], ALU.add).then_inc(gate_done, 1)

            def statistics(t):
                dve.wait_ge(c_sq, t + 1)
                dve.tensor_reduce(cst3[:, 0, t, :], heads(y_sq[:, :], HB), AXX, ALU.add).then_inc(c_ssq, 1)
                dve.wait_ge(c_ssq, 2 * t + 1)
                dve.tensor_scalar(cst3[:, 1, t, :], cst3[:, 0, t, :], 1.0 / (2 * HD), EPS, ALU.mult, ALU.add
                                  ).then_inc(c_ssq, 1)
                dve.wait_ge(c_std, t + 1)
                dve.reciprocal(cst3[:, 3, t, :], cst3[:, 2, t, :]).then_inc(c_rstd, 1)
                dve.wait_ge(c_rstd, t + 1)
                dve.tensor_tensor(heads(y_b[:, t, :], HB), heads(y_b[:, t, :], HB),
                                  cst3[:, 3, t, :].unsqueeze(2).broadcast_to([P, HB, 2 * HD]), ALU.mult
                                  ).then_inc(c_norm, 1)

            def y_low(t):
                dve.wait_ge(c_hi, t + 1)
                dve.tensor_tensor(yt_lo[:, t % 2, :, :].rearrange("p k s -> p (k s)"),
                                  ps[2][:, :, :].rearrange("p a c -> p (a c)"),
                                  yt_hi[:, t % 2, :, :].rearrange("p k s -> p (k s)").bitcast(F32), ALU.subtract
                                  ).then_inc(c_lo, 1)

            def scaled(t):
                dve.wait_ge(c_mm, t + 1)
                if t >= 2:
                    dve.wait_ge(stored[t % 2], 16 * (t // 2))
                dve.tensor_tensor(o_out[:, t % 2, :], ps[t % 2][:, :, :].rearrange("p a c -> p (a c)"),
                                  gate_row[:, :], ALU.mult).then_inc(c_scaled, 1)

            statistics(0)
            for t in range(NT):
                if t + 1 < NT:
                    statistics(t + 1)
                y_low(t)
                if t >= 1:
                    scaled(t - 1)
            scaled(NT - 1)

        @block.tensor
        def _(pe):
            ident = const("identity")
            pe.wait_ge(load, 48)
            pe.wait_ge(setup_dve, 4)
            for t in range(NT):
                pe.wait_ge(x_normed, t + 1)
                if t >= 2:
                    pe.wait_ge(x_kept, 2 * (t - 1))
                for k in range(NK):
                    last = pe.transpose(ps[2 + t % 2][:, k // 4, (k % 4) * P:(k % 4 + 1) * P],
                                        x_in[:, t % 2, k * P:(k + 1) * P], ident)
                last.then_inc(x_turned, 1)
            pe.wait_ge(ada_sum, NK)
            for j in range(16):
                last = pe.matmul(ps[0][:, 0, j:j + 1], mod_acc[:, j * P:(j + 1) * P], ones, start=True, stop=True)
            last.then_inc(mod_cols, 1)
            pe.wait_ge(mod_done, 2)

            def proj_chunk(ci, n):
                for t in range(NT):
                    pe.wait_ge(bank_free[t % 4], 2 * ci + t // 4 + BANK0)
                    if t in (0, 1, 4):
                        pe.wait_ge(h_ready, (0, 1, 4).index(t) + 1)
                    tok = slice(t * P, (t + 1) * P)
                    for k in range(NK):
                        if t == 0:
                            pe.wait_ge(w_ready, NK * ci + k + 1)
                        pe.matmul(acc[t % 4][:, 0:n], h_hi[:, k, tok], w_hi[:, k, 0:n], start=(k == 0), stop=False)
                        pe.matmul(acc[t % 4][:, 0:n], h_hi[:, k, tok], w_lo[:, k, 0:n], start=False, stop=False)
                        last = pe.matmul(acc[t % 4][:, 0:n], h_lo[:, k, tok], w_hi[:, k, 0:n], start=False,
                                         stop=(k == NK - 1))
                        if t == NT - 1 and k < NK - 1:
                            last.then_inc(w_slot_free, 1)
                    last.then_inc(proj_done, 1)

            with pe.Fori(0, NFULL) as ci:
                proj_chunk(ci, CW)
            proj_chunk(NFULL, 4 * HD)

            def sets(h, which):
                if which[0] > 0:
                    pass
                elif isinstance(h, int):
                    pe.wait_ge(b_first_hi, 3)
                    pe.wait_ge(b_first_lo, 2)
                else:
                    pe.wait_ge(b_stage, 10 * h)
                for n in which:
                    if n >= 2 and n % 2 == 0:
                        pe.wait_ge(b_set_act, 3 * h + n // 2)
                    elif n >= 2:
                        pe.wait_ge(b_set_dve, 3 * h + n // 2)
                    elif not isinstance(h, int):
                        pe.wait_ge(b_exp, 2 * NT * h + n - 1)
                    c, kind = n // 3, n % 3
                    for t in range(NT):
                        src = (q_st[:, t, c, 0:2, :], q_st[:, t, c, 1:3, :], k_st[:, t, c, :, :])[kind]
                        last = pe.transpose(ps[n % 2][:, t // 4, (t % 4) * P:(t % 4 + 1) * P].bitcast(F32R),
                                            src.rearrange("p a d -> p (a d)"), ident_r[:, :])
                    last.then_inc(b_set, 1)

            def scores(h, j, c):
                if j == 0:
                    pe.wait_ge(b_set_act, 3 * h + 3)
                    pe.wait_ge(b_set_dve, 3 * h + (1 if c == 0 else 3))
                else:
                    pe.wait_ge(b_exp, 2 * (NT * h + j) + c - 1)
                q = slice(j * P, (j + 1) * P)
                for half in range(2):
                    kk = kt[:, c, half * 512:(half + 1) * 512]
                    pe.matmul(ps[c][:, half, :], q1t[:, c, q], kk, start=True, stop=False)
                    last = pe.matmul(ps[c][:, half, :], q2t[:, c, q], kk, start=False, stop=True)
                last.then_inc(b_qk, 1)

            def turn(h, j):
                pe.wait_ge(b_attn[j % 2], 4 * h + j // 2 + 1)
                if not (isinstance(h, int) and h == 0 and j == 0):
                    pe.wait_ge(b_lo, NT * h + j)
                for k in range(NT):
                    last = pe.transpose(ps[2][:, k // 4, (k % 4) * P:(k % 4 + 1) * P],
                                        prob[:, j % 2, 0, k * P:(k + 1) * P], ident)
                last.then_inc(b_turn, 1)

            def pv(h, m, half):
                if half == 0:
                    pe.wait_ge(b_lo, NT * h + 2 * m + 2)
                    if not (isinstance(h, int) and h == 0 and m == 0):
                        pe.wait_ge(b_ot, 4 * h + m)
                pe.wait_ge(b_v, 4 * (h + m // 4) + 2 * half + 2)
                o = ps[3][:, 0, (m % 2) * 2 * P:(m % 2 + 1) * 2 * P]
                for k in range(4 * half, 4 * half + 4):
                    pe.matmul(o, v_hi[:, k, :], at_hi[:, k, m % 2, :], start=(k == 0), stop=False)
                    pe.matmul(o, v_hi[:, k, :], at_lo[:, k, m % 2, :], start=False, stop=False)
                    last = pe.matmul(o, v_lo[:, k, :], at_hi[:, k, m % 2, :], start=False, stop=(k == NT - 1))
                if half == 1:
                    last.then_inc(b_pv, 1)
                elif m == 3:
                    last.then_inc(b_v_free, 1)

            def back(h, m):
                pe.wait_ge(b_ot, 4 * h + m + 1)
                pe.wait_ge(b_y, 4 * h + m)
                for t in range(2):
                    last = pe.transpose(ps[3][:, 1, (2 * (m % 2) + t) * P:(2 * (m % 2) + t + 1) * P],
                                        o_tb[:, m % 2, t * P:(t + 1) * P], ident)
                last.then_inc(b_back, 1)

            def step(h, s, new):
                change = s == NT - 1
                more = new and not (isinstance(h, int) and h == HB - 1 and change)
                head, j = (h + 1, s + 1 - NT) if s + 1 >= NT else (h, s + 1)
                if more and not change:
                    scores(head, j, 0)
                if more and change:
                    sets(head, (0, 1))
                if s >= 1 and (new or s < NT + 1):
                    turn(h, s - 1)
                if more and change:
                    sets(head, (2, 3, 4, 5))
                    scores(head, 0, 0)
                    scores(head, 0, 1)
                if more and not change:
                    scores(head, j, 1)
                if s >= 6 and s % 2 == 0:
                    back(h, (s - 6) // 2)
                if s >= 3 and (new or s < NT + 3):
                    pv(h, (s - 3) // 2, (s - 3) % 2)

            sets(0, range(6))
            scores(0, 0, 0)
            scores(0, 0, 1)
            steps(pe, step)

            pe.wait_ge(a_kst, 4)
            for g in range(GA):
                for t in range(NT):
                    last = pe.transpose(ps[g][:, t // 4, (t % 4) * P:(t % 4 + 1) * P].bitcast(F32R),
                                        ka_st[:, t, g, :, :].rearrange("p a d -> p (a d)"), ident_r[:, :])
                last.then_inc(a_kset, 1)

            def q_sets(i):
                pe.wait_ge(a_qst, 3 * i + 3)
                for n in range(2):
                    if n == 1:
                        pe.wait_ge(a_qt_act, i + 1)
                    for hh in range(HA):
                        last = pe.transpose(ps[3][:, hh // 4, (hh % 4) * P:(hh % 4 + 1) * P].bitcast(F32R),
                                            qa_st[:, hh, n:n + 2, :].rearrange("p a d -> p (a d)"), ident_r[:, :])
                    last.then_inc(a_qset, 1)

            def scores_a(i, hh, k0, nk, wait):
                if wait:
                    pe.wait_ge(a_max, HA * i + hh - 1)
                elif hh == 0:
                    pe.wait_ge(a_qt_dve, i + 1)
                keys = kta[:, hh // 4, bass.ds(k0 * P, nk * P)]
                pe.matmul(ps[0][:, hh % 2, 0:nk * P], qa1[:, hh, :], keys, start=True, stop=False)
                pe.matmul(ps[0][:, hh % 2, 0:nk * P], qa2[:, hh, :], keys, start=False, stop=True
                          ).then_inc(a_qk, 1)

            def turn_a(i, hh, nk):
                pe.wait_ge(a_exp, HA * i + hh + 1)
                if hh >= 2:
                    pe.wait_ge(a_lo, HA * i + hh - 1)
                for k in range(nk):
                    last = pe.transpose(ps[1][:, hh % 2, k * P:(k + 1) * P], prob_a[:, hh % 4, k * P:(k + 1) * P],
                                        ident)
                last.then_inc(a_turn, 1)

            def pv_a(i, g, nk, first):
                pe.wait_ge(a_lo, HA * i + 4 * g + 4)
                pe.wait_ge(a_vst, 4 * i + 4)
                if not (first and g == 0):
                    pe.wait_ge(a_ot, 2 * i + g)
                for k in range(nk):
                    v = va_st[:, k, g, :, :].rearrange("p a d -> p (a d)")
                    pe.matmul(ps[2][:, 0, :], v, pt_hi[:, g, k, :], start=(k == 0), stop=False)
                    last = pe.matmul(ps[2][:, 0, :], v, pt_lo[:, g, k, :], start=False, stop=(k == nk - 1))
                last.then_inc(a_pv, 1)

            def back_a(i, first):
                for g in range(GA):
                    pe.wait_ge(a_ot, 2 * i + g + 1)
                    for n in range(4):
                        last = pe.matmul(ps[2][:, 1, (4 * g + n) * HD:(4 * g + n + 1) * HD],
                                         o_ta[:, g, n * P:(n + 1) * P], const("halves"), start=True, stop=True)
                    last.then_inc(a_back, 1)

            def tile_a(i, k0, nk, nk1, first, last):
                for hh in range(HA):
                    if hh + 2 < HA:
                        scores_a(i, hh + 2, k0, nk, True)
                    turn_a(i, hh, nk)
                    if hh == 2 and not first:
                        back_a(i - 1, first)
                    if hh == 5:
                        pv_a(i, 0, nk, first)
                if not last:
                    q_sets(i + 1)
                    k1 = 0 if first else k0 + 1
                    pe.wait_ge(a_max, HA * i + HA)
                    scores_a(i + 1, 0, k1, nk1, False)
                    scores_a(i + 1, 1, k1, nk1, False)
                pv_a(i, 1, nk, first)
                if last:
                    back_a(i, first)

            q_sets(0)
            pe.wait_ge(a_kt_act, 1)
            pe.wait_ge(a_kt_dve, 1)
            scores_a(0, 0, 0, 2, False)
            scores_a(0, 1, 0, 2, False)
            tile_a(0, 0, 2, 3, True, False)
            with pe.Fori(1, NT - 2) as i:
                tile_a(i, i - 1, 3, 3, False, False)
            tile_a(NT - 2, NT - 3, 3, 2, False, False)
            tile_a(NT - 1, NT - 2, 2, 0, False, True)

            for half in range(2):
                last = pe.matmul(ps[3][:, half, :], const("ones"), gate_row[:, half * 512:(half + 1) * 512],
                                 start=True, stop=True)
            last.then_inc(gate_mm, 1)

            def turn_y(t):
                pe.wait_ge(c_cat, 2 * t + 2)
                if t >= 1:
                    pe.wait_ge(c_lo, t)
                for k in range(NK):
                    last = pe.transpose(ps[2][:, k // 4, (k % 4) * P:(k % 4 + 1) * P],
                                        y_cat[:, t % 2, k * P:(k + 1) * P], ident)
                last.then_inc(c_turn, 1)

            pe.wait_ge(wo_split, 2 * NK)
            pe.wait_ge(a_y, NT)
            turn_y(0)
            for t in range(NT):
                pe.wait_ge(c_lo, t + 1)
                if t >= 2:
                    pe.wait_ge(c_scaled, t - 1)
                for half in range(2):
                    o = ps[t % 2][:, half, :]
                    w = slice(half * 512, (half + 1) * 512)
                    for k in range(NK):
                        pe.matmul(o, yt_hi[:, t % 2, k, :], wo_hi[:, k, w], start=(k == 0), stop=False)
                        pe.matmul(o, yt_hi[:, t % 2, k, :], wo_lo[:, k, w], start=False, stop=False)
                        last = pe.matmul(o, yt_lo[:, t % 2, k, :], wo_hi[:, k, w], start=False, stop=(k == NK - 1))
                    if half == 0 and t + 1 < NT:
                        turn_y(t + 1)
                last.then_inc(c_mm, 1)
    return nc


def constants():
    c = np.zeros((P, N_CONSTS), np.float32)

    def put(name, value):
        c[:, CONSTS[name][0]:CONSTS[name][1]] = value

    put("identity", np.eye(P))
    put("halves", np.concatenate([np.eye(HD)] * 2))
    put("ones", 1.0)
    q, k = np.arange(P)[:, None], np.arange(P)[None, :]
    band = np.zeros((P, 3 * P), np.float32)
    band[:, 0:P][k < q] = MASKED
    band[:, 2 * P:][k > q] = MASKED
    put("band", band)
    put("inv_freq", np.float32(1.0) / np.float32(ROPE_THETA) ** (np.arange(0, HD, 2, dtype=np.float32) / np.float32(HD)))
    scale = np.repeat(np.float32([HD ** -0.5, 1.0, HD ** -0.5, 1.0]), HD)
    put("gain_scale", scale)
    sign = np.tile(np.repeat(np.float32([-1.0, 1.0]), HD // 2), 4)
    put("swap_scale", scale * sign)
    return c


def kernel(x, c, positions, w_ada, b_ada, norm_gain, w_in, q_norm_a, k_norm_a, sink_a, q_norm_b, k_norm_b,
           lambda_q1, lambda_k1, lambda_q2, lambda_k2, subln_gain, w_out):
    import concourse.bacc as bacc
    from concourse.bass_utils import run_bass_kernel_spmd

    def a(v):
        return np.ascontiguousarray(np.asarray(v))

    gains = [a(v)[0] for v in (q_norm_b, k_norm_b, q_norm_a, k_norm_a)]
    swapped = [np.concatenate([g[HD // 2:], g[:HD // 2]]) for g in gains]
    b = a(b_ada)[0]

    def rows(v):
        return np.broadcast_to(v.reshape(1, -1), (P, v.size))

    def cols(v):
        return v.reshape(NK, P).T

    params = np.concatenate([
        rows(np.concatenate(gains)), rows(np.concatenate(swapped)), rows(a(sink_a)[0]), rows(a(subln_gain)[0]),
        rows(np.concatenate([a(v)[0] for v in (lambda_q1, lambda_k1, lambda_q2, lambda_k2)])),
        cols(a(c)[0]), cols(b[0:D]), cols(b[D:2 * D]), cols(a(norm_gain)[0])], axis=1)
    w = a(w_in)[0]
    starts = (1280, 1792, 2304, 768, 2816, 0)
    chunks = np.stack([w[:, s:s + CW] for s in starts]).reshape(NFULL * NK, P, CW)
    arrays = {
        "x": a(x)[0], "w_ada": a(w_ada)[0], "w_in": a(chunks), "w_kv": a(w[:, 512:768].reshape(NK, P, 4 * HD)),
        "w_out": a(w_out)[0], "params": a(params), "positions": a(a(positions)[0].reshape(NT, P).T),
        "b_gate": a(b[2 * D:].reshape(1, D)), "consts": constants(),
    }
    nc = bacc.Bacc("TRN2", target_bir_lowering=False, num_devices=1)
    args = [nc.dram_tensor(f"in_{n}", v.shape, mybir.dt.from_np(v.dtype), kind="ExternalInput").ap()
            for n, v in arrays.items()]
    out = nc.dram_tensor("out", (S, D), F32, kind="ExternalOutput").ap()
    hymba_kernel(nc, *args, out)
    r = run_bass_kernel_spmd(nc, [{f"in_{n}": v for n, v in arrays.items()}], core_ids=[0])
    return r.results[0]["out"].reshape(1, S, D)
```

```python
import numpy as np
from contextlib import ExitStack

import concourse.bass as bass
from concourse import mybir

F32 = mybir.dt.float32
F32R = mybir.dt.float32r
I32 = mybir.dt.int32
ACT = mybir.ActivationFunctionType
ALU = mybir.AluOpType
AXX = mybir.AxisListType.X

P = 128
S = 1024
D = 1024
HD = 64
NT = S // P
NK = D // P
CW = 512
HB = 4
HA = 8
GA = 2
NFULL = 6
NPROJ = (NFULL + 1) * NT
EPS = 1e-6
LAMBDA_INIT = 0.2
ROPE_THETA = 10000.0
MAGIC = 1.5 * 2.0 ** 23
PI_IN = 3.1415925
MASKED = -2.0 ** 100


def columns(parts):
    at, out = 0, {}
    for name, n in parts:
        out[name] = (at, at + n)
        at += n
    return out, at


PARAMS, N_PARAMS = columns((("gain", 4 * HD), ("gain_swapped", 4 * HD), ("sink", HA), ("subln", 2 * HD),
                            ("lambdas", 4 * HD), ("c", NK), ("b_shift", NK), ("b_scale", NK),
                            ("norm_gain", NK)))
CONSTS, N_CONSTS = columns((("identity", P), ("halves", HD), ("ones", P), ("band", 3 * P), ("inv_freq", HD // 2),
                            ("gain_scale", 4 * HD), ("swap_scale", 4 * HD)))


def two_pi_parts():
    rest, parts = 2 * np.pi, []
    for _ in range(3):
        step = 2.0 ** (np.floor(np.log2(rest)) - 8)
        parts.append(float(np.floor(rest / step) * step))
        rest -= parts[-1]
    return parts + [float(np.float32(rest))]


def hymba_kernel(nc, x, w_ada, w_in, w_kv, w_out, params, positions, b_gate, consts, out):
    gates_dram = nc.dram_tensor("gates_dram", [S, D], F32, kind="Internal").ap()
    mem = ExitStack()

    def sb(name, shape, dt=F32):
        return mem.enter_context(nc.sbuf_tensor(name, shape, dt))

    def sem(name):
        return mem.enter_context(nc.semaphore(name))

    def phase_tensors(makers):
        with ExitStack() as scope:
            return [scope.enter_context(nc.sbuf_tensor(n, s, d)) for n, s, d in makers]

    with mem:
        cst = sb("cst", [P, N_CONSTS])
        par = sb("par", [P, N_PARAMS])
        ident_r = sb("ident_r", [P, P], F32R)
        gate_row = sb("gate_row", [P, D])
        small = sb("small", [P, 128])
        y_stat = sb("y_stat", [P, 4, NT, HB])
        kv_a = sb("kv_a", [P, NT, 4 * HD])
        q_a = sb("q_a", [P, NT, HA * HD])

        def const(name):
            return cst[:, CONSTS[name][0]:CONSTS[name][1]]

        def param(name):
            return par[:, PARAMS[name][0]:PARAMS[name][1]]

        first = [("qk_b", [P, 2, NT, CW], F32), ("v_b", [P, NT, CW], F32)]
        (qk_b, v_b, h_hi, h_lo, w_hi, w_lo, w_raw, sq, rot, cos_sin, tab, stat) = phase_tensors(first + [
            ("h_hi", [P, NK, S], F32R), ("h_lo", [P, NK, S], F32R),
            ("w_hi", [P, NK, CW], F32R), ("w_lo", [P, NK, CW], F32R),
            ("w_raw", [P, 4, CW], F32), ("sq", [P, 2, CW], F32), ("rot", [P, 2, CW], F32),
            ("cos_sin", [P, 2, NT, HD // 2], F32), ("tab", [P, 2, NT, HD], F32),
            ("stat", [P, 4, NT, HA], F32)])
        _, mod_acc, x_in, x_sq = phase_tensors([("hold_qkv", [P, 3, NT, CW], F32), ("mod_acc", [P, 2 * D], F32),
                                                ("x_in", [P, 4, D], F32), ("x_sq", [P, D], F32)])
        (_, y_b, o_tb, prob, q1t, q2t, kt, q_st, k_st, v_hi, v_lo, at_hi, at_lo, bst) = phase_tensors([
            ("hold_qkv2", [P, 3, NT, CW], F32),
            ("y_b", [P, NT, CW], F32), ("o_tb", [P, 2, 2 * P], F32), ("prob", [P, 2, 2, S], F32),
            ("q1t", [P, 2, S], F32R), ("q2t", [P, 2, S], F32R), ("kt", [P, 2, S], F32R),
            ("q_st", [P, NT, 2, 3, HD], F32R), ("k_st", [P, NT, 2, 2, HD], F32R),
            ("v_hi", [P, NT, P], F32R), ("v_lo", [P, NT, P], F32R),
            ("at_hi", [P, NT, 2, 2 * P], F32R), ("at_lo", [P, NT, 2, 2 * P], F32R),
            ("bst", [P, 8, NT], F32)])
        lower = [("wo_hi", [P, NK, D], F32R), ("before_raw", [P, 2, D], F32), ("wo_raw", [P, 2, D], F32),
                 ("hold_yb", [P, NT, CW], F32), ("wo_lo", [P, NK, D], F32R)]
        _, ka_st = phase_tensors([("wo_hi_", [P, NK, D], F32R), ("ka_st", [P, NT, GA, 3, HD], F32R)])
        (wo_hi, _, wo_raw, _, wo_lo, kta, qa_st, mask, qa_even, prob_a, va_st, o_ta, qa_odd, pt_hi, pt_lo,
         ast) = phase_tensors(lower + [
            ("kta", [P, GA, 2, S], F32R),
            ("qa_st", [P, HA, 2, HD], F32R), ("mask", [P, 3 * P], F32R), ("qa_even", [P, HA, P], F32R),
            ("prob_a", [P, 4, 3 * P], F32), ("va_st", [P, 3, GA, 2, HD], F32R),
            ("o_ta", [P, 2, GA, 4 * P], F32), ("qa_odd", [P, HA, P], F32R),
            ("pt_hi", [P, GA, 3, 4 * P], F32R), ("pt_lo", [P, GA, 3, 4 * P], F32R),
            ("ast", [P, 2, 8, HA], F32)])
        qa_t = (qa_even, qa_odd)
        (_, gates, _, _, _, yt_hi, yt_lo, y_cat, _, x_res, o_out) = phase_tensors([
            ("hold_wo_hi", [P, NK, D], F32), ("gates", [P, 2, D], F32), ("hold_raw", [P, 2, D], F32),
            ("hold_yb3", [P, NT, CW], F32), ("hold_wo_lo", [P, NK, D], F32),
            ("yt_hi", [P, 2, NK, P], F32R), ("yt_lo", [P, 2, NK, P], F32R), ("y_cat", [P, 2, D], F32),
            ("hold_late", [P, 33 * P], F32), ("x_res", [P, 2, D], F32), ("o_out", [P, 2, D], F32)])
        y_sq = kv_a[:, :, 0:2 * HD].rearrange("p (s h) d -> p s h d", s=2)

        ps = [mem.enter_context(nc.psum_tensor(f"ps{i}", [P, 2, 512], F32)) for i in range(4)]
        acc = [ps[i // 2][:, i % 2, :] for i in range(4)]

        silu_c, scale_a, shift_b = small[:, 0:8], small[:, 8:16], small[:, 16:24]
        x_ssq, x_ms, x_std, x_rstd = (small[:, 24 + 8 * i:32 + 8 * i] for i in range(4))
        ones, neg_lam = small[:, 56:57], small[:, 57:58]
        lam_sum, lam_exp = small[:, 58:60], small[:, 60:62]
        pos_f = small[:, 72:80]
        neg_sink = small[:, 88:96]
        pos_i = small[:, 64:72].bitcast(I32)

        ada = qk_b[:, :, :, :].rearrange("p a t c -> p (a t c)").rearrange("p (s n) -> p s n", s=4)
        x_t = [v_b[:, :, :].rearrange("p t c -> p (t c)").rearrange("p (k s) -> p k s", k=NK // 2),
               q_a[:, :, :].rearrange("p t c -> p (t c)").rearrange("p (k s) -> p k s", k=NK // 2)]
        gate_in = [place[:, :, :].rearrange("p t c -> p (t c)").rearrange("p (s n) -> p s n", s=4)[:, i, :]
                   for place in (v_b, q_a) for i in range(4)]
        ang = sq[:, :, :].rearrange("p a c -> p (a c)")[:, 0:NT * HD // 2]
        ang_n, ang_r = (rot[:, i, 0:NT * HD // 2] for i in range(2))
        ang_c = sq[:, 1, 0:NT * HD // 2]

        load = sem("load")
        ada_in = [sem(f"ada_in{i}") for i in range(4)]
        ada_sum = sem("ada_sum")
        x_loaded = [sem(f"x_loaded{i}") for i in range(4)]
        x_squared, x_mean, x_root = sem("x_squared"), sem("x_mean"), sem("x_root")
        x_recip, x_normed, x_turned, x_kept = sem("x_recip"), sem("x_normed"), sem("x_turned"), sem("x_kept")
        setup_dve, setup_act, trig_step = sem("setup_dve"), sem("setup_act"), sem("trig_step")
        mod_cols, mod_done = sem("mod_cols"), sem("mod_done")
        h_affine, h_split, h_ready, h_low = sem("h_affine"), sem("h_split"), sem("h_ready"), sem("h_low")
        w_loaded = [sem(f"w_loaded{i}") for i in range(4)]
        w_hi_done, w_ready, w_slot_free = sem("w_hi_done"), sem("w_ready"), sem("w_slot_free")
        proj_done = sem("proj_done")
        bank_free = [sem(f"bank_free{i}") for i in range(4)]
        squared, ssq_done, std_done, rstd_done = sem("squared"), sem("ssq_done"), sem("std_done"), sem("rstd_done")
        table_done, rot_step, rope_done = sem("table_done"), sem("rot_step"), sem("rope_done")
        gate_stored = [sem(f"gate_stored{i}") for i in range(2)]
        gate_loaded = [sem(f"gate_loaded{i}") for i in range(NK)]
        gate_zero, gate_bias, gate_sum, gate_mm = sem("gate_zero"), sem("gate_bias"), sem("gate_sum"), sem("gate_mm")
        b_stage, b_v, b_v_free = sem("b_stage"), sem("b_v"), sem("b_v_free")
        b_first_hi, b_first_lo, b_scaled = sem("b_first_hi"), sem("b_first_lo"), sem("b_scaled")
        b_set, b_set_act, b_set_dve = sem("b_set"), sem("b_set_act"), sem("b_set_dve")
        b_qk, b_max, b_exp = sem("b_qk"), sem("b_max"), sem("b_exp")
        b_small, b_turn, b_hi, b_lo = sem("b_small"), sem("b_turn"), sem("b_hi"), sem("b_lo")
        b_attn = sem("b_attn")
        b_pv, b_ot, b_back, b_y = sem("b_pv"), sem("b_ot"), sem("b_back"), sem("b_y")
        a_kst, a_kset, a_kt_act, a_kt_dve = sem("a_kst"), sem("a_kset"), sem("a_kt_act"), sem("a_kt_dve")
        a_qst, a_vst, a_qset, a_qt_act, a_qt_dve = (sem("a_qst"), sem("a_vst"), sem("a_qset"),
                                                    sem("a_qt_act"), sem("a_qt_dve"))
        a_qk, a_max, a_neg, a_exp, a_turn, a_hi, a_lo = (sem("a_qk"), sem("a_max"), sem("a_neg"), sem("a_exp"),
                                                         sem("a_turn"), sem("a_hi"), sem("a_lo"))
        a_pv, a_ot, a_back, a_y = sem("a_pv"), sem("a_ot"), sem("a_back"), sem("a_y")
        a_mask = sem("a_mask")
        a_sink, a_sink_exp, a_den = sem("a_sink"), sem("a_sink_exp"), sem("a_den")
        wo_in = [sem(f"wo_in{i}") for i in range(2)]
        wo_split = sem("wo_split")
        gates_in = [sem(f"gates_in{i}") for i in range(2)]
        x_in_again = [sem(f"x_in_again{i}") for i in range(2)]
        c_mean = sem("c_mean")
        c_sq, c_ssq, c_std, c_rstd, c_norm, c_gain, c_cat = (sem("c_sq"), sem("c_ssq"), sem("c_std"), sem("c_rstd"),
                                                             sem("c_norm"), sem("c_gain"), sem("c_cat"))
        c_turn, c_hi, c_lo, c_mm, c_scaled, c_out = (sem("c_turn"), sem("c_hi"), sem("c_lo"), sem("c_mm"),
                                                     sem("c_scaled"), sem("c_out"))
        carrier = sem("wait_carrier")
        stored = [sem(f"stored{i}") for i in range(2)]

        groups = ((0, 1), (1, 2), (2, 4), (4, 8))
        ROPE0 = 2
        BANK0 = 1
        Y0 = 1

        def heads(ap, n):
            return ap.rearrange("p (h d) -> p h d", h=n)

        def wait_apart(engine, semaphore, value):
            engine.wait_ge(semaphore, value)
            if not isinstance(value, int):
                engine.sem_inc(carrier, 1)

        STEP0 = 6

        def steps(engine, step, phase_3):
            for s in range(STEP0):
                step(0, s, True)
            with engine.Fori(0, HB - 1) as h:
                for s in range(STEP0, STEP0 + NT):
                    step(h, s, True)
            for s in range(STEP0, STEP0 + NT):
                step(HB - 1, s, s < NT)
                if s in phase_3:
                    phase_3[s]()

        def tile_steps(engine, step, phase_3b):
            def both(i0):
                for parity in range(2):
                    for s in range(4):
                        step(i0 + parity, parity, s)

            both(0)
            with engine.Fori(1, NT // 2 - 1) as half:
                both(half * 2)
            both(NT - 2)
            for s in range(4):
                step(NT, 0, s)
            phase_3b()
            for s in range(2):
                step(NT + 1, 1, s)

        def token_steps(engine, step):
            def both(pair):
                for parity in range(2):
                    step(pair, parity)

            both(0)
            with engine.Fori(1, NT // 2 - 1) as pair:
                both(pair)
            both(NT // 2 - 1)

        def exists(i):
            return not isinstance(i, int) or 0 <= i < NT

        def n_keys(i):
            return 2 if isinstance(i, int) and i in (0, NT - 1) else 3

        def pair_before(i, s):
            return (i, s - 1) if s else (i - 1, 3)

        def head_q(h):
            return qk_b[:, 0, :, bass.ds(h * P, P)].rearrange("p t (c d) -> p t c d", c=2)

        def head_k(h):
            return qk_b[:, 1, :, bass.ds(h * P, P)].rearrange("p t (c d) -> p t c d", c=2)

        block = mem.enter_context(nc.Block())

        @block.sync
        def _(sp):
            sp.dma_start(par[:, :], params).then_inc(load, 16)
            sp.dma_start(cst[:, :], consts).then_inc(load, 16)
            sp.dma_start(pos_i, positions).then_inc(load, 16)
            sp.wait_ge(gate_zero, 1)
            sp.dma_start(gate_row[0:1, :], b_gate).then_inc(gate_bias, 16)
            for k in range(NK):
                for a in range(2 * k, min(2 * k + 2, NK)):
                    if a >= 4:
                        sp.wait_ge(ada_sum, a - 3)
                    sp.dma_start(ada[:, a % 4, :], w_ada[a * P:(a + 1) * P, 0:2 * D]).then_inc(ada_in[a % 4], 16)
                    if a == 2 * k:
                        sp.dma_start(x_in[:, k % 4, :], x[k * P:(k + 1) * P, :]).then_inc(x_loaded[k % 4], 16)
                if k >= 4:
                    sp.wait_ge(x_turned, k - 3)
                    sp.dma_start(x_in[:, k % 4, :], x[k * P:(k + 1) * P, :]).then_inc(x_loaded[k % 4], 16)
                    sp.dma_start(w_raw[:, k - 4, :], w_in[k - 4, :, :]).then_inc(w_loaded[k - 4], 16)
            def w_load(ci):
                for k in range(4, 4 + NK):
                    sp.wait_ge(w_ready, ci * NK + k - 3)
                    sp.dma_start(w_raw[:, k % 4:k % 4 + 1, :],
                                 w_in[bass.ds(ci * NK + k, 1), :, :].rearrange("o p n -> p o n")
                                 ).then_inc(w_loaded[k % 4], 16)

            w_load(0)
            sp.wait_ge(h_ready, len(groups))
            sp.wait_ge(h_low, len(groups) - 2)
            for k in range(NK):
                sp.dma_start(gate_in[k], w_ada[k * P:(k + 1) * P, 2 * D:3 * D]).then_inc(gate_loaded[k], 16)
            with sp.Fori(1, NFULL - 1) as ci:
                w_load(ci)
            for k in range(4, NK):
                sp.wait_ge(w_ready, (NFULL - 1) * NK + k - 3)
                sp.dma_start(w_raw[:, k % 4, :], w_in[(NFULL - 1) * NK + k, :, :]).then_inc(w_loaded[k % 4], 16)
            for k in range(NK):
                sp.wait_ge(w_ready, NFULL * NK + k - 3)
                sp.dma_start(w_raw[:, k % 4, 0:4 * HD], w_kv[k, :, :]).then_inc(w_loaded[k % 4], 16)
            sp.wait_ge(a_kset, 2 * GA)
            for k in range(NK):
                if k >= 2:
                    sp.wait_ge(wo_split, 2 * (k - 1))
                sp.dma_start(wo_raw[:, k % 2, :], w_out[k * P:(k + 1) * P, :]).then_inc(wo_in[k % 2], 16)
            def gates_load(t, parity):
                sp.dma_start(gates[:, parity, :], gates_dram[bass.ds(t * P, P), :]).then_inc(gates_in[parity], 16)

            def x_load(t, parity):
                sp.dma_start(x_res[:, parity, :], x[bass.ds(t * P, P), :]).then_inc(x_in_again[parity], 16)

            for b in range(2):
                sp.wait_ge(gate_stored[b], 16 * (1 + NT))
            for t in range(2):
                gates_load(t, t)
            sp.wait_ge(a_back, NT)
            for t in range(2):
                x_load(t, t)

            def token(pair, parity):
                t = 2 * pair + parity
                if exists(t + 2):
                    sp.wait_ge(c_cat, 2 * t + 2)
                    gates_load(t + 2, parity)
                sp.wait_ge(c_out, 2 * t + 2)
                sp.dma_start(out[bass.ds(t * P, P), :], o_out[:, parity, :]).then_inc(stored[parity], 16)
                if exists(t + 2):
                    x_load(t + 2, parity)

            token_steps(sp, token)
            for b in range(2):
                sp.wait_ge(stored[b], 16 * NT // 2)

        @block.gpsimd
        def _(pool):
            def rope(place, n_heads, t, m):
                n = n_heads * HD
                v = place.rearrange("p (h e d) -> p h e d", h=n_heads, e=2)
                c = tab[:, 0, t, :].unsqueeze(1).broadcast_to([P, n_heads, HD])
                s = tab[:, 1, t, :].rearrange("p (e d) -> p e d", e=2)
                r = rot[:, t % 2, 0:n].rearrange("p (h e d) -> p h e d", h=n_heads, e=2)
                pool.tensor_tensor(heads(sq[:, t % 2, 0:n], n_heads), heads(place, n_heads), c, ALU.mult
                                   ).then_inc(rot_step, 1)
                for e in range(2):
                    pool.tensor_tensor(r[:, :, e, :], v[:, :, 1 - e, :],
                                       s[:, e, :].unsqueeze(1).broadcast_to([P, n_heads, HD // 2]), ALU.mult
                                       ).then_inc(rot_step, 1)
                wait_apart(pool, rot_step, 3 * m + 3)
                pool.tensor_tensor(place, sq[:, t % 2, 0:n], rot[:, t % 2, 0:n], ALU.add).then_inc(rope_done, 1)

            def tables(g, m0):
                wait_apart(pool, rope_done, ROPE0 + m0)
                gain = heads(param("gain"), 4)[:, bass.ds(g, 1), :].rearrange("p o (e d) -> p o e d", e=2)
                swap = heads(param("gain_swapped"), 4)[:, bass.ds(g, 1), :].rearrange("p o (e d) -> p o e d", e=2)
                for i, w in enumerate((gain, swap)):
                    for e in range(2):
                        dst = tab[:, i, :, :].rearrange("p t (e d) -> p t e d", e=2)[:, :, e, :]
                        pool.tensor_tensor(dst, cos_sin[:, i, :, :],
                                           w[:, :, e, :].broadcast_to([P, NT, HD // 2]),
                                           ALU.mult).then_inc(table_done, 1)

            def norm_chunk(ci, g, place, n_heads):
                tables(g, g * NT)
                wait_apart(pool, table_done, 4 * g + 4)
                for t in range(NT):
                    wait_apart(pool, bank_free[t % 4], 2 * ci + t // 4 + 1 + BANK0)
                    rope(place(t), n_heads, t, g * NT + t)

            for b in range(4):
                pool.sem_inc(bank_free[b], BANK0)
            for b in range(2):
                pool.sem_inc(gate_stored[b], 16)
            pool.sem_inc(rope_done, ROPE0)
            pool.sem_inc(b_y, Y0)
            for n in range(2, len(groups)):
                a, b = groups[n]
                pool.wait_ge(h_split, 2 * n + 2)
                pool.tensor_tensor(h_lo[:, 4:8, a * P:b * P], x_t[1][:, :, a * P:b * P],
                                   h_hi[:, 4:8, a * P:b * P].bitcast(F32), ALU.subtract).then_inc(h_low, 1)
            pool.wait_ge(setup_act, 3)
            pool.wait_ge(setup_dve, 3)
            with pool.Fori(0, 2) as ci:
                norm_chunk(ci, ci, lambda t: qk_b[:, bass.ds(ci, 1), t, :].rearrange("p o c -> p (o c)"), 8)
            norm_chunk(5, 2, lambda t: q_a[:, t, :], HA)
            norm_chunk(6, 3, lambda t: kv_a[:, t, 0:2 * HD], GA)

            wait_apart(pool, rope_done, ROPE0 + 4 * NT)
            for b in range(4):
                pool.wait_ge(bank_free[b], 2 * (NFULL + 1) + BANK0)
            for b in range(2):
                pool.wait_ge(gate_stored[b], 16 * (1 + NT))

            def hi(dst, src, done):
                one = ones
                while len(one.shape) < len(src.shape):
                    one = one.unsqueeze(1)
                pool.tensor_tensor(dst, src, one.broadcast_to(list(src.shape)), ALU.mult).then_inc(done, 1)

            def lo(dst, src, high, done):
                pool.tensor_tensor(dst, src, high.bitcast(F32), ALU.subtract).then_inc(done, 1)

            def stage_high(h, c):
                if c == 0:
                    wait_apart(pool, b_set, 6 * h)
                hi(q_st[:, :, c, 0, :], head_q(h)[:, :, c, :], b_stage)
                hi(q_st[:, :, c, 2, :], head_q(h)[:, :, c, :], b_stage)
                hi(k_st[:, :, c, 0, :], head_k(h)[:, :, c, :], b_stage)

            def stage_low(h, c):
                wait_apart(pool, b_stage, 10 * h - 10 + 5 * c + 3)
                lo(q_st[:, :, c, 1, :], head_q(h)[:, :, c, :], q_st[:, :, c, 0, :], b_stage)
                lo(k_st[:, :, c, 1, :], head_k(h)[:, :, c, :], k_st[:, :, c, 0, :], b_stage)

            def stage_v(h, half):
                r = slice(4 * half, 4 * half + 4)
                v = v_b[:, r, bass.ds(h * P, P)]
                hi(v_hi[:, r, :], v, b_v)
                wait_apart(pool, b_v, 4 * h + 2 * half + 1)
                lo(v_lo[:, r, :], v, v_hi[:, r, :], b_v)

            def combine(h, s):
                wait_apart(pool, b_scaled, NT * h + s + 1)
                pool.tensor_tensor(prob[:, s % 2, 0, :], prob[:, s % 2, 0, :], prob[:, s % 2, 1, :], ALU.add
                                   ).then_inc(b_attn, 1)

            keys_of_a = kv_a[:, :, 0:2 * HD].rearrange("p t (g d) -> p t g d", g=GA)

            def between(h, more):
                for s in range(STEP0, STEP0 + NT):
                    combine(h, s)
                    if s == 10:
                        wait_apart(pool, b_v_free, h + 1)
                        stage_v(h + 1, 0)
                    if s == 11:
                        wait_apart(pool, b_pv, 4 * h + 4)
                        stage_v(h + 1, 1)
                    if more and s in (8, 12):
                        stage_high(h + 2, s // 4 - 2)
                    if more and s in (9, 13):
                        stage_low(h + 2, s // 4 - 2)
                    if not more and s in (12, 13):
                        pool.wait_ge(b_v, 4 * HB)
                        hi(ka_st[:, :, :, 2 * (s - 12), :], keys_of_a, a_kst)

            stage_v(0, 0)
            stage_v(0, 1)
            for s in range(STEP0):
                combine(0, s)
                if s in (0, 2):
                    stage_high(1, s // 2)
                if s in (1, 3):
                    stage_low(1, s // 2)
            with pool.Fori(0, HB - 2) as h:
                between(h, True)
            between(HB - 2, False)
            for s in range(STEP0, NT):
                combine(HB - 1, s)
                if s == STEP0:
                    pool.wait_ge(a_kst, 1)
                    lo(ka_st[:, :, :, 1, :], keys_of_a, ka_st[:, :, :, 0, :], a_kst)

            def stage_qa(i):
                if i >= 1:
                    pool.wait_ge(a_qset, 2 * i)
                else:
                    pool.wait_ge(b_set, 6 * HB)
                q = heads(q_a[:, i, :], HA)
                hi(qa_st[:, :, 0, :], q, a_qst)
                pool.wait_ge(a_qst, 2 * i + 1)
                lo(qa_st[:, :, 1, :], q, qa_st[:, :, 0, :], a_qst)

            def stage_va(i, g):
                if i >= 1:
                    pool.wait_ge(a_pv, 2 * i - 1 + g)
                k0 = max(i - 1, 0)
                v = kv_a[:, k0:k0 + n_keys(i), 2 * HD + g * HD:2 * HD + (g + 1) * HD]
                hi(va_st[:, 0:n_keys(i), g, 0, :], v, a_vst)
                pool.wait_ge(a_vst, 4 * i + 2 * g + 1)
                lo(va_st[:, 0:n_keys(i), g, 1, :], v, va_st[:, 0:n_keys(i), g, 0, :], a_vst)

            def split_wo(k):
                pool.wait_ge(wo_in[k % 2], 16 * (k // 2 + 1))
                hi(wo_hi[:, k, :], wo_raw[:, k % 2, :], wo_split)
                pool.wait_ge(wo_split, 2 * k + 1)
                lo(wo_lo[:, k, :], wo_raw[:, k % 2, :], wo_hi[:, k, :], wo_split)

            stage_qa(0)
            pool.tensor_tensor(mask[:, :], const("band"), ones.broadcast_to([P, 3 * P]), ALU.mult).then_inc(a_mask, 1)
            stage_qa(1)
            pool.wait_ge(b_pv, 4 * HB)
            stage_va(0, 0)
            stage_va(0, 1)

            def squares(t):
                if t >= 2:
                    pool.wait_ge(c_ssq, t - 1)
                yb = heads(y_b[:, t, :], HB)
                pool.tensor_tensor(y_sq[:, t % 2, :, :], yb, yb, ALU.mult).then_inc(c_sq, 1)

            pool.wait_ge(b_lo, HB * NT)
            pool.wait_ge(b_back, HB * 4)
            pool.wait_ge(b_y, HB * 4 + Y0)
            split_wo(0)
            for i in range(1, NT):
                if i + 1 < NT:
                    stage_qa(i + 1)
                stage_va(i, 0)
                stage_va(i, 1)
                squares(i - 1)
                split_wo(i)

            def gain(t):
                wait_apart(pool, c_norm, t + 1)
                yb = y_b[:, bass.ds(t, 1), :].rearrange("p o (h d) -> p (o h) d", h=HB)
                pool.tensor_tensor(yb, yb, param("subln").unsqueeze(1).broadcast_to([P, HB, 2 * HD]), ALU.mult
                                   ).then_inc(c_gain, 1)

            def gated(t, pair, parity):
                wait_apart(pool, gates_in[parity], 16 * pair + 16)
                if exists(t - 2):
                    wait_apart(pool, c_turn, t - 1)
                pool.tensor_tensor(y_cat[:, parity, 0:CW], q_a[:, bass.ds(t, 1), :].rearrange("p o c -> p (o c)"),
                                   gates[:, parity, 0:CW], ALU.mult).then_inc(c_cat, 1)
                wait_apart(pool, c_gain, t + 1)
                pool.tensor_tensor(y_cat[:, parity, CW:D], y_b[:, bass.ds(t, 1), :].rearrange("p o c -> p (o c)"),
                                   gates[:, parity, CW:D], ALU.mult).then_inc(c_cat, 1)

            def token(pair, parity):
                t = 2 * pair + parity
                if exists(t + 2):
                    gain(t + 2)
                    gated(t + 2, pair + 1, parity)
                wait_apart(pool, x_in_again[parity], 16 * pair + 16)
                for half in range(2):
                    w = slice(half * 512, (half + 1) * 512)
                    wait_apart(pool, c_scaled, 2 * t + half + 1)
                    pool.tensor_tensor(o_out[:, parity, w], o_out[:, parity, w], x_res[:, parity, w], ALU.add
                                       ).then_inc(c_out, 1)

            gain(0)
            pool.wait_ge(a_qk, 4 * NT)
            gated(0, 0, 0)
            squares(NT - 1)
            gain(1)
            gated(1, 0, 1)
            token_steps(pool, token)

        @block.scalar
        def _(act):
            act.wait_ge(load, 48)
            act.activation(silu_c, param("c"), ACT.Silu).then_inc(setup_act, 1)

            def split_w(k):
                act.wait_ge(w_loaded[k % 4], 16 * (k // 4 + 1))
                act.activation(w_hi[:, k, :], w_raw[:, k % 4, :], ACT.Copy).then_inc(w_hi_done, 1)

            def square(k):
                act.wait_ge(x_loaded[k % 4], 16 * (k // 4 + 1))
                act.activation(x_sq[:, :], x_in[:, k % 4, :], ACT.Square, accum_out=x_ssq[:, k:k + 1]
                               ).then_inc(x_squared, 1)

            def keep(k):
                act.wait_ge(x_turned, k + 1)
                for half in range(2):
                    act.activation(x_t[half][:, :, k * P:(k + 1) * P], ps[2 + k % 2][:, half, :].rearrange(
                        "p (k s) -> p k s", k=4), ACT.Copy).then_inc(x_kept, 1)

            def affine(n):
                a, b = groups[n]
                for k in range(NK):
                    place = x_t[k // 4][:, k % 4, a * P:b * P]
                    act.activation(place, place, ACT.Identity, bias=shift_b[:, k:k + 1],
                                   scale=scale_a[:, k:k + 1]).then_inc(h_affine, 1)

            square(0)
            for k in range(NK):
                act.wait_ge(x_mean, k + 1)
                act.activation(x_std[:, k:k + 1], x_ms[:, k:k + 1], ACT.Sqrt).then_inc(x_root, 1)
                if k + 1 < NK:
                    square(k + 1)
                if k >= 4:
                    split_w(k - 4)
                if k >= 1:
                    keep(k - 1)
                if k == 7:
                    act.wait_ge(mod_done, 2)
                    act.wait_ge(x_kept, 2 * k)
                    affine(0)
            keep(NK - 1)
            for k in range(4, NK):
                split_w(k)
            act.wait_ge(x_kept, 2 * NK)
            for n in range(1, len(groups)):
                affine(n)
            act.wait_ge(setup_dve, 4)
            act.activation(cos_sin[:, 0, :, :].rearrange("p t d -> p (t d)"), ang_c, ACT.Sin).then_inc(setup_act, 1)
            act.activation(cos_sin[:, 1, :, :].rearrange("p t d -> p (t d)"), ang_r, ACT.Sin).then_inc(setup_act, 1)
            act.wait_ge(setup_act, 3)

            def refill(ci, n):
                for k in range(NK):
                    if k < NK - 1:
                        act.wait_ge(w_slot_free, (NK - 1) * ci + k + 1)
                    else:
                        act.wait_ge(proj_done, NT * ci + NT)
                    act.wait_ge(w_loaded[k % 4], 32 * ci + 16 * (k // 4) + 48)
                    act.activation(w_hi[:, k, 0:n], w_raw[:, k % 4, 0:n], ACT.Copy).then_inc(w_hi_done, 1)

            def norm_tile(ci, t, m, n):
                act.wait_ge(proj_done, NT * ci + t + 1)
                act.wait_ge(rope_done, m + t + 1)
                act.activation(sq[:, t % 2, 0:n], acc[t % 4][:, 0:n], ACT.Square).then_inc(squared, 1)
                act.wait_ge(ssq_done, 2 * (m + t) + 2)
                act.activation(stat[:, 2, t, 0:n // HD], stat[:, 1, t, 0:n // HD], ACT.Sqrt).then_inc(std_done, 1)

            def copy_tile(ci, t):
                act.wait_ge(proj_done, NT * ci + t + 1)
                act.activation(v_b[:, t, :], acc[t % 4], ACT.Copy).then_inc(bank_free[t % 4], 1)

            def gate_tile(ci, t):
                act.wait_ge(proj_done, NT * ci + t + 1)
                act.wait_ge(gate_stored[t % 2], (ci - 3) * (16 * NT // 2) + 16 * (t // 2) + 16)
                act.activation(sq[:, t % 2, :], acc[t % 4], ACT.Silu).then_inc(bank_free[t % 4], 1)
                act.wait_ge(bank_free[t % 4], 2 * ci + t // 4 + 1 + BANK0)
                act.dma_start(gates_dram[t * P:(t + 1) * P, bass.ds((ci - 3) * CW, CW)], sq[:, t % 2, :]
                              ).then_inc(gate_stored[t % 2], 16)

            with act.Fori(0, 2) as ci:
                for t in range(NT - 1):
                    norm_tile(ci, t, ci * NT, CW)
                refill(ci, CW)
                norm_tile(ci, NT - 1, ci * NT, CW)
            act.wait_ge(gate_sum, NK // 2)
            for t in range(NT - 1):
                copy_tile(2, t)
            refill(2, CW)
            copy_tile(2, NT - 1)
            act.wait_ge(rope_done, ROPE0 + 2 * NT)
            with act.Fori(3, 5) as ci:
                for t in range(NT - 1):
                    gate_tile(ci, t)
                refill(ci, CW)
                gate_tile(ci, NT - 1)
            for b in range(2):
                act.wait_ge(gate_stored[b], 16 * (1 + NT))
            for t in range(NT - 1):
                norm_tile(5, t, 2 * NT, CW)
            refill(5, 4 * HD)
            norm_tile(5, NT - 1, 2 * NT, CW)
            for t in range(NT):
                norm_tile(6, t, 3 * NT, 2 * HD)

            act.wait_ge(proj_done, NPROJ)
            for place, src in ((0, 0), (2, 0)):
                act.activation(q_st[:, :, :, place, :], head_q(0), ACT.Copy).then_inc(b_first_hi, 1)
                if place == 0:
                    act.activation(k_st[:, :, :, 0, :], head_k(0), ACT.Copy).then_inc(b_first_hi, 1)

            def set_copy(h, n):
                act.wait_ge(b_set, 6 * h + n + 1)
                act.activation((q1t, q2t, kt)[n % 3][:, n // 3, :],
                               ps[n % 2][:, :, :].rearrange("p a c -> p (a c)"), ACT.Copy).then_inc(b_set_act, 1)

            act.wait_ge(setup_dve, 6)
            act.activation(lam_exp, lam_sum, ACT.Exp).then_inc(setup_act, 1)
            for n in (0, 2, 4):
                set_copy(0, n)

            def o_copy(h, s, new):
                if s % 2 == 1 and s >= 5 and (new or s < NT + 5):
                    m = (s - 5) // 2
                    act.wait_ge(b_pv, 4 * h + m + 1)
                    act.activation(o_tb[:, m % 2, :], ps[3][:, 0, (m % 2) * 2 * P:(m % 2 + 1) * 2 * P], ACT.Copy
                                   ).then_inc(b_ot, 1)

            def step(h, s, new):
                g = NT * h + s
                if s >= 2 and (new or s < NT + 2):
                    act.wait_ge(b_turn, g - 1)
                    act.activation(at_hi[:, :, (s - 2) // 2 % 2, (s % 2) * P:(s % 2 + 1) * P],
                                   ps[2][:, :, :].rearrange("p a (k s) -> p (a k) s", k=4), ACT.Copy
                                   ).then_inc(b_hi, 1)
                if not new:
                    o_copy(h, s, new)
                    return
                for c in range(2):
                    act.wait_ge(b_max, 2 * g + c + 1)
                    act.activation(prob[:, s % 2, c, :], ps[c][:, :, :].rearrange("p a c -> p (a c)"), ACT.Exp,
                                   bias=bst[:, c, s % NT:s % NT + 1],
                                   accum_out=bst[:, 2 + c, s % NT:s % NT + 1]).then_inc(b_exp, 1)
                if s == NT - 1 and not (isinstance(h, int) and h == HB - 1):
                    for n in (0, 2, 4):
                        set_copy(h + 1, n)
                act.wait_ge(b_small, 2 * g + 2)
                act.activation(prob[:, s % 2, 1, :], prob[:, s % 2, 1, :], ACT.Copy,
                               scale=bst[:, 6, s % NT:s % NT + 1]).then_inc(b_scaled, 1)
                o_copy(h, s, new)

            def keys_a():
                for n in range(2):
                    act.wait_ge(a_kset, 2 * n + 1)
                    act.activation(kta[:, 0, n, :], ps[0][:, :, :].rearrange("p a c -> p (a c)"), ACT.Copy
                                   ).then_inc(a_kt_act, 1)

            def q_copy(i, parity, first=False):
                act.wait_ge(a_qset, 2 * i + 1)
                act.activation(qa_t[parity][:, 0:4, :].rearrange("p h s -> p (h s)"),
                               ps[0][:, 0, :] if first else ps[3][:, 1, :], ACT.Copy).then_inc(a_qt_act, 1)

            def first_q():
                q_copy(0, 0, True)

            steps(act, step, {8: keys_a, 9: first_q})


            def step_a(i, parity, s):
                n = 4 * i + s
                bi, bs = pair_before(i, s)
                if exists(bi):
                    nk = n_keys(bi)
                    act.wait_ge(a_turn, n)
                    act.activation(pt_hi[:, bs // 2, 0:nk, (bs % 2) * 2 * P:(bs % 2 + 1) * 2 * P].rearrange(
                        "p k (h s) -> p h k s", h=2), ps[2][:, :, 0:nk * P].rearrange("p h (k s) -> p h k s", k=nk),
                        ACT.Copy).then_inc(a_hi, 1)
                if exists(i):
                    nk = n_keys(i)
                    act.wait_ge(a_neg, n + 1)
                    for hh in range(2):
                        act.activation(prob_a[:, 2 * (s % 2) + hh, 0:nk * P], ps[s % 2][:, hh, 0:nk * P], ACT.Exp,
                                       bias=ast[:, parity, 1, 2 * s + hh:2 * s + hh + 1],
                                       accum_out=ast[:, parity, 2, 2 * s + hh:2 * s + hh + 1]).then_inc(a_exp, 1)
                if s % 2 == 0 and exists(i - 1):
                    act.wait_ge(a_pv, 2 * i - 1 + s // 2)
                    act.activation(o_ta[:, 1 - parity, s // 2, :], ps[3][:, 0, :], ACT.Copy).then_inc(a_ot, 1)
                if s == 1 and exists(i) and exists(i + 1):
                    q_copy(i + 1, 1 - parity)
                if isinstance(i, int) and i == NT - 1 and s == 1:
                    root(0, NT - 2, 1)
                if s == 3 and exists(i):
                    act.wait_ge(a_sink, i + 1)
                    act.activation(ast[:, parity, 4, :], ast[:, parity, 3, :], ACT.Exp).then_inc(a_sink_exp, 1)

            def root(t0, t1, n):
                act.wait_ge(c_mean, n)
                act.activation(y_stat[:, 2, t0:t1, :], y_stat[:, 1, t0:t1, :], ACT.Sqrt).then_inc(c_std, 1)

            def y_hi(t, parity):
                act.wait_ge(c_turn, t + 1)
                act.activation(yt_hi[:, parity, :, :].rearrange("p k s -> p (k s)"),
                               ps[2][:, :, :].rearrange("p a c -> p (a c)"), ACT.Copy).then_inc(c_hi, 1)

            def token(pair, parity):
                t = 2 * pair + parity
                if exists(t + 1):
                    y_hi(t + 1, 1 - parity)

            tile_steps(act, step_a, lambda: y_hi(0, 0))

            root(NT - 2, NT, 2)
            token_steps(act, token)

        @block.vector
        def _(dve):
            dve.memset(ones, 1.0).then_inc(setup_dve, 1)
            dve.memset(gate_row[:, :], 0.0).then_inc(gate_zero, 1)
            dve.wait_ge(load, 48)
            dve.tensor_tensor(param("gain"), param("gain"), const("gain_scale"), ALU.mult).then_inc(setup_dve, 1)
            dve.tensor_tensor(param("gain_swapped"), param("gain_swapped"), const("swap_scale"), ALU.mult
                              ).then_inc(setup_dve, 1)
            n_trig = [0]

            def link(instruction):
                n_trig[0] += 1
                instruction.then_inc(trig_step, 1)
                dve.wait_ge(trig_step, n_trig[0])

            link(dve.tensor_copy(ident_r[:, :], const("identity")))
            link(dve.tensor_copy(pos_f, pos_i))
            link(dve.tensor_tensor(ang.rearrange("p (t d) -> p t d", t=NT),
                                   pos_f.unsqueeze(2).broadcast_to([P, NT, HD // 2]),
                                   const("inv_freq").unsqueeze(1).broadcast_to([P, NT, HD // 2]), ALU.mult))

            def whole_turns(turn):
                link(dve.tensor_scalar(ang_n, ang, 1.0 / (2 * np.pi), turn, ALU.mult, ALU.add))
                link(dve.tensor_scalar(ang_n, ang_n, MAGIC, MAGIC, ALU.add, ALU.subtract))

            def less_turns(place, which):
                for n in which:
                    link(dve.scalar_tensor_tensor(place, ang_n, -two_pi_parts()[n], ang if n == 0 else place,
                                                  ALU.mult, ALU.add))

            def bounded(place, turn):
                link(dve.tensor_scalar(place, place, turn * 2 * np.pi, PI_IN, ALU.add, ALU.min))
                link(dve.tensor_scalar(place, place, -PI_IN, None, ALU.max))

            def angles(k):
                place, turn = (ang_r, 0.0) if k < 4 else (ang_c, 0.25)
                if k % 4 == 0:
                    whole_turns(turn)
                elif k % 4 < 3:
                    less_turns(place, (2 * (k % 4) - 2, 2 * (k % 4) - 1))
                else:
                    bounded(place, turn)
                if k == NK - 1:
                    dve.tensor_copy(small[:, 80:81], ones).then_inc(setup_dve, 1)

            def low_w(k):
                dve.wait_ge(w_hi_done, k + 1)
                dve.tensor_tensor(w_lo[:, k, :], w_raw[:, k % 4, :], w_hi[:, k, :].bitcast(F32), ALU.subtract
                                  ).then_inc(w_ready, 1)

            acc2 = mod_acc[:, :]

            def sum_ada(k):
                dve.wait_ge(ada_in[k % 4], 16 * (k // 4 + 1))
                if k == 0:
                    dve.wait_ge(setup_act, 1)
                    dve.tensor_scalar(acc2, ada[:, 0, :], silu_c[:, 0:1], None, ALU.mult).then_inc(ada_sum, 1)
                else:
                    dve.wait_ge(ada_sum, k)
                    dve.scalar_tensor_tensor(acc2, ada[:, k % 4, :], silu_c[:, k:k + 1], acc2, ALU.mult, ALU.add
                                             ).then_inc(ada_sum, 1)

            for k in range(NK):
                if 2 * k < NK:
                    sum_ada(2 * k)
                dve.wait_ge(x_squared, k + 1)
                dve.tensor_scalar(x_ms[:, k:k + 1], x_ssq[:, k:k + 1], 1.0 / D, EPS, ALU.mult, ALU.add
                                  ).then_inc(x_mean, 1)
                angles(k)
                dve.wait_ge(x_root, k + 1)
                dve.reciprocal(x_rstd[:, k:k + 1], x_std[:, k:k + 1]).then_inc(x_recip, 1)
                dve.wait_ge(x_recip, k + 1)
                dve.tensor_scalar(x_in[:, k % 4, :], x_in[:, k % 4, :], x_rstd[:, k:k + 1], None, ALU.mult
                                  ).then_inc(x_normed, 1)
                if 2 * k < NK:
                    sum_ada(2 * k + 1)
                if k >= 4:
                    low_w(k - 4)
                if k == 5:
                    dve.wait_ge(mod_cols, 1)
                    dve.tensor_tensor(shift_b, ps[0][:, 0, 0:8], param("b_shift"), ALU.add).then_inc(mod_done, 1)
                    link(dve.tensor_tensor(scale_a, ps[0][:, 0, 8:16], param("b_scale"), ALU.add))
                    dve.scalar_tensor_tensor(scale_a, scale_a, 1.0, param("norm_gain"), ALU.add, ALU.mult
                                             ).then_inc(mod_done, 1)
            dve.wait_ge(x_turned, NK)
            for n, (a, b) in enumerate(groups):
                for half in range(2):
                    dve.wait_ge(h_affine, NK * n + 4 * half + 4)
                    dve.tensor_copy(h_hi[:, 4 * half:4 * half + 4, a * P:b * P], x_t[half][:, :, a * P:b * P]
                                    ).then_inc(h_split, 1)
                for half in range(2 if n < 2 else 1):
                    dve.wait_ge(h_split, 2 * n + half + 1)
                    low = dve.tensor_tensor(h_lo[:, 4 * half:4 * half + 4, a * P:b * P],
                                            x_t[half][:, :, a * P:b * P],
                                            h_hi[:, 4 * half:4 * half + 4, a * P:b * P].bitcast(F32), ALU.subtract)
                low.then_inc(h_ready, 1)
                if n == 0:
                    for k in range(4, NK):
                        low_w(k)

            def refill(ci, n):
                for k in range(NK):
                    dve.wait_ge(w_hi_done, NK * ci + k + NK + 1)
                    dve.tensor_tensor(w_lo[:, k, 0:n], w_raw[:, k % 4, 0:n], w_hi[:, k, 0:n].bitcast(F32),
                                      ALU.subtract).then_inc(w_ready, 1)

            def norm_tile(ci, t, m, place, n):
                nh = n // HD
                dve.wait_ge(squared, m + t + 1)
                dve.tensor_reduce(stat[:, 0, t, 0:nh], heads(sq[:, t % 2, 0:n], nh), AXX, ALU.add
                                  ).then_inc(ssq_done, 1)
                dve.wait_ge(ssq_done, 2 * (m + t) + 1)
                dve.tensor_scalar(stat[:, 1, t, 0:nh], stat[:, 0, t, 0:nh], 1.0 / HD, EPS, ALU.mult, ALU.add
                                  ).then_inc(ssq_done, 1)
                dve.wait_ge(std_done, m + t + 1)
                dve.reciprocal(stat[:, 3, t, 0:nh], stat[:, 2, t, 0:nh]).then_inc(rstd_done, 1)
                dve.wait_ge(rstd_done, m + t + 1)
                if n < CW:
                    dve.tensor_copy(kv_a[:, t, 2 * HD:4 * HD], acc[t % 4][:, 2 * HD:4 * HD])
                dve.tensor_tensor(heads(place, nh), heads(acc[t % 4][:, 0:n], nh),
                                  stat[:, 3, t, 0:nh].unsqueeze(2).broadcast_to([P, nh, HD]), ALU.mult
                                  ).then_inc(bank_free[t % 4], 1)

            def norm_chunk(ci, m, place, n, next_n):
                for t in range(NT - 1):
                    norm_tile(ci, t, m, place(t), n)
                if next_n:
                    refill(ci, next_n)
                norm_tile(ci, NT - 1, m, place(NT - 1), n)

            with dve.Fori(0, 2) as ci:
                norm_chunk(ci, ci * NT, lambda t: qk_b[:, bass.ds(ci, 1), t, :].rearrange("p o c -> p (o c)"),
                           CW, CW)
            for k in range(NK):
                dve.wait_ge(gate_loaded[k], 16)
                dve.wait_ge(gate_sum, k) if k else dve.wait_ge(gate_bias, 16)
                dve.scalar_tensor_tensor(gate_row[:, :], gate_in[k], silu_c[:, k:k + 1],
                                         gate_row[:, :], ALU.mult, ALU.add).then_inc(gate_sum, 1)
            lam = param("lambdas").rearrange("p (a b d) -> p a b d", a=2, b=2)
            link(dve.tensor_tensor(lam[:, :, 0, :], lam[:, :, 0, :], lam[:, :, 1, :], ALU.mult))
            dve.tensor_reduce(lam_sum, lam[:, :, 0, :], AXX, ALU.add).then_inc(setup_dve, 1)
            dve.tensor_scalar(param("subln"), param("subln"), 1.0 - LAMBDA_INIT, None, ALU.mult
                              ).then_inc(setup_dve, 1)
            refill(2, CW)
            with dve.Fori(3, 5) as ci:
                refill(ci, CW)
            norm_chunk(5, 2 * NT, lambda t: q_a[:, t, :], CW, 4 * HD)
            dve.wait_ge(gate_mm, 1)
            dve.tensor_copy(gate_row[:, :], ps[2][:, :, :].rearrange("p a c -> p (a c)"))
            norm_chunk(6, 3 * NT, lambda t: kv_a[:, t, 0:2 * HD], 2 * HD, 0)


            for n, (st, src) in enumerate(((q_st, head_q(0)), (k_st, head_k(0)))):
                dve.wait_ge(b_first_hi, n + 1)
                dve.tensor_tensor(st[:, :, :, 1, :], src, st[:, :, :, 0, :].bitcast(F32), ALU.subtract
                                  ).then_inc(b_first_lo, 1)

            def set_copy(h, n):
                dve.wait_ge(b_set, 6 * h + n + 1)
                dve.tensor_copy((q1t, q2t, kt)[n % 3][:, n // 3, :],
                                ps[n % 2][:, :, :].rearrange("p a c -> p (a c)")).then_inc(b_set_dve, 1)

            dve.wait_ge(setup_act, 4)
            link(dve.tensor_scalar(neg_sink, param("sink"), -1.0, None, ALU.mult))
            link(dve.tensor_scalar(neg_lam, lam_exp[:, 1:2], lam_exp[:, 0:1], -LAMBDA_INIT, ALU.subtract, ALU.add))
            for n in (1, 3, 5):
                set_copy(0, n)

            def write_y(h, s):
                if s % 2 == 1 and s >= 7:
                    m = (s - 7) // 2
                    dve.wait_ge(b_back, 4 * h + m + 1)
                    dve.tensor_tensor(y_b[:, 2 * (m % 4):2 * (m % 4) + 2, bass.ds((h + m // 4) * P, P)],
                                      ps[3][:, 1, (m % 2) * 2 * P:(m % 2 + 1) * 2 * P].rearrange(
                                          "p (t d) -> p t d", t=2),
                                      bst[:, 4, 2 * (m % 4):2 * (m % 4) + 2].unsqueeze(2).broadcast_to([P, 2, P]),
                                      ALU.mult).then_inc(b_y, 1)

            def step(h, s, new):
                g = NT * h + s
                j = s % NT
                if new:
                    for c in range(2):
                        dve.wait_ge(b_qk, 2 * g + c + 1)
                        dve.tensor_reduce(bst[:, c, j:j + 1], ps[c][:, :, :].rearrange("p a c -> p (a c)"), AXX,
                                          ALU.max, negate=True).then_inc(b_max, 1)
                if s >= 2 and (new or s < NT + 2):
                    dve.wait_ge(b_hi, g - 1)
                    place = slice((s % 2) * P, (s % 2 + 1) * P)
                    dve.tensor_tensor(at_lo[:, :, (s - 2) // 2 % 2, place],
                                      ps[2][:, :, :].rearrange("p a (k s) -> p (a k) s", k=4),
                                      at_hi[:, :, (s - 2) // 2 % 2, place].bitcast(F32), ALU.subtract
                                      ).then_inc(b_lo, 1)
                write_y(h, s)
                if not new:
                    return
                dve.wait_ge(b_exp, 2 * g + 2)
                dve.reciprocal(bst[:, 4:6, j:j + 1], bst[:, 2:4, j:j + 1]).then_inc(b_small, 1)
                dve.wait_ge(b_small, 2 * g + 1)
                dve.scalar_tensor_tensor(bst[:, 6, j:j + 1], bst[:, 2, j:j + 1], bst[:, 5, j:j + 1], neg_lam,
                                         ALU.mult, ALU.mult).then_inc(b_small, 1)
                if s == NT - 1 and not (isinstance(h, int) and h == HB - 1):
                    for n in (1, 3, 5):
                        set_copy(h + 1, n)

            def keys_a():
                for n in range(2):
                    dve.wait_ge(a_kset, 2 * n + 2)
                    dve.tensor_copy(kta[:, 1, n, :], ps[1][:, :, :].rearrange("p a c -> p (a c)")
                                    ).then_inc(a_kt_dve, 1)

            def q_copy(i, parity, first=False):
                dve.wait_ge(a_qset, 2 * i + 2)
                dve.tensor_copy(qa_t[parity][:, 4:8, :].rearrange("p h s -> p (h s)"),
                                ps[1][:, 0, :] if first else ps[3][:, 1, :]).then_inc(a_qt_dve, 1)

            def first_q():
                q_copy(0, 0, True)

            steps(dve, step, {8: keys_a, 9: first_q})


            def step_a(i, parity, s):
                n = 4 * i + s
                bi, bs = pair_before(i, s)
                if exists(i):
                    nk = n_keys(i)
                    pair = slice(2 * s, 2 * s + 2)
                    dve.wait_ge(a_qk, n + 1)
                    dve.tensor_reduce(ast[:, parity, 0, pair], ps[s % 2][:, :, 0:nk * P], AXX, ALU.max, negate=True
                                      ).then_inc(a_max, 1)
                    dve.wait_ge(a_max, n + 1)
                    dve.tensor_tensor(ast[:, parity, 1, pair], ast[:, parity, 0, pair], neg_sink[:, pair], ALU.min
                                      ).then_inc(a_neg, 1)
                if s == 3 and exists(i):
                    dve.wait_ge(a_neg, n + 1)
                    dve.tensor_tensor(ast[:, parity, 3, :], ast[:, parity, 1, :], param("sink"), ALU.add
                                      ).then_inc(a_sink, 1)
                if s == 1 and exists(i - 2):
                    dve.wait_ge(a_back, i - 1)
                    dve.wait_ge(a_den, 2 * i - 2)
                    dve.tensor_tensor(heads(q_a[:, bass.ds(i - 2, 1), :].rearrange("p o c -> p (o c)"), HA),
                                      heads(ps[3][:, 1, :], HA),
                                      ast[:, parity, 6, :].unsqueeze(2).broadcast_to([P, HA, HD]), ALU.mult
                                      ).then_inc(a_y, 1)
                if exists(bi):
                    nk = n_keys(bi)
                    place = pt_hi[:, bs // 2, 0:nk, (bs % 2) * 2 * P:(bs % 2 + 1) * 2 * P]
                    low = pt_lo[:, bs // 2, 0:nk, (bs % 2) * 2 * P:(bs % 2 + 1) * 2 * P]
                    dve.wait_ge(a_hi, n)
                    dve.tensor_tensor(low.rearrange("p k (h s) -> p h k s", h=2),
                                      ps[2][:, :, 0:nk * P].rearrange("p h (k s) -> p h k s", k=nk),
                                      place.rearrange("p k (h s) -> p h k s", h=2).bitcast(F32), ALU.subtract
                                      ).then_inc(a_lo, 1)
                if s == 0 and exists(i - 1):
                    dve.wait_ge(a_sink_exp, i)
                    dve.tensor_tensor(ast[:, 1 - parity, 5, :], ast[:, 1 - parity, 4, :], ast[:, 1 - parity, 2, :],
                                      ALU.add).then_inc(a_den, 1)
                    dve.wait_ge(a_den, 2 * i - 1)
                    dve.reciprocal(ast[:, 1 - parity, 6, :], ast[:, 1 - parity, 5, :]).then_inc(a_den, 1)
                if s == 3 and exists(i) and exists(i + 1):
                    q_copy(i + 1, 1 - parity)
                if s == 2 and exists(i - 1) and exists(i + 1):
                    sums(i - 1, 1 - parity)
                if isinstance(i, int) and i == NT - 2 and s == 3:
                    means(0, NT - 2, 1)
                if isinstance(i, int) and i == NT - 1 and s == 2:
                    reciprocals(0, NT - 2, 1)
                if isinstance(i, int) and i == NT - 1 and s == 3:
                    normed(0)
                    normed(1)

            def sums(t, parity):
                dve.wait_ge(c_sq, t + 1)
                dve.tensor_reduce(y_stat[:, 0, bass.ds(t, 1), :].rearrange("p o h -> p (o h)"),
                                  y_sq[:, parity, :, :], AXX, ALU.add).then_inc(c_ssq, 1)

            def means(t0, t1, n):
                dve.wait_ge(c_ssq, t1)
                dve.tensor_scalar(y_stat[:, 1, t0:t1, :], y_stat[:, 0, t0:t1, :], 1.0 / (2 * HD), EPS,
                                  ALU.mult, ALU.add).then_inc(c_mean, 1)

            def reciprocals(t0, t1, n):
                dve.wait_ge(c_std, n)
                dve.reciprocal(y_stat[:, 3, t0:t1, :], y_stat[:, 2, t0:t1, :]).then_inc(c_rstd, 1)
                dve.wait_ge(c_rstd, n)

            def normed(t):
                yb = y_b[:, bass.ds(t, 1), :].rearrange("p o (h d) -> p (o h) d", h=HB)
                rstd = y_stat[:, 3, bass.ds(t, 1), :].rearrange("p o h -> p (o h)")
                dve.tensor_tensor(yb, yb, rstd.unsqueeze(2).broadcast_to([P, HB, 2 * HD]), ALU.mult
                                  ).then_inc(c_norm, 1)

            def y_low(t, parity):
                dve.wait_ge(c_hi, t + 1)
                dve.tensor_tensor(yt_lo[:, parity, :, :].rearrange("p k s -> p (k s)"),
                                  ps[2][:, :, :].rearrange("p a c -> p (a c)"),
                                  yt_hi[:, parity, :, :].rearrange("p k s -> p (k s)").bitcast(F32), ALU.subtract
                                  ).then_inc(c_lo, 1)

            def token(pair, parity):
                t = 2 * pair + parity
                if exists(t + 2):
                    normed(t + 2)
                if exists(t + 1):
                    y_low(t + 1, 1 - parity)
                for half in range(2):
                    w = slice(half * 512, (half + 1) * 512)
                    dve.wait_ge(c_mm, 2 * t + half + 1)
                    if half == 0 and exists(t - 2):
                        dve.wait_ge(stored[parity], 16 * pair)
                    dve.tensor_tensor(o_out[:, parity, w], ps[parity][:, half, :], gate_row[:, w], ALU.mult
                                      ).then_inc(c_scaled, 1)

            tile_steps(dve, step_a, lambda: y_low(0, 0))

            for t in range(NT - 2, NT):
                sums(t, t % 2)
            means(NT - 2, NT, 2)
            reciprocals(NT - 2, NT, 2)
            token_steps(dve, token)

        @block.tensor
        def _(pe):
            ident = const("identity")
            pe.wait_ge(load, 48)
            pe.wait_ge(setup_dve, 3)

            def turn_x(t):
                pe.wait_ge(x_normed, t + 1)
                if t >= 2:
                    pe.wait_ge(x_kept, 2 * (t - 1))
                for k in range(NK):
                    last = pe.transpose(ps[2 + t % 2][:, k // 4, (k % 4) * P:(k % 4 + 1) * P],
                                        x_in[:, t % 4, k * P:(k + 1) * P], ident)
                last.then_inc(x_turned, 1)

            for t in range(4):
                turn_x(t)
            pe.wait_ge(ada_sum, NK)
            for j in range(16):
                last = pe.matmul(ps[0][:, 0, j:j + 1], mod_acc[:, j * P:(j + 1) * P], ones, start=True, stop=True)
            last.then_inc(mod_cols, 1)
            for t in range(4, NT):
                turn_x(t)
            pe.wait_ge(mod_done, 2)

            def proj_chunk(ci, n):
                for t in range(NT):
                    for i, (first, _) in enumerate(groups):
                        if t == first:
                            pe.wait_ge(h_ready, i + 1)
                            if i >= 2:
                                pe.wait_ge(h_low, i - 1)
                    pe.wait_ge(bank_free[t % 4], 2 * ci + t // 4 + BANK0)
                    tok = slice(t * P, (t + 1) * P)
                    for k in range(NK):
                        if t == 0:
                            pe.wait_ge(w_ready, NK * ci + k + 1)
                        pe.matmul(acc[t % 4][:, 0:n], h_hi[:, k, tok], w_hi[:, k, 0:n], start=(k == 0), stop=False)
                        pe.matmul(acc[t % 4][:, 0:n], h_hi[:, k, tok], w_lo[:, k, 0:n], start=False, stop=False)
                        last = pe.matmul(acc[t % 4][:, 0:n], h_lo[:, k, tok], w_hi[:, k, 0:n], start=False,
                                         stop=(k == NK - 1))
                        if t == NT - 1 and k < NK - 1:
                            last.then_inc(w_slot_free, 1)
                    last.then_inc(proj_done, 1)

            with pe.Fori(0, NFULL) as ci:
                proj_chunk(ci, CW)
            pe.wait_ge(gate_sum, NK)
            for half in range(2):
                last = pe.matmul(ps[2][:, half, :], const("ones"), gate_row[:, half * 512:(half + 1) * 512],
                                 start=True, stop=True)
            last.then_inc(gate_mm, 1)
            proj_chunk(NFULL, 4 * HD)

            def sets(h, which):
                if which[0] == 0 and isinstance(h, int):
                    pe.wait_ge(b_first_hi, 3)
                    pe.wait_ge(b_first_lo, 2)
                elif which[0] == 0:
                    pe.wait_ge(b_stage, 10 * h)
                for n in which:
                    if n >= 2 and n % 2 == 0:
                        pe.wait_ge(b_set_act, 3 * h + n // 2)
                    elif n >= 2:
                        pe.wait_ge(b_set_dve, 3 * h + n // 2)
                    elif not isinstance(h, int):
                        pe.wait_ge(b_exp, 2 * NT * h + n - 1)
                    c, kind = n // 3, n % 3
                    for t in range(NT):
                        src = (q_st[:, t, c, 0:2, :], q_st[:, t, c, 1:3, :], k_st[:, t, c, :, :])[kind]
                        last = pe.transpose(ps[n % 2][:, t // 4, (t % 4) * P:(t % 4 + 1) * P].bitcast(F32R),
                                            src.rearrange("p a d -> p (a d)"), ident_r[:, :])
                    last.then_inc(b_set, 1)

            def scores(h, j, c):
                if j == 0:
                    pe.wait_ge(b_set_act, 3 * h + 3)
                    pe.wait_ge(b_set_dve, 3 * h + (1 if c == 0 else 3))
                else:
                    pe.wait_ge(b_exp, 2 * (NT * h + j) + c - 1)
                q = slice(j * P, (j + 1) * P)
                for half in range(2):
                    kk = kt[:, c, half * 512:(half + 1) * 512]
                    pe.matmul(ps[c][:, half, :], q1t[:, c, q], kk, start=True, stop=False)
                    last = pe.matmul(ps[c][:, half, :], q2t[:, c, q], kk, start=False, stop=True)
                last.then_inc(b_qk, 1)

            def turn(h, j):
                pe.wait_ge(b_attn, NT * h + j + 1)
                if not (isinstance(h, int) and h == 0 and j == 0):
                    pe.wait_ge(b_lo, NT * h + j)
                for k in range(NT):
                    last = pe.transpose(ps[2][:, k // 4, (k % 4) * P:(k % 4 + 1) * P],
                                        prob[:, j % 2, 0, k * P:(k + 1) * P], ident)
                last.then_inc(b_turn, 1)

            def pv(h, m, half):
                if half == 0:
                    pe.wait_ge(b_lo, NT * h + 2 * m + 2)
                    if not (isinstance(h, int) and h == 0 and m == 0):
                        pe.wait_ge(b_ot, 4 * h + m)
                pe.wait_ge(b_v, 4 * (h + m // 4) + 2 * half + 2)
                o = ps[3][:, 0, (m % 2) * 2 * P:(m % 2 + 1) * 2 * P]
                for k in range(4 * half, 4 * half + 4):
                    pe.matmul(o, v_hi[:, k, :], at_hi[:, k, m % 2, :], start=(k == 0), stop=False)
                    pe.matmul(o, v_hi[:, k, :], at_lo[:, k, m % 2, :], start=False, stop=False)
                    last = pe.matmul(o, v_lo[:, k, :], at_hi[:, k, m % 2, :], start=False, stop=(k == NT - 1))
                if half == 1:
                    last.then_inc(b_pv, 1)
                elif m == 3:
                    last.then_inc(b_v_free, 1)

            def back(h, m):
                pe.wait_ge(b_ot, 4 * h + m + 1)
                pe.wait_ge(b_y, 4 * h + m + Y0)
                for t in range(2):
                    last = pe.transpose(ps[3][:, 1, (2 * (m % 2) + t) * P:(2 * (m % 2) + t + 1) * P],
                                        o_tb[:, m % 2, t * P:(t + 1) * P], ident)
                last.then_inc(b_back, 1)

            def step(h, s, new):
                change = s == NT - 1
                more = new and not (isinstance(h, int) and h == HB - 1 and change)
                head, j = (h + 1, s + 1 - NT) if s + 1 >= NT else (h, s + 1)
                if more and not change:
                    scores(head, j, 0)
                if more and change:
                    sets(head, (0, 1))
                if s >= 1 and (new or s < NT + 1):
                    turn(h, s - 1)
                if more and change:
                    sets(head, (2, 3, 4, 5))
                    scores(head, 0, 0)
                    scores(head, 0, 1)
                if more and not change:
                    scores(head, j, 1)
                if s >= 6 and s % 2 == 0:
                    back(h, (s - 6) // 2)
                if s >= 3 and (new or s < NT + 3):
                    pv(h, (s - 3) // 2, (s - 3) % 2)

            sets(0, range(6))
            scores(0, 0, 0)
            scores(0, 0, 1)
            def keys_a():
                pe.wait_ge(a_kst, 3)
                pe.wait_ge(b_exp, 2 * NT * HB)
                for n in range(2):
                    for g in range(GA):
                        if n == 1:
                            pe.wait_ge((a_kt_act, a_kt_dve)[g], 1)
                        for t in range(NT):
                            last = pe.transpose(ps[g][:, t // 4, (t % 4) * P:(t % 4 + 1) * P].bitcast(F32R),
                                                ka_st[:, t, g, n:n + 2, :].rearrange("p a d -> p (a d)"),
                                                ident_r[:, :])
                        last.then_inc(a_kset, 1)

            def q_unit(i, u):
                first = isinstance(i, int) and i == 0
                if u == 0:
                    pe.wait_ge(a_qst, 2 * i + 2)
                    if first:
                        pe.wait_ge(a_kt_act, 2)
                    elif isinstance(i, int) and i == 1:
                        pe.wait_ge(b_y, 4 * HB + Y0)
                    elif isinstance(i, int) and i == 2:
                        pe.wait_ge(a_qt_dve, i)
                    else:
                        pe.wait_ge(a_y, i - 2)
                elif first:
                    pe.wait_ge(a_kt_dve, 2)
                else:
                    pe.wait_ge(a_qt_act, i + 1)
                bank = ps[u][:, 0, :] if first else ps[3][:, 1, :]
                for hh in range(4):
                    last = pe.transpose(bank[:, hh * P:(hh + 1) * P].bitcast(F32R),
                                        qa_st[:, 4 * u + hh, :, :].rearrange("p a d -> p (a d)"),
                                        ident_r[:, :])
                last.then_inc(a_qset, 1)

            def scores_a(i, parity, s):
                if s == 0:
                    pe.wait_ge(a_qt_act, i + 1)
                elif s == 2:
                    pe.wait_ge(a_qt_dve, i + 1)
                if isinstance(i, int) and i == 0 and s == 1:
                    pe.wait_ge(a_qt_dve, 1)
                if not (isinstance(i, int) and i == 0 and s < 2):
                    pe.wait_ge(a_exp, 2 * (4 * i + s) - 2)
                nk = n_keys(i)
                first = isinstance(i, int) and i == 0
                for hh in range(2):
                    o = ps[s % 2][:, hh, 0:nk * P]
                    for n in range(2):
                        keys = kta[:, s // 2, n, bass.ds(0 if first else (i - 1) * P, nk * P)]
                        pe.matmul(o, qa_t[parity][:, 2 * s + hh, :], keys, start=(n == 0), stop=False)
                    last = pe.matmul(o, ident_r[:, :], mask[:, P if first else 0:(P if first else 0) + nk * P],
                                     start=False, stop=True)
                last.then_inc(a_qk, 1)

            def turn_a(i, s):
                n = 4 * i + s
                pe.wait_ge(a_exp, 2 * n + 2)
                if not (isinstance(i, int) and n == 0):
                    pe.wait_ge(a_lo, n)
                for hh in range(2):
                    for k in range(n_keys(i)):
                        last = pe.transpose(ps[2][:, hh, k * P:(k + 1) * P],
                                            prob_a[:, 2 * (s % 2) + hh, k * P:(k + 1) * P], ident)
                last.then_inc(a_turn, 1)

            def pv_a(i, g):
                pe.wait_ge(a_lo, 4 * i + 2 * g + 2)
                pe.wait_ge(a_vst, 4 * i + 2 * g + 2)
                if not (isinstance(i, int) and i == 0 and g == 0):
                    pe.wait_ge(a_ot, 2 * i + g)
                nk = n_keys(i)
                for k in range(nk):
                    v = va_st[:, k, g, :, :].rearrange("p a d -> p (a d)")
                    pe.matmul(ps[3][:, 0, :], v, pt_hi[:, g, k, :], start=(k == 0), stop=False)
                    last = pe.matmul(ps[3][:, 0, :], v, pt_lo[:, g, k, :], start=False, stop=(k == nk - 1))
                last.then_inc(a_pv, 1)

            def back_a(i, parity):
                pe.wait_ge(a_ot, 2 * i + 2)
                if exists(i + 2):
                    pe.wait_ge(a_qt_dve, i + 3)
                else:
                    pe.wait_ge(a_y, i)
                for n in range(2 * 4):
                    last = pe.matmul(ps[3][:, 1, n * HD:(n + 1) * HD],
                                     o_ta[:, parity, n // 4, (n % 4) * P:(n % 4 + 1) * P], const("halves"),
                                     start=True, stop=True)
                last.then_inc(a_back, 1)

            def step_a(i, parity, s):
                bi, bs = pair_before(i, s)
                more = exists(i) and exists(i + 1)
                if exists(bi):
                    turn_a(bi, bs)
                if s < 3 and exists(i):
                    scores_a(i, parity, s + 1)
                elif s == 3 and more:
                    scores_a(i + 1, 1 - parity, 0)
                if s == 3 and exists(i):
                    pv_a(i, 0)
                if s == 1 and exists(i - 1):
                    pv_a(i - 1, 1)
                if s == 0 and exists(i - 2):
                    back_a(i - 2, parity)
                if s in (1, 2) and more:
                    q_unit(i + 1, s - 1)

            def keys_and_first_q():
                keys_a()
                for u in range(2):
                    q_unit(0, u)

            def first_scores():
                pe.wait_ge(a_mask, 1)
                scores_a(0, 0, 0)

            steps(pe, step, {8: keys_and_first_q, 10: first_scores})

            def turn_y(t, parity):
                pe.wait_ge(c_cat, 2 * t + 2)
                for k in range(NK):
                    last = pe.transpose(ps[2][:, k // 4, (k % 4) * P:(k % 4 + 1) * P],
                                        y_cat[:, parity, k * P:(k + 1) * P], ident)
                last.then_inc(c_turn, 1)

            def token(pair, parity):
                t = 2 * pair + parity
                pe.wait_ge(c_lo, t + 1)
                if exists(t - 2):
                    pe.wait_ge(c_scaled, 2 * t - 2)
                for half in range(2):
                    o = ps[parity][:, half, :]
                    w = slice(half * 512, (half + 1) * 512)
                    for k in range(NK):
                        pe.matmul(o, yt_hi[:, parity, k, :], wo_hi[:, k, w], start=(k == 0), stop=False)
                        pe.matmul(o, yt_hi[:, parity, k, :], wo_lo[:, k, w], start=False, stop=False)
                        last = pe.matmul(o, yt_lo[:, parity, k, :], wo_hi[:, k, w], start=False, stop=(k == NK - 1))
                    last.then_inc(c_mm, 1)
                    if half == 0 and exists(t + 1):
                        turn_y(t + 1, 1 - parity)

            tile_steps(pe, step_a, lambda: turn_y(0, 0))

            pe.wait_ge(wo_split, 2 * NK)
            token_steps(pe, token)
    return nc


def constants():
    c = np.zeros((P, N_CONSTS), np.float32)

    def put(name, value):
        c[:, CONSTS[name][0]:CONSTS[name][1]] = value

    put("identity", np.eye(P))
    put("halves", np.concatenate([np.eye(HD)] * 2))
    put("ones", 1.0)
    q, k = np.arange(P)[:, None], np.arange(P)[None, :]
    band = np.zeros((P, 3 * P), np.float32)
    band[:, 0:P][k < q] = MASKED
    band[:, 2 * P:][k > q] = MASKED
    put("band", band)
    put("inv_freq", np.float32(1.0) / np.float32(ROPE_THETA) ** (np.arange(0, HD, 2, dtype=np.float32) / np.float32(HD)))
    scale = np.repeat(np.float32([HD ** -0.5, 1.0, HD ** -0.5, 1.0]), HD)
    put("gain_scale", scale)
    sign = np.tile(np.repeat(np.float32([-1.0, 1.0]), HD // 2), 4)
    put("swap_scale", scale * sign)
    return c


def kernel(x, c, positions, w_ada, b_ada, norm_gain, w_in, q_norm_a, k_norm_a, sink_a, q_norm_b, k_norm_b,
           lambda_q1, lambda_k1, lambda_q2, lambda_k2, subln_gain, w_out):
    import concourse.bacc as bacc
    from concourse.bass_utils import run_bass_kernel_spmd

    def a(v):
        return np.ascontiguousarray(np.asarray(v))

    gains = [a(v)[0] for v in (q_norm_b, k_norm_b, q_norm_a, k_norm_a)]
    swapped = [np.concatenate([g[HD // 2:], g[:HD // 2]]) for g in gains]
    b = a(b_ada)[0]

    def rows(v):
        return np.broadcast_to(v.reshape(1, -1), (P, v.size))

    def cols(v):
        return v.reshape(NK, P).T

    params = np.concatenate([
        rows(np.concatenate(gains)), rows(np.concatenate(swapped)), rows(a(sink_a)[0]), rows(a(subln_gain)[0]),
        rows(np.concatenate([a(v)[0] for v in (lambda_q1, lambda_k1, lambda_q2, lambda_k2)])),
        cols(a(c)[0]), cols(b[0:D]), cols(b[D:2 * D]), cols(a(norm_gain)[0])], axis=1)
    w = a(w_in)[0]
    starts = (1280, 1792, 2304, 768, 2816, 0)
    chunks = np.stack([w[:, s:s + CW] for s in starts]).reshape(NFULL * NK, P, CW)
    arrays = {
        "x": a(x)[0], "w_ada": a(w_ada)[0], "w_in": a(chunks), "w_kv": a(w[:, 512:768].reshape(NK, P, 4 * HD)),
        "w_out": a(w_out)[0], "params": a(params), "positions": a(a(positions)[0].reshape(NT, P).T),
        "b_gate": a(b[2 * D:].reshape(1, D)), "consts": constants(),
    }
    nc = bacc.Bacc("TRN2", target_bir_lowering=False, num_devices=1)
    args = [nc.dram_tensor(f"in_{n}", v.shape, mybir.dt.from_np(v.dtype), kind="ExternalInput").ap()
            for n, v in arrays.items()]
    out = nc.dram_tensor("out", (S, D), F32, kind="ExternalOutput").ap()
    hymba_kernel(nc, *args, out)
    r = run_bass_kernel_spmd(nc, [{f"in_{n}": v for n, v in arrays.items()}], core_ids=[0])
    return r.results[0]["out"].reshape(1, S, D)
```
